# Optimizing a Trainium2 kernel written in Bass

```python
import jax
import jax.numpy as jnp
from jax import lax
import numpy as np
import jax, jax.numpy as jnp

D_MODEL = 1024
BATCH = 1
SEQ = 256
DEPTH = 1

HEAD_DIM = 64
N_ATTN_HEADS = (D_MODEL // 2) // HEAD_DIM
ATTN_WIDTH = N_ATTN_HEADS * HEAD_DIM
MOBA_BLOCK = 256
MOBA_TOPK = 3
Q_CHUNK = 128
SGU_WIDTH = D_MODEL // 2
N_SGU_GROUPS = 8
SGU_GROUP_DIM = SGU_WIDTH // N_SGU_GROUPS
SGU_CHUNK = 128
D_FF = 4 * D_MODEL
N_MOD = 6
IN_WIDTH = 3 * ATTN_WIDTH + 2 * SGU_WIDTH + 2 * D_MODEL
EPS = 1e-6


def rmsnorm(x, g):
    xf = x.astype(jnp.float32)
    y = xf * lax.rsqrt(jnp.mean(xf * xf, axis=-1, keepdims=True) + EPS)
    return (y * g.astype(jnp.float32)).astype(x.dtype)

def moba_attention(q, k, v):
    B, S, H, Dh = q.shape
    L = MOBA_BLOCK
    nb = -(-S // L)
    s_pad = nb * L
    nqc = S // Q_CHUNK
    k_sel = min(MOBA_TOPK, nb - 1)
    scale = Dh ** -0.5
    qh = q.transpose(0, 2, 1, 3)
    pad = ((0, 0), (0, 0), (0, s_pad - S), (0, 0))
    kb = jnp.pad(k.transpose(0, 2, 1, 3), pad).reshape(B, H, nb, L, Dh)
    vb = jnp.pad(v.transpose(0, 2, 1, 3), pad).reshape(B, H, nb, L, Dh)
    qblk = jnp.arange(S) // L
    if k_sel > 0:
        kmean = jnp.mean(kb.astype(jnp.float32), axis=3)
        gate = jnp.einsum('bhsd,bhnd->bhsn', qh.astype(jnp.float32), kmean)
        fully_past = jnp.arange(nb)[None, :] < qblk[:, None]
        gate = jnp.where(fully_past[None, None], gate, -jnp.inf)
        _, idx = lax.top_k(gate, k_sel)
    else:
        idx = jnp.zeros((B, H, S, 0), jnp.int32)
    valid = idx < qblk[None, None, :, None]

    def to_chunks(a):
        tail = a.shape[3:]
        a = a.reshape((B, H, nqc, Q_CHUNK) + tail).swapaxes(1, 2)
        return a.reshape((B * nqc, H, Q_CHUNK) + tail)

    q_c = to_chunks(qh)
    idx_c = to_chunks(idx)
    valid_c = to_chunks(valid)
    b_ids = jnp.repeat(jnp.arange(B, dtype=jnp.int32), nqc)
    c_ids = jnp.tile(jnp.arange(nqc, dtype=jnp.int32), B)
    heads = jnp.arange(H)[:, None, None]
    offs_q = jnp.arange(Q_CHUNK)
    offs_k = jnp.arange(L)

    def attend_chunk(args):
        qi, ii, vi, bi, ci = args
        kb_b = lax.dynamic_index_in_dim(kb, bi, 0, keepdims=False)
        vb_b = lax.dynamic_index_in_dim(vb, bi, 0, keepdims=False)
        blk = (ci * Q_CHUNK) // L
        k_own = lax.dynamic_index_in_dim(kb_b, blk, 1, keepdims=False)
        v_own = lax.dynamic_index_in_dim(vb_b, blk, 1, keepdims=False)
        qf = qi.astype(jnp.float32) * scale
        s_own = jnp.einsum('hqd,hld->hql', qf, k_own.astype(jnp.float32))
        causal = (blk * L + offs_k)[None, :] <= (ci * Q_CHUNK + offs_q)[:, None]
        s_own = jnp.where(causal[None], s_own, -jnp.inf)
        k_g = kb_b[heads, ii]
        v_g = vb_b[heads, ii]
        s_g = jnp.einsum('hqd,hqkld->hqkl', qf, k_g.astype(jnp.float32))
        s_g = jnp.where(vi[..., None], s_g, -jnp.inf).reshape(H, Q_CHUNK, k_sel * L)
        p = jax.nn.softmax(jnp.concatenate([s_own, s_g], axis=-1), axis=-1)
        p_own = p[..., :L]
        p_g = p[..., L:].reshape(H, Q_CHUNK, k_sel, L)
        o = (jnp.einsum('hql,hld->hqd', p_own, v_own.astype(jnp.float32))
             + jnp.einsum('hqkl,hqkld->hqd', p_g, v_g.astype(jnp.float32)))
        return o.astype(qi.dtype)

    o = lax.map(attend_chunk, (q_c, idx_c, valid_c, b_ids, c_ids))
    o = o.reshape(B, nqc, H, Q_CHUNK, Dh).transpose(0, 1, 3, 2, 4)
    return o.reshape(B, S, H * Dh)

def spatial_gating(u, vs, g_v, w_s, b_s):
    B, S, _ = u.shape
    nc = S // SGU_CHUNK
    vs = rmsnorm(vs, g_v)
    vg = vs.reshape(B, nc, SGU_CHUNK, N_SGU_GROUPS, SGU_GROUP_DIM)
    w_causal = jnp.tril(w_s)
    z = jnp.einsum('gts,bcsgd->bctgd', w_causal, vg) + b_s.T[None, None, :, :, None]
    return u * z.reshape(B, S, SGU_WIDTH)

def first_inputs(seed: int = 0) -> dict:
    key = jax.random.key(seed)
    ks = jax.random.split(key, 16)
    f32 = jnp.float32
    nrm = lambda k, shape, s: jax.random.normal(k, shape, f32) * s
    return {
        "x": nrm(ks[0], (BATCH, SEQ, D_MODEL), 1.0),
        "c": nrm(ks[1], (BATCH, D_MODEL), 1.0),
        "w_ada": nrm(ks[2], (DEPTH, D_MODEL, N_MOD * D_MODEL), 0.5 * D_MODEL ** -0.5),
        "b_ada": nrm(ks[3], (DEPTH, N_MOD * D_MODEL), 0.01),
        "g_mix": 1.0 + nrm(ks[4], (DEPTH, D_MODEL), 0.01),
        "w_in": nrm(ks[5], (DEPTH, D_MODEL, IN_WIDTH), D_MODEL ** -0.5),
        "w_proj_attn": nrm(ks[6], (DEPTH, ATTN_WIDTH, D_MODEL), ATTN_WIDTH ** -0.5),
        "g_sgu": 1.0 + nrm(ks[7], (DEPTH, SGU_WIDTH), 0.01),
        "w_sgu": nrm(ks[8], (DEPTH, N_SGU_GROUPS, SGU_CHUNK, SGU_CHUNK), SGU_CHUNK ** -0.5),
        "b_sgu": 1.0 + nrm(ks[9], (DEPTH, N_SGU_GROUPS, SGU_CHUNK), 0.01),
        "w_proj_sgu": nrm(ks[10], (DEPTH, SGU_WIDTH, D_MODEL), SGU_WIDTH ** -0.5),
        "w_out": nrm(ks[11], (DEPTH, D_MODEL, D_MODEL), D_MODEL ** -0.5),
        "g_ffn": 1.0 + nrm(ks[12], (DEPTH, D_MODEL), 0.01),
        "w_ff1": nrm(ks[13], (DEPTH, D_MODEL, D_FF), D_MODEL ** -0.5),
        "w_ff2": nrm(ks[14], (DEPTH, D_FF, D_MODEL), D_FF ** -0.5),
        "g_final": 1.0 + nrm(ks[15], (D_MODEL,), 0.01),
    }

def first_block(x, c, w_ada, b_ada, g_mix, w_in, w_proj_attn, g_sgu, w_sgu, b_sgu,
              w_proj_sgu, w_out, g_ffn, w_ff1, w_ff2, g_final):
    B, S, _ = x.shape
    A, W, D = ATTN_WIDTH, SGU_WIDTH, D_MODEL
    splits = [A, 2 * A, 3 * A, 3 * A + W, 3 * A + 2 * W, 3 * A + 2 * W + D]
    c_act = jax.nn.silu(c)
    for l in range(DEPTH):
        mod = (c_act @ w_ada[l] + b_ada[l])[:, None, :]
        shift1, scale1, gate1, shift2, scale2, gate2 = jnp.split(mod, N_MOD, axis=-1)
        h = rmsnorm(x, g_mix[l]) * (1 + scale1) + shift1
        proj = h @ w_in[l]
        q, k, v, u, vs, ga, gb = jnp.split(proj, splits, axis=-1)
        hs = (B, S, N_ATTN_HEADS, HEAD_DIM)
        y_attn = moba_attention(q.reshape(hs), k.reshape(hs), v.reshape(hs)) @ w_proj_attn[l]
        y_sgu = spatial_gating(jax.nn.gelu(u), jax.nn.gelu(vs), g_sgu[l], w_sgu[l], b_sgu[l]) @ w_proj_sgu[l]
        merged = jax.nn.sigmoid(ga) * y_attn + jax.nn.sigmoid(gb) * y_sgu
        x = x + gate1 * (merged @ w_out[l])
        h = rmsnorm(x, g_ffn[l]) * (1 + scale2) + shift2
        x = x + gate2 * (jnp.square(jax.nn.relu(h @ w_ff1[l])) @ w_ff2[l])
    return rmsnorm(x, g_final)


_first_inputs = first_inputs


def first_inputs(seed=0):
    import zlib

    import numpy as np

    out = dict(_first_inputs(seed))
    spreads = {}
    factors = {'b_ada': 3.749, 'g_mix': 8.0, 'g_sgu': 8.0, 'b_sgu': 8.0, 'g_ffn': 8.0, 'g_final': 5.676}
    for name, (base, spread) in spreads.items():
        noise = np.random.default_rng([zlib.crc32(name.encode()), seed]).standard_normal(out[name].shape)
        drawn = base * np.exp(spread * noise) if base else spread * noise
        out[name] = jnp.asarray(drawn.astype(out[name].dtype))
    for name, factor in factors.items():
        out[name] = (out[name] * factor).astype(out[name].dtype)
    return out


_narrow_inputs = first_inputs


def first_inputs(seed=0):

    out = dict(_narrow_inputs(seed))
    wider = {'g_sgu': 10.09, 'b_sgu': 7.06, 'g_ffn': 6.21, 'g_final': 6.26}
    for name, times in wider.items():
        mean = out[name].mean()
        out[name] = (mean + times * (out[name] - mean)).astype(out[name].dtype)
    return out


DEPTH_2 = 2

GRID_W = 64
CTX_LEN = 256
MLA_HEADS = 8
Q_LORA = 256
KV_LORA = 128
QK_NOPE = 64
QK_ROPE = 32
V_HEAD = 64
QK_HEAD = QK_NOPE + QK_ROPE
ROPE_BASE = 10000.0
Q_BLOCK = 128
FNET_GROUPS = 4
FNET_GROUP_DIM = 64
FNET_C = FNET_GROUPS * FNET_GROUP_DIM
CONV_C = 256
CONV_W = 31
N_BRANCH = 3
PEER_HEADS = 8
N_KEYS = 128
N_EXPERTS = N_KEYS * N_KEYS
D_KEY = 128
PEER_TOPK = 16
PEER_CHUNK = 128
KV_IN = KV_LORA + QK_ROPE
REST_SPLITS = [Q_LORA, Q_LORA + FNET_C, Q_LORA + FNET_C + 2 * CONV_C]
IN_COLS = KV_IN + Q_LORA + FNET_C + 2 * CONV_C + N_BRANCH * D_MODEL


def rmsnorm_2(x, g):
    xf = x.astype(jnp.float32)
    y = xf * lax.rsqrt(jnp.mean(xf * xf, axis=-1, keepdims=True) + EPS)
    return (y * g.astype(jnp.float32)).astype(x.dtype)

def layernorm(x, g, b):
    xf = x.astype(jnp.float32)
    mu = jnp.mean(xf, axis=-1, keepdims=True)
    var = jnp.mean(jnp.square(xf - mu), axis=-1, keepdims=True)
    y = (xf - mu) * lax.rsqrt(var + EPS)
    return (y * g.astype(jnp.float32) + b.astype(jnp.float32)).astype(x.dtype)

def adaln(cond, w_mod, b_mod):
    return jnp.split(jax.nn.silu(cond) @ w_mod + b_mod, 6, axis=-1)

def modulate(h, shift, scale):
    return h * (1.0 + scale[:, None, :]) + shift[:, None, :]

def axial_rope_tables(n, dtype):
    rows = n // GRID_W
    row = jnp.repeat(jnp.arange(rows, dtype=jnp.float32), GRID_W)
    col = jnp.tile(jnp.arange(GRID_W, dtype=jnp.float32), rows)
    half = QK_ROPE // 2
    inv = ROPE_BASE ** (-jnp.arange(0, half, 2, dtype=jnp.float32) / half)
    ar = row[:, None] * inv
    ac = col[:, None] * inv
    ang = jnp.concatenate([ar, ar, ac, ac], axis=-1)
    return jnp.cos(ang).astype(dtype), jnp.sin(ang).astype(dtype)

def _rotate_half(z):
    z1, z2 = jnp.split(z, 2, axis=-1)
    return jnp.concatenate([-z2, z1], axis=-1)

def apply_axial_rope(z, cos, sin):
    zr, zc = jnp.split(z, 2, axis=-1)
    rot = jnp.concatenate([_rotate_half(zr), _rotate_half(zc)], axis=-1)
    return z * cos[:, None, :] + rot * sin[:, None, :]

def mla_q(cq, lp, rope):
    b, t, _ = cq.shape
    q = (rmsnorm_2(cq, lp['g_cq']) @ lp['w_uq']).reshape(b, t, MLA_HEADS, QK_HEAD)
    q = rmsnorm_2(q, lp['g_qn'])
    if rope is not None:
        q = jnp.concatenate([q[..., :QK_NOPE], apply_axial_rope(q[..., QK_NOPE:], *rope)], axis=-1)
    return q

def mla_kv(z, lp, rope):
    b, t, _ = z.shape
    ckv, kr = jnp.split(z, [KV_LORA], axis=-1)
    kv = (rmsnorm_2(ckv, lp['g_ckv']) @ lp['w_ukv']).reshape(b, t, MLA_HEADS, QK_NOPE + V_HEAD)
    k_nope, v = kv[..., :QK_NOPE], kv[..., QK_NOPE:]
    k_rope = jnp.broadcast_to(kr[:, :, None, :], (b, t, MLA_HEADS, QK_ROPE))
    k = rmsnorm_2(jnp.concatenate([k_nope, k_rope], axis=-1), lp['g_kn'])
    if rope is not None:
        k = jnp.concatenate([k[..., :QK_NOPE], apply_axial_rope(k[..., QK_NOPE:], *rope)], axis=-1)
    return k, v

def softmax_attend(q, k, v):
    s = jnp.einsum('bqhd,bkhd->bhqk', q, k).astype(jnp.float32) * (QK_HEAD ** -0.5)
    p = jax.nn.softmax(s, axis=-1).astype(v.dtype)
    return jnp.einsum('bhqk,bkhd->bqhd', p, v)

def latent_attention(q, k, v):
    b, s, h, _ = q.shape
    nb = s // Q_BLOCK
    qb = q.reshape(b, nb, Q_BLOCK, h, QK_HEAD).transpose(1, 0, 2, 3, 4)
    o = lax.map(lambda qi: softmax_attend(qi, k, v), qb)
    return o.transpose(1, 0, 2, 3, 4).reshape(b, s, h * V_HEAD)

def fourier_mix(z):
    b, t, _ = z.shape
    zz = z.astype(jnp.float32).reshape(b, t, FNET_GROUPS, FNET_GROUP_DIM)
    f = jnp.fft.fft2(zz, axes=(1, 3), norm='ortho').real
    return f.reshape(b, t, FNET_C).astype(z.dtype)

def conformer_conv(z, lp):
    a, g = jnp.split(z, 2, axis=-1)
    u = a * jax.nn.sigmoid(g)
    u = lax.conv_general_dilated(u, lp['w_dw'], window_strides=(1,), padding=[(CONV_W // 2, CONV_W // 2)],
                                 dimension_numbers=('NWC', 'WIO', 'NWC'), feature_group_count=CONV_C) + lp['b_dw']
    return jax.nn.silu(layernorm(u, lp['g_cln'], lp['b_cln']))

def branch_merge(a_o, zf, zc, zg, lp):
    b, t, _ = zg.shape
    g = jax.nn.sigmoid(zg.astype(jnp.float32)).astype(zg.dtype).reshape(b, t, N_BRANCH, D_MODEL)
    m = (g[:, :, 0] * (a_o @ lp['wb_attn'])
         + g[:, :, 1] * (fourier_mix(zf) @ lp['wb_fnet'])
         + g[:, :, 2] * (conformer_conv(zc, lp) @ lp['wb_conv']))
    return m @ lp['w_out']

def mixer_sublayer(x, ctx, mod_x, mod_c, lp, rope, update_ctx):
    sh, sc, gt = mod_x
    csh, csc, cgt = mod_c
    hx = modulate(rmsnorm_2(x, lp['g_norm1']), sh, sc)
    hc = modulate(rmsnorm_2(ctx, lp['g_norm1']), csh, csc)
    k_c, v_c = mla_kv(hc @ lp['w_in'][:, :KV_IN], lp, None)
    k_x, v_x = mla_kv(hx @ lp['w_in'][:, :KV_IN], lp, rope)
    cq_x, zf_x, zc_x, zg_x = jnp.split(hx @ lp['w_in'][:, KV_IN:], REST_SPLITS, axis=-1)
    q_x = mla_q(cq_x, lp, rope)
    a_x = latent_attention(q_x, jnp.concatenate([k_c, k_x], axis=1), jnp.concatenate([v_c, v_x], axis=1))
    x = x + gt[:, None, :] * branch_merge(a_x, zf_x, zc_x, zg_x, lp)
    if update_ctx:
        b, l, _ = ctx.shape
        cq_c, zf_c, zc_c, zg_c = jnp.split(hc @ lp['w_in'][:, KV_IN:], REST_SPLITS, axis=-1)
        a_c = softmax_attend(mla_q(cq_c, lp, None), k_c, v_c).reshape(b, l, MLA_HEADS * V_HEAD)
        ctx = ctx + cgt[:, None, :] * branch_merge(a_c, zf_c, zc_c, zg_c, lp)
    return x, ctx

def peer_ffn(h, w_query, sub_keys, u_tab, v_tab):
    b, t, d = h.shape
    chunks = h.reshape(-1, PEER_CHUNK, d)

    def chunk(hc):
        q = (hc @ w_query).reshape(PEER_CHUNK, PEER_HEADS, 2, D_KEY // 2)
        s = jnp.einsum('chpd,hpnd->chpn', q, sub_keys).astype(jnp.float32)
        s_top, i_top = lax.top_k(s, PEER_TOPK)
        cand = (s_top[:, :, 0, :, None] + s_top[:, :, 1, None, :]).reshape(PEER_CHUNK, PEER_HEADS, PEER_TOPK * PEER_TOPK)
        cand_id = (i_top[:, :, 0, :, None] * N_KEYS + i_top[:, :, 1, None, :]).reshape(PEER_CHUNK, PEER_HEADS, PEER_TOPK * PEER_TOPK)
        best, pos = lax.top_k(cand, PEER_TOPK)
        eid = jnp.take_along_axis(cand_id, pos, axis=-1)
        gate = jax.nn.softmax(best, axis=-1).astype(hc.dtype)
        u = jnp.take(u_tab, eid, axis=0)
        act = jax.nn.gelu(jnp.einsum('chkd,cd->chk', u, hc)) * gate
        v = jnp.take(v_tab, eid, axis=0)
        return jnp.einsum('chk,chkd->cd', act, v)

    return lax.map(chunk, chunks).reshape(b, t, d)

def second_inputs(seed: int = 0) -> dict:
    key = jax.random.key(seed)
    ks = jax.random.split(key, 28)
    f32 = jnp.float32

    def nrm(k, shape, scale):
        return jax.random.normal(k, shape, f32) * scale

    def gain(k, shape):
        return 1.0 + 0.02 * jax.random.normal(k, shape, f32)

    L = DEPTH_2
    return {
        'x': nrm(ks[0], (BATCH, SEQ, D_MODEL), 1.0),
        'c': nrm(ks[1], (BATCH, D_MODEL), 1.0),
        'ctx': nrm(ks[2], (BATCH, CTX_LEN, D_MODEL), 1.0),
        'c_ctx': nrm(ks[3], (D_MODEL,), 1.0),
        'w_mod': nrm(ks[4], (L, D_MODEL, 6 * D_MODEL), 0.5 * D_MODEL ** -0.5),
        'b_mod': nrm(ks[5], (L, 6 * D_MODEL), 0.02),
        'g_norm1': gain(ks[6], (L, D_MODEL)),
        'w_in': nrm(ks[7], (L, D_MODEL, IN_COLS), D_MODEL ** -0.5),
        'g_ckv': gain(ks[8], (L, KV_LORA)),
        'w_ukv': nrm(ks[9], (L, KV_LORA, MLA_HEADS * (QK_NOPE + V_HEAD)), KV_LORA ** -0.5),
        'g_cq': gain(ks[10], (L, Q_LORA)),
        'w_uq': nrm(ks[11], (L, Q_LORA, MLA_HEADS * QK_HEAD), Q_LORA ** -0.5),
        'g_qn': gain(ks[12], (L, QK_HEAD)),
        'g_kn': gain(ks[13], (L, QK_HEAD)),
        'w_dw': nrm(ks[14], (L, CONV_W, 1, CONV_C), CONV_W ** -0.5),
        'b_dw': nrm(ks[15], (L, CONV_C), 0.02),
        'g_cln': gain(ks[16], (L, CONV_C)),
        'b_cln': nrm(ks[17], (L, CONV_C), 0.02),
        'wb_attn': nrm(ks[18], (L, MLA_HEADS * V_HEAD, D_MODEL), (MLA_HEADS * V_HEAD) ** -0.5),
        'wb_fnet': nrm(ks[19], (L, FNET_C, D_MODEL), FNET_C ** -0.5),
        'wb_conv': nrm(ks[20], (L, CONV_C, D_MODEL), CONV_C ** -0.5),
        'w_out': nrm(ks[21], (L, D_MODEL, D_MODEL), D_MODEL ** -0.5),
        'g_norm2': gain(ks[22], (L, D_MODEL)),
        'w_query': nrm(ks[23], (L, D_MODEL, PEER_HEADS * D_KEY), D_MODEL ** -0.5),
        'sub_keys': nrm(ks[24], (L, PEER_HEADS, 2, N_KEYS, D_KEY // 2), (D_KEY // 2) ** -0.5),
        'u_tab': nrm(ks[25], (L, N_EXPERTS, D_MODEL), D_MODEL ** -0.5),
        'v_tab': nrm(ks[26], (L, N_EXPERTS, D_MODEL), PEER_HEADS ** -0.5),
    }

def second_block(x, c, ctx, c_ctx, w_mod, b_mod, g_norm1, w_in, g_ckv, w_ukv, g_cq, w_uq, g_qn, g_kn,
              w_dw, b_dw, g_cln, b_cln, wb_attn, wb_fnet, wb_conv, w_out, g_norm2, w_query, sub_keys,
              u_tab, v_tab):
    rope = axial_rope_tables(x.shape[1], x.dtype)
    for i in range(DEPTH_2):
        lp = {'g_norm1': g_norm1[i], 'w_in': w_in[i], 'g_ckv': g_ckv[i], 'w_ukv': w_ukv[i],
              'g_cq': g_cq[i], 'w_uq': w_uq[i], 'g_qn': g_qn[i], 'g_kn': g_kn[i],
              'w_dw': w_dw[i], 'b_dw': b_dw[i], 'g_cln': g_cln[i], 'b_cln': b_cln[i],
              'wb_attn': wb_attn[i], 'wb_fnet': wb_fnet[i], 'wb_conv': wb_conv[i], 'w_out': w_out[i]}
        sh1, sc1, gt1, sh2, sc2, gt2 = adaln(c, w_mod[i], b_mod[i])
        csh1, csc1, cgt1, csh2, csc2, cgt2 = adaln(c_ctx[None, :], w_mod[i], b_mod[i])
        update_ctx = i < DEPTH_2 - 1
        x, ctx = mixer_sublayer(x, ctx, (sh1, sc1, gt1), (csh1, csc1, cgt1), lp, rope, update_ctx)
        x = x + gt2[:, None, :] * peer_ffn(modulate(rmsnorm_2(x, g_norm2[i]), sh2, sc2),
                                           w_query[i], sub_keys[i], u_tab[i], v_tab[i])
        if update_ctx:
            ctx = ctx + cgt2[:, None, :] * peer_ffn(modulate(rmsnorm_2(ctx, g_norm2[i]), csh2, csc2),
                                                    w_query[i], sub_keys[i], u_tab[i], v_tab[i])
    return x


def setup_inputs(seed=0):
    out = dict(first_inputs(seed))
    for name, value in second_inputs(seed + 1).items():
        if name != "x":
            out[name + "_2"] = value
    return out


def reference(
    x, c, w_ada, b_ada, g_mix, w_in, w_proj_attn, g_sgu, w_sgu, b_sgu, w_proj_sgu, w_out, g_ffn,
    w_ff1, w_ff2, g_final, c_2, ctx_2, c_ctx_2, w_mod_2, b_mod_2, g_norm1_2, w_in_2, g_ckv_2,
    w_ukv_2, g_cq_2, w_uq_2, g_qn_2, g_kn_2, w_dw_2, b_dw_2, g_cln_2, b_cln_2, wb_attn_2,
    wb_fnet_2, wb_conv_2, w_out_2, g_norm2_2, w_query_2, sub_keys_2, u_tab_2, v_tab_2,
):
    x = first_block(
        x, c, w_ada, b_ada, g_mix, w_in, w_proj_attn, g_sgu, w_sgu, b_sgu, w_proj_sgu, w_out,
        g_ffn, w_ff1, w_ff2, g_final,
    )
    return second_block(
        x, c_2, ctx_2, c_ctx_2, w_mod_2, b_mod_2, g_norm1_2, w_in_2, g_ckv_2, w_ukv_2, g_cq_2,
        w_uq_2, g_qn_2, g_kn_2, w_dw_2, b_dw_2, g_cln_2, b_cln_2, wb_attn_2, wb_fnet_2,
        wb_conv_2, w_out_2, g_norm2_2, w_query_2, sub_keys_2, u_tab_2, v_tab_2,
    )


_drawn_inputs = setup_inputs


def setup_inputs(seed=0):
    import zlib

    import numpy as np

    out = dict(_drawn_inputs(seed))
    spreads = {}
    factors = {'ctx_2': 8.0,
     'c_ctx_2': 8.0,
     'b_mod_2': 8.0,
     'g_norm1_2': 8.0,
     'g_ckv_2': 8.0,
     'w_ukv_2': 4.322,
     'g_cq_2': 8.0,
     'w_uq_2': 8.0,
     'g_qn_2': 8.0,
     'g_kn_2': 8.0,
     'b_dw_2': 8.0,
     'g_cln_2': 8.0,
     'b_cln_2': 8.0,
     'wb_attn_2': 4.219,
     'g_norm2_2': 8.0,
     'w_query_2': 3.843,
     'sub_keys_2': 3.848,
     'u_tab_2': 4.317,
     'v_tab_2': 3.868}
    for name, (base, spread) in spreads.items():
        noise = np.random.default_rng([zlib.crc32(name.encode()), seed]).standard_normal(out[name].shape)
        drawn = base * np.exp(spread * noise) if base else spread * noise
        out[name] = jnp.asarray(drawn.astype(out[name].dtype))
    for name, factor in factors.items():
        out[name] = (out[name] * factor).astype(out[name].dtype)
    return out
```

```python
import concourse.bass as bass
from concourse import mybir
from contextlib import ExitStack

P = 128
D = 1024
DT = D // P
SEQ = 256
TALL = 2 * SEQ
EPS = 1e-6
LAYERS = 2

HEADS1, HD1 = 8, 64
SGU_W, SGU_G = 512, 8
FF_T = 4096 // P

MH, QK, NOPE, ROPE, VH = 8, 96, 64, 32, 64
KV_IN, Q_LORA, FN_C, CV_C, CV_W = 160, 256, 256, 256, 31
COL_ZF = KV_IN + Q_LORA
COL_ZC = COL_ZF + FN_C
COL_ZG = COL_ZC + 2 * CV_C
PH, NKEY, TOPK = 8, 128, 16
NEXP = NKEY * NKEY

SLOTS = 8
QUAD = 4
OUTER = 32

VEC = {}
_at = 0
for _n, _w in [("c", 8), ("b_ada", 48), ("g_mix", 8), ("g_sgu", 4), ("g_ffn", 8), ("g_final", 8),
               ("c_ctx_2", 8), ("c_2", 8)]:
    VEC[_n] = (_at, _w)
    _at += _w
for _l in range(LAYERS):
    for _n, _w in [("b_mod", 48), ("g_norm1", 8), ("g_ckv", 1), ("g_cq", 2), ("b_dw", 2), ("g_cln", 2),
                   ("b_cln", 2), ("w_dw", 2 * CV_W), ("g_norm2", 8)]:
        VEC[_n, _l] = (_at, _w)
        _at += _w
NVEC = _at


def two_blocks_kernel(nc, A, out):
    f32, bf16, u32 = mybir.dt.float32, mybir.dt.bfloat16, mybir.dt.uint32
    ALU = mybir.AluOpType
    ACT = mybir.ActivationFunctionType
    AX = mybir.AxisListType
    MUL, ADD, SUB = ALU.mult, ALU.add, ALU.subtract

    ctx = ExitStack()
    with ctx:
        def sb(name, shape, dt=f32):
            return ctx.enter_context(nc.sbuf_tensor(name, shape, dt))

        sems = {}

        def sem(name):
            if name not in sems:
                sems[name] = ctx.enter_context(nc.semaphore(name))
            return sems[name]

        X = sb("X", [P, DT, TALL])
        H = sb("H", [P, DT, TALL])
        RING = 2
        W = sb("W", [P, RING, 4096])
        vec = sb("vec", [P, NVEC])
        ident = sb("ident", [P, P])
        ones = sb("ones", [P, P])
        dft = sb("dft", [P, 2, 512])
        dftc = sb("dftc", [P, 2, P])
        ropet = sb("ropet", [QK, 2, TALL])
        rotm = sb("rotm", [QK, QK])
        gqk = sb("gqk", [QK, 2 * LAYERS])
        iota16 = sb("iota16", [P, TOPK])
        selb = sb("selb", [96, 32], bf16)
        minus_half = sb("minus_half", [P, 1])
        cond = sb("cond", [P, 3, DT])
        condt = sb("condt", [P, 3 * DT])
        cond2 = sb("cond2", [P, DT, 2])
        mod1 = sb("mod1", [P, 48])
        mod2 = sb("mod2", [P, 48, 2])
        gs = sb("gs", [P, 2, DT, 2])
        half = sb("half", [P, DT, 2])
        lnh = sb("lnh", [P, 4])
        stat = sb("stat", [P, 4, 16])
        varb = sb("varb", [P, TALL])
        rstd = sb("rstd", [P, TALL])
        idxT = sb("idxT", [P, P], u32)
        gateT = sb("gateT", [P, P])
        idl = sb("idl", [P, 2, QUAD], u32)
        dots = sb("dots", [P, SLOTS])
        gel = sb("gel", [P, SLOTS])
        acts = sb("acts", [P, SLOTS, SLOTS])
        yev = sb("yev", [SLOTS, 2, D])
        ARENA = 29696
        arena = sb("arena", [P, ARENA])

        def view(at, *shape, dt=None, parts=P):
            n = 1
            for s in shape:
                n *= s
            words = n if dt is None else (n + 1) // 2
            assert at + words <= ARENA
            ap = arena[0:parts, at:at + words]
            if dt is not None:
                ap = ap.bitcast(dt)
            if len(shape) == 2:
                ap = ap.rearrange("p (a b) -> p a b", b=shape[1])
            if len(shape) == 3:
                ap = ap.rearrange("p (a b c) -> p a b c", b=shape[1], c=shape[2])
            if len(shape) == 4:
                ap = ap.rearrange("p (a b c d) -> p a b c d", b=shape[1], c=shape[2], d=shape[3])
            return ap

        q1 = view(0, 4, SEQ)
        k1 = view(1024, 4, SEQ)
        v1 = view(2048, 2, 512)
        u1 = view(3072, 4, SEQ)
        vs1 = view(4096, 2, SGU_W)
        vsq1 = view(5120, 2, SGU_W)
        gate1 = view(6144, DT, 2, SEQ)
        P1 = view(10240, 16, SEQ)
        PT1 = view(14336, 2, 2, SEQ)
        att1 = view(15360, 4, SEQ)
        ysg1 = view(16384, 4, SEQ)
        wsg1 = view(17408, SGU_G, P)
        bsg1 = view(18432, 4, P)
        mrg1 = view(18944, DT, SEQ)
        sq1 = view(20992, DT, SEQ)
        mask1 = view(23040, 2, SEQ)
        mt1 = view(23552, 2, 2, SEQ)
        ff1 = view(0, FF_T, SEQ)
        ssg1 = stat[:, 0, 0:2]
        kT = view(0, MH, TALL, parts=QK)
        qT = view(4096, MH, TALL, parts=QK)
        vtok = view(8192, 4, 512)
        PT2 = view(10240, 2, 4, SEQ)
        P2 = view(12288, 16, TALL)
        hraw = view(12288, 3, TALL, parts=QK)
        hsq = view(13824, 3, TALL, parts=QK)
        hvar = view(15360, 3, TALL, parts=QK)
        hrs = view(16896, 3, TALL, parts=QK)
        hqn = view(18432, 3, TALL, parts=QK)
        htmp = view(19968, TALL, parts=QK)
        br = view(20480, DT, TALL)
        ckv = view(24576, TALL)
        cq = view(25088, 2, TALL)
        lsq = view(26112, 3, TALL)
        ckvn = view(24576, TALL)
        cqn = view(25088, 2, TALL)
        zft = view(0, 4, FN_C)
        g1f = view(1024, 4, 512)
        upad = view(3072, 2, 2, SEQ + CV_W - 1)
        acc = view(4224, 2, TALL)
        csq = view(5248, 2, TALL)
        mu = view(6272, TALL)
        cah = view(6784, TALL)
        cth = view(7296, TALL)
        sqx = view(12288, DT, TALL)
        m2 = view(0, DT, TALL)
        sig2 = view(10240, 2, TALL)
        br2 = view(11264, 2, TALL)
        Us = view(0, SLOTS, D)
        Vs = view(8192, SLOTS, D)
        hs = view(16384, 4, D, dt=bf16, parts=96)
        qp = view(20480, DT, TALL)
        sc = view(24576, 16, NKEY)
        cand = view(26624, PH, 256)
        eqp = view(28672, PH, TOPK, TOPK, dt=bf16)
        hp1 = view(24576, D, dt=bf16)
        hp2 = view(25088, D, dt=bf16)
        hp3 = view(25600, D, dt=bf16)
        hres = view(26624, D)
        ytok = view(24576, D)
        top = sb("top", [P, 16, TOPK])
        tix = varb[:, 0:256].bitcast(u32).rearrange("p (a b) -> p a b", b=TOPK)
        tixf = varb[:, 256:512].rearrange("p (a b) -> p a b", b=TOPK)
        best = rstd[:, 0:128].rearrange("p (a b) -> p a b", b=TOPK)
        pos = rstd[:, 128:256].bitcast(u32).rearrange("p (a b) -> p a b", b=TOPK)
        posi = rstd[:, 256:512].bitcast(u32).rearrange("p (a b) -> p a b", a=2)
        posf = view(24576, 2, PH, TOPK)
        ij = view(24832, 2, PH, TOPK)
        eid = view(25088, P)
        gat = view(25216, PH, TOPK)
        gsum = view(25344, 2, PH)
        yscr = nc.dram_tensor("yscr", (6 * P, D), f32, kind="Internal").ap()

        NB = 8
        ps = ctx.enter_context(nc.psum_tensor("ps", [P, NB, 512], f32))

        def V(name, l=None):
            a, n = VEC[name] if l is None else VEC[name, l]
            return vec[:, a:a + n]

        chunks = []

        def chunk(name, src, kt, n):
            chunks.append((name, src, kt, n))

        def rows(ap):
            return ap.rearrange("(k p) n -> p k n", p=P)

        for j in range(12):
            chunk(("ada", j), rows(A["w_ada"][0])[:, :, j * 512:(j + 1) * 512], 8, 512)
        for j in range(9):
            chunk(("in1", j), rows(A["w_in"][0])[:, :, j * 512:(j + 1) * 512], 8, 512)
        chunk("pa1", rows(A["w_proj_attn"][0]), 4, 1024)
        chunk("ps1", rows(A["w_proj_sgu"][0]), 4, 1024)
        for j in range(2):
            chunk(("out1", j), rows(A["w_out"][0])[:, :, j * 512:(j + 1) * 512], 8, 512)
        for j in range(8):
            chunk(("ffa", j), rows(A["w_ff1"][0])[:, :, j * 512:(j + 1) * 512], 8, 512)
        for j in range(8):
            chunk(("ffb", j), rows(A["w_ff2"][0])[:, :, j * P:(j + 1) * P], 32, P)
        for l in range(LAYERS):
            for j in range(12):
                chunk(("mod", l, j), rows(A["w_mod_2"][l])[:, :, j * 512:(j + 1) * 512], 8, 512)
            win = rows(A["w_in_2"][l])
            chunk(("inA", l), win[:, :, 0:COL_ZF], 8, COL_ZF)
            chunk(("inB", l), win[:, :, COL_ZF:COL_ZC], 8, FN_C)
            chunk(("inC", l), win[:, :, COL_ZC:COL_ZG], 8, 512)
            chunk(("ukv", l), rows(A["w_ukv_2"][l]), 1, MH * P)
            chunk(("uq", l), rows(A["w_uq_2"][l]), 2, MH * QK)
            for j in range(2):
                for b, (wb, kt) in enumerate([("wb_attn_2", 4), ("wb_fnet_2", 2), ("wb_conv_2", 2)]):
                    at = COL_ZG + b * D + j * 512
                    chunk(("zg", l, j, b), win[:, :, at:at + 512], 8, 512)
                    chunk(("wb", l, j, b), rows(A[wb][l])[:, :, j * 512:(j + 1) * 512], kt, 512)
            for j in range(2):
                chunk(("out2", l, j), rows(A["w_out_2"][l])[:, :, j * 512:(j + 1) * 512], 8, 512)
            for j in range(2):
                chunk(("wq", l, j), rows(A["w_query_2"][l])[:, :, j * 512:(j + 1) * 512], 8, 512)
            chunk(("keys", l), A["keys"][l], PH, NKEY)
        chunk_at = {c[0]: i for i, c in enumerate(chunks)}

        def ring_slot(i):
            _, _, kt, n = chunks[i]
            return W[:, i % RING, 0:kt * n].rearrange("p (k n) -> p k n", n=n)

        QC = [0, SEQ]
        TILES = [(l, t) for l in range(LAYERS) for t in range(QC[l] // P, TALL // P)]

        def streams(l):
            return range(QC[l] // SEQ, 2)

        ATT = [("a1", None, 0, SEQ)] + [(f"a2{l}{s}", l, s * SEQ, (s + 1) * SEQ) for l in range(LAYERS) for s in streams(l)]

        group = {}

        block = ctx.enter_context(nc.Block())

        @block.tensor
        def _(pe):
            mm = pe.matmul

            def bank(name):
                g = len(group)
                group[name] = g
                if g >= NB:
                    pe.wait_ge(sem(f"bank_free{g % NB}"), g // NB)
                return ps[:, g % NB, :]

            def full(last):
                last.then_inc(sem("psum_full"), 1)

            def weights(name):
                i = chunk_at[name]
                pe.wait_ge(sem(f"w_arrived{i % RING}"), 16 * (i // RING + 1))
                return ring_slot(i)

            def done_with_weights():
                pe.drain().then_inc(sem("w_used"), 1)

            def acc_mm(o, lhs, rhs):
                n = len(lhs)
                for k in range(n):
                    last = mm(o, lhs[k], rhs[k], start=(k == 0), stop=(k == n - 1))
                return last

            def features(name, w, col, src, kt, c0, c1, m=P):
                o = bank(name)
                full(acc_mm(o[0:m, 0:c1 - c0], [w[:, k, col:col + m] for k in range(kt)],
                            [src[:, k, c0:c1] for k in range(kt)]))

            def modulation(name, parts, rhs, n):
                o = bank(name)
                for j in range(12):
                    w = weights((*parts, j))
                    for t in range(4):
                        last = acc_mm(o[:, (4 * j + t) * n:(4 * j + t + 1) * n], [w[:, k, t * P:(t + 1) * P] for k in range(8)], rhs)
                    if j < 11:
                        last.then_inc(sem("w_used"), 1)
                full(last)
                done_with_weights()

            def square_sums(name, sq, kt, c0, c1, m=P, sem_name="squares_ready", count=None):
                pe.wait_ge(sem(sem_name), count)
                o = bank(name)
                full(acc_mm(o[0:m, 0:c1 - c0], [ones[0:m, 0:m]] * kt, [sq[0:m, k, c0:c1] for k in range(kt)]))

            def attention(tag, q, k, v, pt, prob, qcols, nk, scores_of):
                ktiles = nk // P
                for i in range(16 + 5):
                    if i < 16:
                        h, t = i // 2, i % 2
                        lhs, rhs = scores_of(h, t)
                        o = bank((tag, "s", i))
                        full(mm(o[:, 0:nk], lhs, rhs, start=True, stop=True))
                    if 0 <= i - 3 < 16:
                        pe.wait_ge(sem(f"{tag}_probs"), i - 2)
                        o = bank((tag, "t", i - 3))
                        for kt in range(ktiles):
                            last = pe.transpose(o[:, kt * P:(kt + 1) * P], prob[:, i - 3, kt * P:(kt + 1) * P], ident[:, :])
                        full(last)
                    if 0 <= i - 5 < 16 and (i - 5) % 2:
                        h = (i - 5) // 2
                        pe.wait_ge(sem(f"{tag}_probsT"), 2 * h + 2)
                        o = bank((tag, "o", h))
                        full(acc_mm(o[:, 0:SEQ], [v(kt)[:, (h // 2) * P:(h // 2 + 1) * P] for kt in range(ktiles)],
                                    [pt[:, h % 2, kt, :] for kt in range(ktiles)]))

            pe.wait_ge(sem("ones_set"), 1)
            pe.wait_ge(sem("cond_ready"), 1)
            modulation("mod1", ("ada",), [cond[:, 0, k:k + 1] for k in range(8)], 1)
            square_sums("ss_n1", sq1, DT, 0, SEQ, count=1)
            pe.wait_ge(sem("h_ready"), 1)
            X0 = SEQ
            for j in range(9):
                w = weights(("in1", j))
                for t in range(4):
                    if j in (2, 4):
                        if t < 2:
                            o = bank(("in1", j, t))
                            full(acc_mm(o, [H[:, k, X0 + t * P:X0 + (t + 1) * P] for k in range(8)], [w[:, k, :] for k in range(8)]))
                    else:
                        features(("in1", j, t), w, t * P, H, 8, X0, TALL)
                done_with_weights()

            def scores1(h, t):
                r = slice((h % 2) * HD1, (h % 2) * HD1 + HD1)
                return q1[r, h // 2, t * P:(t + 1) * P], k1[r, h // 2, :]

            pe.wait_ge(sem("qkv1_ready"), 10)
            pe.wait_ge(sem("ident_set"), 16)
            attention("a1", q1, k1, lambda kt: v1[:, kt, :], PT1, P1, 0, SEQ, scores1)
            pe.wait_ge(sem("sgu_ready"), 2)
            for p in range(4):
                o = bank(("sg", p))
                for c in range(2):
                    last = mm(o[:, c * SEQ:(c + 1) * SEQ], vs1[:, c, p * P:(p + 1) * P], wsg1[:, 2 * p:2 * p + 2, :], start=True, stop=True)
                full(last)
            pe.wait_ge(sem("mix1_ready"), 12)
            wa, ws = weights("pa1"), weights("ps1")
            for n in range(DT):
                o = bank(("mg1", n))
                acc_mm(o[:, 0:SEQ], [wa[:, k, n * P:(n + 1) * P] for k in range(4)], [att1[:, k, :] for k in range(4)])
                full(acc_mm(o[:, SEQ:], [ws[:, k, n * P:(n + 1) * P] for k in range(4)], [ysg1[:, k, :] for k in range(4)]))
            done_with_weights()
            done_with_weights()
            pe.wait_ge(sem("merged1"), DT)
            for j in range(2):
                w = weights(("out1", j))
                for t in range(4):
                    features(("out1", 4 * j + t), w, t * P, mrg1, 8, 0, SEQ)
                done_with_weights()
            square_sums("ss_n2", sq1, DT, 0, SEQ, count=2)
            pe.wait_ge(sem("h_ready"), 2)
            for j in range(8):
                w = weights(("ffa", j))
                for t in range(4):
                    features(("ffa", 4 * j + t), w, t * P, H, 8, X0, TALL)
                done_with_weights()
            pe.wait_ge(sem("ff_ready"), FF_T)
            for n in range(DT):
                w = weights(("ffb", n))
                features(("ffb", n), w, 0, ff1, FF_T, 0, SEQ)
                done_with_weights()
            square_sums("ss_n3", sq1, DT, 0, SEQ, count=3)

            pe.wait_ge(sem("const_loaded"), 16 * 6)
            pe.wait_ge(sem("sel_ready"), 1)
            nsq = 3
            tile_no = 0
            for l in range(LAYERS):
                c0 = QC[l]
                modulation(("mod2", l), ("mod", l), [cond2[:, k, :] for k in range(8)], 2)
                nsq += 1
                square_sums(("ss_n1", l), sqx, DT, 0, TALL, count=nsq)
                pe.wait_ge(sem("h_ready"), 3 + 2 * l)
                w = weights(("inA", l))
                features(("ckv", l), w, 0, H, 8, 0, TALL)
                features(("kr", l), w, NOPE, H, 8, 0, TALL, m=QK)
                for t in range(2):
                    features(("cq", l, t), w, KV_IN + t * P, H, 8, c0, TALL)
                done_with_weights()
                w = weights(("inB", l))
                for t in range(c0 // P, 4):
                    o = bank(("zf", l, t))
                    full(acc_mm(o[:, 0:FN_C], [H[:, k, t * P:(t + 1) * P] for k in range(8)], [w[:, k, :] for k in range(8)]))
                done_with_weights()
                w = weights(("inC", l))
                for t in (0, 2, 1, 3):
                    features(("zc", l, t), w, t * P, H, 8, c0, TALL)
                done_with_weights()
                square_sums(("ss_ckv", l), lsq, 1, 0, TALL, sem_name="lat_squares", count=2 * l + 1)
                pe.wait_ge(sem("lat_squares"), 2 * l + 2)
                o = bank(("ss_cq", l))
                full(acc_mm(o[:, 0:TALL - c0], [ones[:, :]] * 2, [lsq[:, 1 + k, c0:TALL] for k in range(2)]))
                pe.wait_ge(sem("zf_ready"), 4 if l == 0 else 6)
                for s in streams(l):
                    for c in range(2):
                        o = bank(("dt", l, s, c))
                        full(acc_mm(o, [zft[:, 2 * s + t, c * P:(c + 1) * P] for t in range(2)], [dft[:, t, :] for t in range(2)]))
                for s in streams(l):
                    pe.wait_ge(sem("dft_ready"), 2 * (s + 1) if l == 0 else 6)
                    o = bank(("dc", l, s))
                    for c in range(2):
                        last = acc_mm(o[:, c * SEQ:(c + 1) * SEQ], [dftc[:, 0, :], dftc[:, 1, :]],
                                      [g1f[:, 2 * s + c, 0:SEQ], g1f[:, 2 * s + c, SEQ:512]])
                    full(last)
                wkv = weights(("ukv", l))
                pe.wait_ge(sem("ckvn_ready"), l + 1)
                vcols = wkv[:, 0, :].rearrange("p (h c) -> p h c", c=P)[:, :, NOPE:P]
                for t in range(4):
                    o = bank(("v", l, t))
                    full(mm(o, ckvn[:, t * P:(t + 1) * P], vcols, start=True, stop=True))
                pe.wait_ge(sem("conv_ready"), l + 1)
                o = bank(("cmean", l))
                full(acc_mm(o[:, 0:TALL - c0], [ones[:, :]] * 2, [acc[:, c, c0:TALL] for c in range(2)]))
                pe.wait_ge(sem("conv_squares"), l + 1)
                o = bank(("cvar", l))
                full(acc_mm(o[:, 0:TALL - c0], [ones[:, :]] * 2, [csq[:, c, c0:TALL] for c in range(2)]))
                pe.wait_ge(sem("conv_done"), l + 1)
                wuq = None
                for i in range(16 + 3):
                    if i < 16:
                        h = i % 8
                        if i < 8:
                            o = bank(("hp", l, i))
                            full(mm(o[0:NOPE, :], wkv[:, 0, h * P:h * P + NOPE], ckvn[:, :], start=True, stop=True))
                        else:
                            if i == 8:
                                wuq = weights(("uq", l))
                                pe.wait_ge(sem("cqn_ready"), l + 1)
                            features(("hp", l, i), wuq, h * QK, cqn, 2, c0, TALL, m=QK)
                        if i in (7, 15):
                            done_with_weights()
                    if 0 <= i - 1 < 16:
                        a = 0 if i - 1 < 8 else c0
                        pe.wait_ge(sem("head_squares"), 16 * l + i)
                        o = bank(("hs", l, i - 1))
                        full(mm(o[0:QK, 0:TALL - a], ones[0:QK, 0:QK], hsq[:, (i - 1) % 3, a:TALL], start=True, stop=True))
                    if 0 <= i - 3 < 16:
                        a = 0 if i - 3 < 8 else c0
                        pe.wait_ge(sem("head_normed"), 16 * l + i - 2)
                        o = bank(("hr", l, i - 3))
                        full(mm(o[0:QK, 0:TALL - a], rotm[:, :], hqn[:, (i - 3) % 3, a:TALL], start=True, stop=True))
                pe.wait_ge(sem("heads_ready"), 16 * (l + 1))
                for tag, al, q0, nk in ATT:
                    if al != l:
                        continue

                    def scores2(h, t):
                        return qT[:, h, q0 + t * P:q0 + (t + 1) * P], kT[:, h, 0:nk]

                    attention(tag, qT, kT, lambda kt: vtok[:, kt, :], PT2, P2, q0, nk, scores2)
                pe.wait_ge(sem("att_ready"), 8 * (len([a for a in ATT if a[1] is not None and a[1] <= l])))
                for j in range(2):
                    for b, (k0, kt) in enumerate([(0, 4), (4, 2), (6, 2)]):
                        wz, wb = weights(("zg", l, j, b)), weights(("wb", l, j, b))
                        for t in range(4):
                            features(("zg", l, j, b, t), wz, t * P, H, 8, c0, TALL)
                            o = bank(("br", l, j, b, t))
                            full(acc_mm(o[:, 0:TALL - c0], [wb[:, k, t * P:(t + 1) * P] for k in range(kt)],
                                        [br[:, k0 + k, c0:TALL] for k in range(kt)]))
                        done_with_weights()
                        done_with_weights()
                pe.wait_ge(sem("merged2"), DT * (l + 1))
                for j in range(2):
                    w = weights(("out2", l, j))
                    for t in range(4):
                        features(("out2", l, 4 * j + t), w, t * P, m2, 8, c0, TALL)
                    done_with_weights()
                nsq += 1
                square_sums(("ss_n2", l), sqx, DT, c0, TALL, count=nsq)
                pe.wait_ge(sem("h_ready"), 4 + 2 * l)
                for j in range(2):
                    w = weights(("wq", l, j))
                    for t in range(4):
                        features(("wq", l, 4 * j + t), w, t * P, H, 8, c0, TALL)
                    done_with_weights()
                keys = weights(("keys", l))
                pe.wait_ge(sem("query_ready"), DT * (l + 1))
                mine = [t for ll, t in TILES if ll == l]
                for tt in mine:
                    n = tile_no
                    tile_no += 1
                    cols = slice(tt * P, (tt + 1) * P)
                    for a in range(2):
                        o = bank(("ht", n, a))
                        for k in range(4):
                            last = pe.transpose(o[:, k * P:(k + 1) * P], H[:, 4 * a + k, cols], ident[:, :])
                        full(last)
                    for a in range(2):
                        for p in range(2):
                            o = bank(("sc", n, a, p))
                            for hh in range(4):
                                h = 4 * a + hh
                                last = mm(o[:, hh * P:(hh + 1) * P], qp[64 * p:64 * p + 64, h, cols], keys[64 * p:64 * p + 64, h, :], start=True, stop=True)
                            full(last)
                    if tt == mine[-1]:
                        done_with_weights()
                    pe.wait_ge(sem("routed"), n + 1)
                    o = bank(("ij", n))
                    pe.transpose(o[:, 0:P], eid[:, :], ident[:, :])
                    full(pe.transpose(o[:, P:2 * P], gat[:, :, :].rearrange("p a b -> p (a b)"), ident[:, :]))

                    for b in range(NB):
                        uses = (len(group) - 1 - b) // NB + 1
                        pe.wait_ge(sem(f"bank_free{b}"), uses)
                    pe.wait_ge(sem("hs_ready"), n + 1)
                    t0 = n * P

                    def body(it, last_one):
                        for c in range(OUTER // QUAD):
                            for j in range(QUAD * (c + 1), QUAD * (c + 2)):
                                if j < OUTER:
                                    spread_at(it, j)
                                elif not last_one:
                                    spread_at(it + 1, j - OUTER)
                            outputs_at(it, c)

                    def spread_at(it, j):
                        pe.wait_ge(sem("dots"), it * OUTER + (t0 + SLOTS + j - 1))
                        rhs = hs[:, it, :] if isinstance(it, int) else hs[:, bass.ds(it, 1), :].rearrange("p a d -> p (a d)")
                        for hf in range(2):
                            last = mm(ps[:, 2 * (j % 2) + hf, :], selb[:, j:j + 1].to_broadcast([96, P]),
                                      rhs[:, hf * 512:(hf + 1) * 512], start=True, stop=True)
                        last.then_inc(sem("spread"), 1)

                    def outputs_at(it, c):
                        pe.wait_ge(sem("acts"), it * (OUTER // QUAD) + (t0 // QUAD + c + 1))
                        yb = 4 + 2 * ((c // 2) % 2)
                        if c % 2 == 0:
                            pe.wait_ge(sem("y_copied"), it * (OUTER // SLOTS) + (t0 // SLOTS + c // 2 + 1))
                        for j in range(QUAD * c, QUAD * (c + 1)):
                            s = j % SLOTS
                            pe.wait_ge(sem(f"v_arrived{s}"), it * (16 * OUTER // SLOTS) + 16 * (t0 // SLOTS + j // SLOTS + 1))
                            for hf in range(2):
                                last = mm(ps[0:SLOTS, yb + hf, :], acts[:, s, :], Vs[:, s, hf * 512:(hf + 1) * 512],
                                          start=(s == 0), stop=(s == SLOTS - 1))
                            last.then_inc(sem("outputs"), 1)

                    if n == 0:
                        pe.sem_inc(sem("outputs"), SLOTS)
                    for j in range(QUAD):
                        spread_at(0, j)
                    with pe.Fori(0, P // OUTER - 1) as it:
                        body(it, False)
                    body(P // OUTER - 1, True)
                    pe.wait_ge(sem("dots"), t0 + P + SLOTS)
                    pe.wait_ge(sem("y_copied"), (t0 + P) // SLOTS + 2)
                    pe.wait_ge(sem("y_back"), 16 * (n + 1))
                    for a in range(2):
                        o = bank(("yt", n, a))
                        for k in range(4):
                            last = pe.transpose(o[:, k * P:(k + 1) * P], ytok[:, (4 * a + k) * P:(4 * a + k + 1) * P], ident[:, :])
                        full(last)

        def full_bank(eng, name):
            g = group[name]
            eng.wait_ge(sem("psum_full"), g + 1)
            return ps[:, g % NB, :]

        def free(name):
            return sem(f"bank_free{group[name] % NB}")

        @block.sync
        def _(sp):
            sp.dma_start(vec[:, :], A["vec"]).then_inc(sem("vec_loaded"), 16)
            sp.dma_start(ident[:, :], A["ident"]).then_inc(sem("ident_set"), 16)
            sp.dma_start(X[:, :, SEQ:], A["xT"]).then_inc(sem("x_loaded"), 16)

            def weight(i):
                if i >= RING:
                    sp.wait_ge(sem("w_used"), i - RING + 1)
                sp.dma_start(ring_slot(i), chunks[i][1]).then_inc(sem(f"w_arrived{i % RING}"), 16)

            for i in range(RING):
                weight(i)
            sp.dma_start(X[:, :, 0:SEQ], A["ctxT"]).then_inc(sem("ctx_loaded"), 16)
            sp.dma_start(mask1, A["mask"]).then_inc(sem("mask_loaded"), 16)
            sp.dma_start(wsg1, A["wsgT"]).then_inc(sem("wsg_loaded"), 16)
            for p in range(4):
                for a in range(2):
                    sp.dma_start(bsg1[64 * a:64 * a + 64, p, :], A["b_sgu"][0, 2 * p + a:2 * p + a + 1, :].to_broadcast([64, P])).then_inc(sem("bsg_loaded"), 16)
            sp.dma_start(dft[:, :, :], A["dft"]).then_inc(sem("const_loaded"), 16)
            sp.dma_start(dftc[:, :, :], A["dftc"]).then_inc(sem("const_loaded"), 16)
            sp.dma_start(ropet[:, :, :], A["rope"]).then_inc(sem("const_loaded"), 16)
            sp.dma_start(rotm[:, :], A["rotm"]).then_inc(sem("const_loaded"), 16)
            sp.dma_start(gqk[:, :], A["gqk"]).then_inc(sem("const_loaded"), 16)
            sp.dma_start(iota16[:, :], A["iota16"]).then_inc(sem("const_loaded"), 16)
            for i in range(RING, len(chunks)):
                weight(i)
            sp.wait_ge(sem("x_final"), 2)
            sp.dma_start(out, X[:, :, SEQ:]).then_inc(sem("stored"), 16)
            sp.wait_ge(sem("stored"), 16)

        var_no = [0]
        pows = []

        @block.vector
        def _(dve):
            chain = [0]

            def link(ins):
                chain[0] += 1
                ins.then_inc(sem("dve_chain"), 1)
                dve.wait_ge(sem("dve_chain"), chain[0])

            def var_step(name, o, r, n, m=P, width=TALL):
                p = full_bank(dve, name)
                link(dve.tensor_scalar(out=o, in0=p[0:m, 0:width], scalar1=1.0 / n, scalar2=EPS, op0=MUL, op1=ADD))
                dve.sem_inc(free(name), 1)
                dve.sem_inc(sem("var_ready"), 1)
                pows.append((o, r, m, width))
                return len(pows)

            def gate_norm(dst, gvec, scale, s):
                dve.scalar_tensor_tensor(out=dst, in0=scale, scalar=1.0, in1=gvec, op0=ADD, op1=MUL)

            def h_from(c0, c1, npow):
                dve.wait_ge(sem("rstd_ready"), npow)
                dve.tensor_tensor(out=H[:, :, c0:c1], in0=X[:, :, c0:c1],
                                  in1=rstd[:, c0:c1].unsqueeze(1).to_broadcast([P, DT, c1 - c0]), op=MUL).then_inc(sem("xn_ready"), 1)

            def attention(tag, prob, nk, scale, mask):
                for i in range(16 + 1):
                    if i < 16:
                        p = full_bank(dve, (tag, "s", i))
                        if mask is not None:
                            link(dve.tensor_tensor(out=p[:, 0:nk], in0=p[:, 0:nk], in1=mask[:, i % 2, :], op=ADD))
                        link(dve.tensor_reduce(out=stat[:, 0, i:i + 1], in_=p[:, 0:nk], axis=AX.X, op=ALU.max))
                        dve.tensor_scalar(out=stat[:, 1, i:i + 1], in0=stat[:, 0, i:i + 1], scalar1=-scale, scalar2=None, op0=MUL).then_inc(sem(f"{tag}_max"), 1)
                    if i >= 1:
                        dve.wait_ge(sem(f"{tag}_exp"), i)
                        link(dve.reciprocal(stat[:, 3, i - 1:i], stat[:, 2, i - 1:i]))
                        dve.tensor_scalar(out=prob[:, i - 1, 0:nk], in0=prob[:, i - 1, 0:nk], scalar1=stat[:, 3, i - 1:i], scalar2=None, op0=MUL).then_inc(sem(f"{tag}_probs"), 1)

            dve.memset(ones[:, :], 1.0).then_inc(sem("ones_set"), 1)
            dve.memset(minus_half[:, :], -0.5)
            dve.memset(acts[:, :, :], 0.0)
            dve.wait_ge(sem("ident_set"), 16)
            for i in range(3):
                last = dve.tensor_copy(selb[32 * i:32 * i + 32, :], ident[0:32, 0:32])
            last.then_inc(sem("sel_ready"), 1)
            dve.wait_ge(sem("vec_loaded"), 16)
            for i, name in enumerate(("c", "c_ctx_2", "c_2")):
                last = dve.tensor_scalar(out=cond[:, i, :], in0=V(name), scalar1=0.5, scalar2=None, op0=MUL)
            link(last)
            dve.sem_inc(sem("cond_half"), 1)
            dve.wait_ge(sem("cond_tanh"), 1)
            ct = condt[:, :].rearrange("p (a b) -> p a b", a=3)
            link(dve.scalar_tensor_tensor(out=cond[:, :, :], in0=ct, scalar=1.0, in1=cond[:, :, :], op0=ADD, op1=MUL))
            link(dve.tensor_copy(cond2[:, :, :], cond[:, 1:3, :].rearrange("p a k -> p k a")))
            dve.sem_inc(sem("cond_ready"), 1)
            def modulations1():
                p = full_bank(dve, "mod1")
                link(dve.tensor_tensor(out=mod1[:, :], in0=p[:, 0:48], in1=V("b_ada"), op=ADD))
                dve.sem_inc(free("mod1"), 1)
                gate_norm(gs[:, 0, :, 0], V("g_mix"), mod1[:, 8:16], 0)
                gate_norm(gs[:, 1, :, 0], V("g_ffn"), mod1[:, 32:40], 0)
                link(dve.tensor_scalar(out=half[:, :, 0], in0=mod1[:, 16:24], scalar1=0.5, scalar2=None, op0=MUL))
                dve.sem_inc(sem("mod_ready"), 1)

            modulations1()
            n = var_step("ss_n1", varb[:, SEQ:], rstd[:, SEQ:], D, width=SEQ)
            h_from(SEQ, TALL, n)
            dve.wait_ge(sem("vs_squares"), 2)
            link(dve.tensor_scalar(out=stat[:, 1, 0:2], in0=ssg1, scalar1=1.0 / SGU_W, scalar2=EPS, op0=MUL, op1=ADD))
            dve.sem_inc(sem("var_ready"), 1)
            pows.append((stat[:, 1, 0:2], stat[:, 2, 0:2], P, 2))
            dve.wait_ge(sem("rstd_ready"), len(pows))
            for c in range(2):
                last = dve.tensor_scalar(out=vs1[:, c, :], in0=vs1[:, c, :], scalar1=stat[:, 2, c:c + 1], scalar2=None, op0=MUL)
            link(last)
            dve.sem_inc(sem("sgu_ready"), 1)
            dve.wait_ge(sem("mask_loaded"), 16)
            attention("a1", P1, SEQ, 1.0, mask1)
            dve.wait_ge(sem("bsg_loaded"), 128)
            for p4 in range(4):
                p = full_bank(dve, ("sg", p4))
                for c in range(2):
                    for a in range(2):
                        rr = slice(64 * a, 64 * a + 64)
                        last = dve.scalar_tensor_tensor(out=ysg1[rr, p4, c * P:(c + 1) * P], in0=p[rr, c * SEQ + a * P:c * SEQ + (a + 1) * P],
                                                        scalar=V("g_sgu")[rr, p4:p4 + 1], in1=bsg1[rr, p4, :], op0=MUL, op1=ADD)
                link(last)
                dve.sem_inc(free(("sg", p4)), 1)
                dve.tensor_tensor(out=ysg1[:, p4, :], in0=ysg1[:, p4, :], in1=u1[:, p4, :], op=MUL).then_inc(sem("mix1_ready"), 1)
            dve.wait_ge(sem("gates1"), 16)
            for t in range(DT):
                p = full_bank(dve, ("mg1", t))
                link(dve.scalar_tensor_tensor(out=mt1[:, t % 2, :, :], in0=gate1[:, t, :, :], scalar=1.0,
                                              in1=p.rearrange("p (a b) -> p a b", a=2), op0=ADD, op1=MUL))
                dve.sem_inc(free(("mg1", t)), 1)
                dve.tensor_tensor(out=mrg1[:, t, :], in0=mt1[:, t % 2, 0, :], in1=mt1[:, t % 2, 1, :], op=ADD).then_inc(sem("merged1"), 1)

            def residual(name_of, gate, c0, c1, tiles=DT):
                for t in range(tiles):
                    p = full_bank(dve, name_of(t))
                    last = dve.scalar_tensor_tensor(out=X[:, t, c0:c1], in0=p[:, 0:c1 - c0], scalar=gate(t), in1=X[:, t, c0:c1], op0=MUL, op1=ADD)
                    last.then_inc(free(name_of(t)), 1)
                return last

            residual(lambda t: ("out1", t), lambda t: half[:, t, 0:1], SEQ, TALL)
            link(dve.memset(stat[:, 3, 0:1], 0.0))
            dve.sem_inc(sem("x_ready"), 1)
            n = var_step("ss_n2", varb[:, SEQ:], rstd[:, SEQ:], D, width=SEQ)
            h_from(SEQ, TALL, n)
            residual(lambda t: ("ffb", t), lambda t: mod1[:, 40 + t:41 + t], SEQ, TALL)
            link(dve.memset(stat[:, 3, 0:1], 0.0))
            dve.sem_inc(sem("x_ready"), 1)
            n = var_step("ss_n3", varb[:, SEQ:], rstd[:, SEQ:], D, width=SEQ)
            dve.wait_ge(sem("rstd_ready"), n)
            link(dve.tensor_tensor(out=X[:, :, SEQ:], in0=X[:, :, SEQ:], in1=rstd[:, SEQ:].unsqueeze(1).to_broadcast([P, DT, SEQ]), op=MUL))
            link(dve.tensor_tensor(out=X[:, :, SEQ:], in0=X[:, :, SEQ:], in1=V("g_final").unsqueeze(2).to_broadcast([P, DT, SEQ]), op=MUL))
            dve.sem_inc(sem("x_ready"), 1)
            tile_no = 0
            dve.wait_ge(sem("const_loaded"), 16 * 6)
            for l in range(LAYERS):
                c0 = QC[l]
                wq = TALL - c0
                p = full_bank(dve, ("mod2", l))
                link(dve.tensor_tensor(out=mod2[:, :, :], in0=p[:, 0:96].rearrange("p (a b) -> p a b", b=2),
                                       in1=V("b_mod", l).unsqueeze(2).to_broadcast([P, 48, 2]), op=ADD))
                dve.sem_inc(free(("mod2", l)), 1)
                for s in range(2):
                    gate_norm(gs[:, 0, :, s], V("g_norm1", l), mod2[:, 8:16, s], s)
                    gate_norm(gs[:, 1, :, s], V("g_norm2", l), mod2[:, 32:40, s], s)
                dve.tensor_scalar(out=lnh[:, 0:2], in0=V("g_cln", l), scalar1=0.5, scalar2=None, op0=MUL)
                dve.tensor_scalar(out=lnh[:, 2:4], in0=V("b_cln", l), scalar1=0.5, scalar2=None, op0=MUL)
                link(dve.tensor_scalar(out=half[:, :, :], in0=mod2[:, 16:24, :], scalar1=0.5, scalar2=None, op0=MUL))
                dve.sem_inc(sem("mod_ready"), 1)
                n = var_step(("ss_n1", l), varb[:, :], rstd[:, :], D)
                h_from(0, TALL, n)
                dve.wait_ge(sem("pad_clear"), l + 1)
                for c in range(2):
                    dve.wait_ge(sem("glu_parts"), 2 * l + c + 1)
                    s0 = c0 // SEQ
                    src = cth[:, c0:TALL].rearrange("p (s t) -> p s t", t=SEQ)
                    oth = cah[:, c0:TALL].rearrange("p (s t) -> p s t", t=SEQ)
                    link(dve.scalar_tensor_tensor(out=upad[:, c, s0:2, CV_W // 2:CV_W // 2 + SEQ], in0=src, scalar=1.0, in1=oth, op0=ADD, op1=MUL))
                    dve.sem_inc(sem("glu_done"), 1)
                n = var_step(("ss_ckv", l), varb[:, :], rstd[:, :], P)
                dve.wait_ge(sem("rstd_ready"), n)
                link(dve.scalar_tensor_tensor(out=ckvn, in0=ckv, scalar=V("g_ckv", l), in1=rstd[:, :], op0=MUL, op1=MUL))
                dve.sem_inc(sem("ckvn_ready"), 1)
                n = var_step(("ss_cq", l), varb[:, c0:], rstd[:, c0:], Q_LORA, width=wq)
                dve.wait_ge(sem("rstd_ready"), n)
                for t in range(2):
                    last = dve.scalar_tensor_tensor(out=cqn[:, t, c0:], in0=cq[:, t, c0:], scalar=V("g_cq", l)[:, t:t + 1], in1=rstd[:, c0:], op0=MUL, op1=MUL)
                link(last)
                dve.sem_inc(sem("cqn_ready"), 1)
                for w in range(CV_W):
                    for c in range(2):
                        s0 = c0 // SEQ
                        u = upad[:, c, s0:2, w:w + SEQ]
                        a = acc[:, c, c0:TALL].rearrange("p (s t) -> p s t", t=SEQ)
                        wt = V("w_dw", l)[:, c * CV_W + w:c * CV_W + w + 1]
                        if w == 0:
                            last = dve.tensor_scalar(out=a, in0=u, scalar1=wt, scalar2=V("b_dw", l)[:, c:c + 1], op0=MUL, op1=ADD)
                        else:
                            last = dve.scalar_tensor_tensor(out=a, in0=u, scalar=wt, in1=a, op0=MUL, op1=ADD)
                    link(last)
                dve.sem_inc(sem("conv_ready"), 1)
                p = full_bank(dve, ("cmean", l))
                link(dve.tensor_scalar(out=mu[:, c0:], in0=p[:, 0:wq], scalar1=1.0 / CV_C, scalar2=None, op0=MUL))
                dve.sem_inc(free(("cmean", l)), 1)
                link(dve.tensor_tensor(out=acc[:, :, c0:], in0=acc[:, :, c0:], in1=mu[:, c0:].unsqueeze(1).to_broadcast([P, 2, wq]), op=SUB))
                dve.sem_inc(sem("centred"), 1)
                n = var_step(("cvar", l), varb[:, c0:], rstd[:, c0:], CV_C, width=wq)
                dve.wait_ge(sem("rstd_ready"), n)
                link(dve.tensor_tensor(out=acc[:, :, c0:], in0=acc[:, :, c0:], in1=rstd[:, c0:].unsqueeze(1).to_broadcast([P, 2, wq]), op=MUL))
                dve.sem_inc(sem("ln_ready"), 1)
                dve.wait_ge(sem("ln_tanh"), l + 1)
                link(dve.scalar_tensor_tensor(out=br[:, 6:8, c0:], in0=csq[:, :, c0:], scalar=1.0, in1=acc[:, :, c0:], op0=ADD, op1=MUL))
                dve.sem_inc(sem("conv_done"), 1)
                for i in range(16 + 2):
                    if i < 16:
                        a = 0 if i < 8 else c0
                        var_step(("hs", l, i), hvar[:, i % 3, a:], hrs[:, i % 3, a:], QK, m=QK, width=TALL - a)
                        if i == 0:
                            first_pow = len(pows)
                    if 1 <= i <= 16:
                        k = i - 1
                        a = 0 if k < 8 else c0
                        dve.wait_ge(sem("rstd_ready"), first_pow + k)
                        gcol = gqk[:, 2 * l + (1 if k < 8 else 0):2 * l + (1 if k < 8 else 0) + 1]
                        link(dve.scalar_tensor_tensor(out=hqn[:, k % 3, a:], in0=hraw[:, k % 3, a:], scalar=gcol, in1=hrs[:, k % 3, a:], op0=MUL, op1=MUL))
                        dve.sem_inc(sem("head_normed"), 1)
                    if i >= 2:
                        k = i - 2
                        a = 0 if k < 8 else c0
                        dst = (kT if k < 8 else qT)[:, k % 8, a:]
                        p = full_bank(dve, ("hr", l, k))
                        dve.tensor_tensor(out=dst, in0=hqn[:, k % 3, a:], in1=ropet[:, 0, a:], op=MUL)
                        link(dve.tensor_tensor(out=htmp[:, a:], in0=p[0:QK, 0:TALL - a], in1=ropet[:, 1, a:], op=MUL))
                        dve.sem_inc(free(("hr", l, k)), 1)
                        link(dve.tensor_tensor(out=dst, in0=dst, in1=htmp[:, a:], op=ADD))
                        dve.sem_inc(sem("heads_ready"), 1)
                for tag, al, q0, nk in ATT:
                    if al == l:
                        attention(tag, P2, nk, QK ** -0.5, None)
                i = 0
                for j in range(2):
                    for b in range(3):
                        for t in range(4):
                            f = 4 * j + t
                            dve.wait_ge(sem("gates2"), 24 * l + i + 1)
                            p = full_bank(dve, ("br", l, j, b, t))
                            dst = m2[:, f, c0:] if b == 0 else br2[:, i % 2, c0:]
                            link(dve.scalar_tensor_tensor(out=dst, in0=sig2[:, i % 2, c0:], scalar=1.0, in1=p[:, 0:wq], op0=ADD, op1=MUL))
                            dve.sem_inc(free(("br", l, j, b, t)), 1)
                            dve.sem_inc(sem("gates_used"), 1)
                            if b:
                                link(dve.tensor_tensor(out=m2[:, f, c0:], in0=m2[:, f, c0:], in1=br2[:, i % 2, c0:], op=ADD))
                            if b == 2:
                                dve.sem_inc(sem("merged2"), 1)
                            i += 1
                for t in range(DT):
                    name = ("out2", l, t)
                    p = full_bank(dve, name)
                    for s in streams(l):
                        last = dve.scalar_tensor_tensor(out=X[:, t, s * SEQ:(s + 1) * SEQ], in0=p[:, s * SEQ - c0:(s + 1) * SEQ - c0],
                                                        scalar=half[:, t, s:s + 1], in1=X[:, t, s * SEQ:(s + 1) * SEQ], op0=MUL, op1=ADD)
                    last.then_inc(free(name), 1)
                link(dve.memset(stat[:, 3, 0:1], 0.0))
                dve.sem_inc(sem("x_ready"), 1)
                n = var_step(("ss_n2", l), varb[:, c0:], rstd[:, c0:], D, width=wq)
                h_from(c0, TALL, n)
                for tt in [t for ll, t in TILES if ll == l]:
                    n = tile_no
                    tile_no += 1
                    t0 = n * P
                    s = tt // 2
                    for a in range(2):
                        dve.wait_ge(sem("part1"), 2 * n + a + 1)
                        p = full_bank(dve, ("ht", n, a))
                        link(dve.tensor_tensor(out=hres[:, a * 512:(a + 1) * 512], in0=p, in1=hp1[:, a * 512:(a + 1) * 512], op=SUB))
                        dve.sem_inc(free(("ht", n, a)), 1)
                    dve.sem_inc(sem("residue"), 1)
                    dve.wait_ge(sem("part2"), n + 1)
                    link(dve.tensor_tensor(out=hp3[:, :], in0=hres[:, :], in1=hp2[:, :], op=SUB))
                    for i, part in enumerate((hp1, hp2, hp3)):
                        for g in range(4):
                            last = dve.tensor_copy(hs[32 * i:32 * i + 32, g, :], part[32 * g:32 * g + 32, :])
                    link(last)
                    dve.sem_inc(sem("hs_ready"), 1)
                    dve.wait_ge(sem("scores_ready"), 4 * (n + 1))
                    R16 = range(16)
                    for i in R16:
                        last = dve.max(top[:, i, 0:8], sc[:, i, :])
                    link(last)
                    for i in R16:
                        last = dve.max_index(tix[:, i, 0:8], top[:, i, 0:8], sc[:, i, :])
                    link(last)
                    for i in R16:
                        last = dve.match_replace(sc[:, i, :], top[:, i, 0:8], sc[:, i, :], -3.0e38)
                    link(last)
                    for i in R16:
                        last = dve.max(top[:, i, 8:16], sc[:, i, :])
                    link(last)
                    for i in R16:
                        last = dve.max_index(tix[:, i, 8:16], top[:, i, 8:16], sc[:, i, :])
                    link(last)
                    dve.tensor_copy(tixf[:, :, :], tix[:, :, :])
                    t4 = top[:, :, :].rearrange("p (h q) k -> p h q k", q=2)
                    f4 = tixf[:, :, :].rearrange("p (h q) k -> p h q k", q=2)
                    full4 = [P, PH, TOPK, TOPK]
                    link(dve.tensor_tensor(out=cand.rearrange("p h (i j) -> p h i j", j=TOPK),
                                           in0=t4[:, :, 0, :].unsqueeze(3).to_broadcast(full4),
                                           in1=t4[:, :, 1, :].unsqueeze(2).to_broadcast(full4), op=ADD))
                    R8 = range(PH)
                    for i in R8:
                        last = dve.max(best[:, i, 0:8], cand[:, i, :])
                    link(last)
                    for i in R8:
                        last = dve.max_index(pos[:, i, 0:8], best[:, i, 0:8], cand[:, i, :])
                    link(last)
                    for i in R8:
                        last = dve.match_replace(cand[:, i, :], best[:, i, 0:8], cand[:, i, :], -3.0e38)
                    link(last)
                    for i in R8:
                        last = dve.max(best[:, i, 8:16], cand[:, i, :])
                    link(last)
                    for i in R8:
                        last = dve.max_index(pos[:, i, 8:16], best[:, i, 8:16], cand[:, i, :])
                    link(last)
                    link(dve.tensor_tensor(out=gat[:, :, :], in0=best[:, :, :], in1=best[:, :, 0:1].to_broadcast([P, PH, TOPK]), op=SUB))
                    dve.sem_inc(sem("best_ready"), 1)
                    posv = pos[:, :, :].rearrange("p a b -> p (a b)")
                    dve.tensor_scalar(out=posi[:, 0, :], in0=posv, scalar1=4, scalar2=None, op0=ALU.logical_shift_right)
                    link(dve.tensor_scalar(out=posi[:, 1, :], in0=posv, scalar1=15, scalar2=None, op0=ALU.bitwise_and))
                    link(dve.tensor_copy(posf[:, :, :, :].rearrange("p a b c -> p (a b c)"), posi[:, :, :].rearrange("p a b -> p (a b)")))
                    for a in range(2):
                        link(dve.tensor_tensor(out=eqp, in0=posf[:, a, :, :].unsqueeze(3).to_broadcast(full4),
                                               in1=iota16[:, :].unsqueeze(1).unsqueeze(1).to_broadcast(full4), op=ALU.is_equal))
                        link(dve.tensor_tensor(out=eqp, in0=eqp, in1=f4[:, :, a, :].unsqueeze(2).to_broadcast(full4), op=MUL))
                        link(dve.tensor_reduce(out=ij[:, a, :, :], in_=eqp, axis=AX.X, op=ADD))
                    link(dve.scalar_tensor_tensor(out=eid[:, :], in0=ij[:, 0, :, :].rearrange("p a b -> p (a b)"), scalar=float(NKEY),
                                                  in1=ij[:, 1, :, :].rearrange("p a b -> p (a b)"), op0=MUL, op1=ADD))
                    dve.wait_ge(sem("best_exp"), n + 1)
                    link(dve.tensor_reduce(out=gsum[:, 0, :], in_=gat[:, :, :], axis=AX.X, op=ADD))
                    link(dve.reciprocal(gsum[:, 1, :], gsum[:, 0, :]))
                    link(dve.tensor_tensor(out=gat[:, :, :], in0=gat[:, :, :], in1=gsum[:, 1, :].unsqueeze(2).to_broadcast([P, PH, TOPK]), op=MUL))
                    dve.sem_inc(sem("routed"), 1)
                    p = full_bank(dve, ("ij", n))
                    dve.tensor_scalar(out=idxT[:, :], in0=p[:, 0:P], scalar1=float(l * NEXP), scalar2=None, op0=ADD)
                    link(dve.tensor_copy(gateT[:, :], p[:, P:2 * P]))
                    dve.sem_inc(free(("ij", n)), 1)
                    dve.sem_inc(sem("idx_ready"), 1)
                    if n == 0:
                        dve.sem_inc(sem("dots"), SLOTS)
                    with dve.Fori(0, P // SLOTS) as it:
                        for j in range(SLOTS):
                            dve.wait_ge(sem(f"u_arrived{j}"), it * 16 + 16 * (t0 // SLOTS + 1))
                            dve.wait_ge(sem("spread"), it * SLOTS + (t0 + j + 1))
                            if j % QUAD == 0:
                                dve.wait_ge(sem("gelus"), it * 2 + (t0 // QUAD + j // QUAD + 1))
                            dve.scalar_tensor_tensor(out=Us[:, j, :], in0=ps[:, 2 * (j % 2):2 * (j % 2) + 2, :].rearrange("p a b -> p (a b)"),
                                                     scalar=1.0, in1=Us[:, j, :], op0=MUL, op1=MUL, accum_out=dots[:, j:j + 1]).then_inc(sem("dots"), 1)
                            if j % QUAD == QUAD - 1:
                                a = j - QUAD + 1
                                dve.wait_ge(sem("gelus"), it * 2 + (t0 // QUAD + j // QUAD + 3))
                                dve.wait_ge(sem("outputs"), it * SLOTS + (t0 + j + 1))
                                diag = acts[:, :, :].rearrange("p a b -> p (a b)")[:, a * (SLOTS + 1):(a + QUAD - 1) * (SLOTS + 1) + 1:SLOTS + 1]
                                dve.tensor_tensor(out=diag, in0=gel[:, a:a + QUAD], in1=gateT[:, bass.ds(it * SLOTS + a, QUAD)], op=MUL).then_inc(sem("acts"), 1)
                    for a in range(2):
                        p = full_bank(dve, ("yt", n, a))
                        for k in range(4):
                            f = 4 * a + k
                            last = dve.scalar_tensor_tensor(out=X[:, f, tt * P:(tt + 1) * P], in0=p[:, k * P:(k + 1) * P], scalar=mod2[:, 40 + f, s:s + 1],
                                                            in1=X[:, f, tt * P:(tt + 1) * P], op0=MUL, op1=ADD)
                        link(last)
                        dve.sem_inc(free(("yt", n, a)), 1)
                dve.sem_inc(sem("x_ready"), 1)
                dve.sem_inc(sem("x_final"), 1)

        @block.scalar
        def _(act):
            link_no = [0]

            def link(ins):
                link_no[0] += 1
                ins.then_inc(sem("act_chain"), 1)
                act.wait_ge(sem("act_chain"), link_no[0])

            def A_(o, i, f=ACT.Copy, **kw):
                return act.activation(o, i, f, **kw)

            def evac(name, o, m=slice(0, P), width=None, f=ACT.Copy, **kw):
                p = full_bank(act, name)
                return A_(o, p[m, 0:width] if width else p[m, :], f, **kw)

            def squares(c0, c1, dst, xr):
                act.wait_ge(*xr)
                A_(dst[:, :, c0:c1] if dst is sqx else dst, X[:, :, c0:c1], ACT.Square).then_inc(sem("squares_ready"), 1)

            def modulate(which, nh, mod, shift, ss, c0, nmod):
                act.wait_ge(sem("xn_ready"), nh)
                act.wait_ge(sem("mod_ready"), nmod)
                for k in range(DT):
                    for s in ss:
                        cs = slice(max(c0, s * SEQ), (s + 1) * SEQ)
                        gi = 0 if mod is mod1 else s
                        bias = mod[:, shift + k:shift + k + 1] if mod is mod1 else mod[:, shift + k, s:s + 1]
                        last = A_(H[:, k, cs], H[:, k, cs], ACT.Identity, bias=bias, scale=gs[:, which, k, gi:gi + 1])
                last.then_inc(sem("h_ready"), 1)

            def attention(tag, prob, pt, dst, nk, scale, done):
                kts = nk // P
                for i in range(16 + 5):
                    if i < 16:
                        act.wait_ge(sem(f"{tag}_max"), i + 1)
                        p = full_bank(act, (tag, "s", i))
                        link(A_(prob[:, i, 0:nk], p[:, 0:nk], ACT.Exp, bias=stat[:, 1, i:i + 1], scale=scale, accum_out=stat[:, 2, i:i + 1]))
                        act.sem_inc(free((tag, "s", i)), 1)
                        act.sem_inc(sem(f"{tag}_exp"), 1)
                    if 0 <= i - 3 < 16:
                        h, t = (i - 3) // 2, (i - 3) % 2
                        p = full_bank(act, (tag, "t", i - 3))
                        link(A_(pt[:, h % 2, 0:kts, t * P:(t + 1) * P], p[:, 0:nk].rearrange("p (k q) -> p k q", q=P)))
                        act.sem_inc(free((tag, "t", i - 3)), 1)
                        act.sem_inc(sem(f"{tag}_probsT"), 1)
                    if 0 <= i - 5 < 16 and (i - 5) % 2:
                        h = (i - 5) // 2
                        r = slice(64 * (h % 2), 64 * (h % 2) + 64)
                        link(evac((tag, "o", h), dst(h)[r], m=r, width=SEQ))
                        act.sem_inc(free((tag, "o", h)), 1)
                        act.sem_inc(sem(done), 1)

            act.wait_ge(sem("cond_half"), 1)
            A_(condt[:, :], cond[:, :, :].rearrange("p a b -> p (a b)"), ACT.Tanh).then_inc(sem("cond_tanh"), 1)
            squares(SEQ, TALL, sq1, (sem("x_loaded"), 16))
            modulate(0, 1, mod1, 0, [1], SEQ, 1)
            for j in range(9):
                for t in range(4):
                    if j in (2, 4) and t >= 2:
                        continue
                    name = ("in1", j, t)
                    if j == 0:
                        ins = evac(name, q1[:, t, :], width=SEQ, scale=HD1 ** -0.5)
                    elif j == 1:
                        ins = evac(name, k1[:, t, :], width=SEQ)
                    elif j == 2:
                        ins = evac(name, v1[:, t, :])
                    elif j == 3:
                        ins = evac(name, u1[:, t, :], width=SEQ, f=ACT.Gelu_apprx_tanh)
                    elif j == 4:
                        ins = evac(name, vs1[:, t, :], f=ACT.Gelu_apprx_tanh)
                    else:
                        g = 4 * ((j - 5) % 2) + t
                        ins = evac(name, gate1[:, g, (j - 5) // 2, :], width=SEQ, f=ACT.Tanh, scale=0.5)
                    link(ins)
                    act.sem_inc(free(name), 1)
                    if j < 3:
                        act.sem_inc(sem("qkv1_ready"), 1)
                    if j == 4:
                        A_(vsq1[:, t, :], vs1[:, t, :], ACT.Square, accum_out=ssg1[:, t:t + 1]).then_inc(sem("vs_squares"), 1)
                    if j > 4:
                        act.sem_inc(sem("gates1"), 1)
            attention("a1", P1, PT1, lambda h: att1[:, h // 2, :], SEQ, 1.0, "mix1_ready")
            squares(SEQ, TALL, sq1, (sem("x_ready"), 1))
            modulate(1, 2, mod1, 24, [1], SEQ, 1)
            for t in range(FF_T):
                link(evac(("ffa", t), ff1[:, t, :], width=SEQ, f=ACT.Relu))
                act.sem_inc(free(("ffa", t)), 1)
                A_(ff1[:, t, :], ff1[:, t, :], ACT.Square).then_inc(sem("ff_ready"), 1)
            squares(SEQ, TALL, sq1, (sem("x_ready"), 2))
            tile_no = 0
            nh = 2
            nx = 3
            for l in range(LAYERS):
                c0 = QC[l]
                wq = TALL - c0
                if l == 0:
                    act.wait_ge(sem("ctx_loaded"), 16)
                squares(0, TALL, sqx, (sem("x_ready"), nx))
                nh += 1
                modulate(0, nh, mod2, 0, [0, 1], 0, 2 + l)
                link(evac(("ckv", l), ckv))
                A_(lsq[:, 0, :], ckv, ACT.Square).then_inc(sem("lat_squares"), 1)
                act.sem_inc(free(("ckv", l)), 1)
                p = full_bank(act, ("kr", l))
                for i in range(3):
                    A_(hraw[NOPE:QK, i, :], p[NOPE:QK, :])
                    last = A_(hsq[NOPE:QK, i, :], p[NOPE:QK, :], ACT.Square)
                last.then_inc(free(("kr", l)), 1)
                for t in range(2):
                    link(evac(("cq", l, t), cq[:, t, c0:], width=wq))
                    act.sem_inc(free(("cq", l, t)), 1)
                A_(lsq[:, 1:3, c0:], cq[:, :, c0:], ACT.Square).then_inc(sem("lat_squares"), 1)
                for t in range(c0 // P, 4):
                    link(evac(("zf", l, t), zft[:, t, :], width=FN_C))
                    act.sem_inc(free(("zf", l, t)), 1)
                    act.sem_inc(sem("zf_ready"), 1)
                for c in range(2):
                    if c or l:
                        act.wait_ge(sem("glu_done"), 2 * l + c)
                    link(evac(("zc", l, c), cah[:, c0:], width=wq, scale=0.5))
                    act.sem_inc(free(("zc", l, c)), 1)
                    link(evac(("zc", l, 2 + c), cth[:, c0:], width=wq, f=ACT.Tanh, scale=0.5))
                    act.sem_inc(free(("zc", l, 2 + c)), 1)
                    act.sem_inc(sem("glu_parts"), 1)
                for s in streams(l):
                    for c in range(2):
                        link(evac(("dt", l, s, c), g1f[:, 2 * s + c, :]))
                        act.sem_inc(free(("dt", l, s, c)), 1)
                        act.sem_inc(sem("dft_ready"), 1)
                for s in streams(l):
                    p = full_bank(act, ("dc", l, s))
                    A_(br[:, 4:6, s * SEQ:(s + 1) * SEQ], p.rearrange("p (a b) -> p a b", a=2)).then_inc(free(("dc", l, s)), 1)
                for t in range(4):
                    evac(("v", l, t), vtok[:, t, :]).then_inc(free(("v", l, t)), 1)
                act.wait_ge(sem("centred"), l + 1)
                A_(csq[:, :, c0:], acc[:, :, c0:], ACT.Square).then_inc(sem("conv_squares"), 1)
                act.wait_ge(sem("ln_ready"), l + 1)
                for c in range(2):
                    last = A_(acc[:, c, c0:], acc[:, c, c0:], ACT.Identity, scale=lnh[:, c:c + 1], bias=lnh[:, 2 + c:3 + c])
                link(last)
                A_(csq[:, :, c0:], acc[:, :, c0:], ACT.Tanh).then_inc(sem("ln_tanh"), 1)
                for i in range(16):
                    a = 0 if i < 8 else c0
                    m = slice(0, NOPE) if i < 8 else slice(0, QK)
                    p = full_bank(act, ("hp", l, i))
                    if i >= 3:
                        act.wait_ge(sem("head_normed"), 16 * l + i - 2)
                    A_(hraw[m, i % 3, a:], p[m, 0:TALL - a])
                    link(A_(hsq[m, i % 3, a:], p[m, 0:TALL - a], ACT.Square))
                    act.sem_inc(free(("hp", l, i)), 1)
                    act.sem_inc(sem("head_squares"), 1)
                for tag, al, q0, nk in ATT:
                    if al == l:
                        attention(tag, P2, PT2, lambda h: br[:, h // 2, q0:q0 + SEQ], nk, QK ** -0.5, "att_ready")
                i = 0
                for j in range(2):
                    for b in range(3):
                        for t in range(4):
                            if 24 * l + i >= 2:
                                act.wait_ge(sem("gates_used"), 24 * l + i - 1)
                            link(evac(("zg", l, j, b, t), sig2[:, i % 2, c0:], width=wq, f=ACT.Tanh, scale=0.5))
                            act.sem_inc(free(("zg", l, j, b, t)), 1)
                            act.sem_inc(sem("gates2"), 1)
                            i += 1
                nx += 1
                squares(c0, TALL, sqx, (sem("x_ready"), nx))
                nh += 1
                modulate(1, nh, mod2, 24, streams(l), c0, 2 + l)
                for t in range(DT):
                    link(evac(("wq", l, t), qp[:, t, c0:], width=wq))
                    act.sem_inc(free(("wq", l, t)), 1)
                    act.sem_inc(sem("query_ready"), 1)
                for tt in [t for ll, t in TILES if ll == l]:
                    n = tile_no
                    tile_no += 1
                    t0 = n * P
                    if n:
                        g = group[("yt", n - 1, 1)]
                        act.wait_ge(sem("psum_full"), g + 1)
                    for a in range(2):
                        evac(("ht", n, a), hp1[:, a * 512:(a + 1) * 512]).then_inc(sem("part1"), 1)
                    act.wait_ge(sem("residue"), n + 1)
                    A_(hp2, hres).then_inc(sem("part2"), 1)
                    act.wait_ge(sem("hs_ready"), n + 1)
                    s4 = sc.rearrange("p (h q) k -> p h q k", q=2)
                    for a in range(2):
                        for q in range(2):
                            p = full_bank(act, ("sc", n, a, q))
                            link(A_(s4[:, 4 * a:4 * a + 4, q, :], p.rearrange("p (a b) -> p a b", b=P)))
                            act.sem_inc(free(("sc", n, a, q)), 1)
                            act.sem_inc(sem("scores_ready"), 1)
                    act.wait_ge(sem("best_ready"), n + 1)
                    A_(gat[:, :, :], gat[:, :, :], ACT.Exp).then_inc(sem("best_exp"), 1)
                    if n == 0:
                        act.sem_inc(sem("gelus"), 2)
                        act.sem_inc(sem("y_copied"), 2)
                        for b in range(2):
                            act.sem_inc(sem(f"y_out{b}"), 16)
                    with act.Fori(0, P // (2 * SLOTS)) as it:
                        for b in range(2):
                            for hf in range(2):
                                q0 = QUAD * hf
                                act.wait_ge(sem("dots"), it * 2 * SLOTS + (t0 + SLOTS + b * SLOTS + q0 + QUAD))
                                A_(gel[:, q0:q0 + QUAD], dots[:, q0:q0 + QUAD], ACT.Gelu_apprx_tanh).then_inc(sem("gelus"), 1)
                            act.wait_ge(sem("outputs"), it * 2 * SLOTS + (t0 + SLOTS + (b + 1) * SLOTS))
                            act.wait_ge(sem(f"y_out{b}"), it * 16 + 16 * (t0 // (2 * SLOTS)) + 16)
                            A_(yev[:, b, :], ps[0:SLOTS, 4 + 2 * b:6 + 2 * b, :].rearrange("p a b -> p (a b)")).then_inc(sem("y_copied"), 1)
                            act.wait_ge(sem("y_copied"), it * 2 + (t0 // SLOTS + b + 3))
                            act.dma_start(yscr[bass.ds(it * 2 * SLOTS + t0 + b * SLOTS, SLOTS), :], yev[:, b, :]).then_inc(sem(f"y_out{b}"), 16)
                    for b in range(2):
                        act.wait_ge(sem(f"y_out{b}"), 16 + 16 * (P // (2 * SLOTS)) * (n + 1))
                    act.dma_start(ytok, yscr[t0:t0 + P, :]).then_inc(sem("y_back"), 16)
                nx += 1

        @block.gpsimd
        def _(pool):
            def raise_(i):
                o, r, m, width = pows[i]
                pool.wait_ge(sem("var_ready"), i + 1)
                pool.tensor_tensor(out=r, in0=o, in1=minus_half[0:m, 0:1].to_broadcast([m, width]), op=ALU.pow).then_inc(sem("rstd_ready"), 1)

            pool.wait_ge(sem("wsg_loaded"), 16)
            pool.affine_select(out=wsg1, in_=wsg1, compare_op=ALU.is_ge, fill=0.0, base=0,
                               pattern=[[0, SGU_G], [1, P]], channel_multiplier=-1).then_inc(sem("sgu_ready"), 1)
            at = 0
            for i in range(4):
                raise_(at)
                at += 1
            tile_no = 0
            for l in range(LAYERS):
                raise_(at)
                at += 1
                for e in (0, SEQ + CV_W // 2):
                    last = pool.memset(upad[:, :, :, e:e + CV_W // 2], 0.0)
                last.then_inc(sem("pad_clear"), 1)
                for i in range(3 + 16 + 1):
                    raise_(at)
                    at += 1
                for tt in [t for ll, t in TILES if ll == l]:
                    n = tile_no
                    tile_no += 1
                    t0 = n * P
                    pool.wait_ge(sem("idx_ready"), n + 1)
                    with pool.Fori(0, P // SLOTS) as it:
                        for hf in range(2):
                            pool.wait_ge(sem("dots"), it * SLOTS + (t0 + QUAD * hf + QUAD))
                            pool.wait_ge(sem("outputs"), it * SLOTS + (t0 + QUAD * hf + QUAD))
                            pool.sem_inc(sem("pool_paced"), 1)
                            pool.tensor_copy(idl[:, hf, :], idxT[:, bass.ds(it * SLOTS + QUAD * hf, QUAD)]).then_inc(sem("idl_ready"), 1)
                            pool.wait_ge(sem("idl_ready"), it * 2 + (2 * (t0 // SLOTS) + hf + 1))
                            pool.sem_inc(sem("pool_paced"), 1)
                            for j in range(QUAD):
                                s = QUAD * hf + j
                                off = bass.IndirectOffsetOnAxis(idl[:, hf, j:j + 1], 0)
                                pool.indirect_dma_start(Us[:, s, :], None, A["u_tab"], off).then_inc(sem(f"u_arrived{s}"), 16)
                                pool.indirect_dma_start(Vs[:, s, :], None, A["v_tab"], off).then_inc(sem(f"v_arrived{s}"), 16)


def _columns(v):
    return v.reshape(-1, P).T


def kernel(**inputs):
    import numpy as np
    import concourse.bacc as bacc
    from concourse.bass_utils import run_bass_kernel_spmd

    I = {k: np.asarray(v) for k, v in inputs.items()}
    arrays = {}
    for name in ("w_ada", "w_in", "w_proj_attn", "w_proj_sgu", "w_out", "w_ff1", "w_ff2", "b_sgu", "w_mod_2", "w_in_2", "w_ukv_2",
                 "w_uq_2", "wb_attn_2", "wb_fnet_2", "wb_conv_2", "w_out_2", "w_query_2"):
        arrays[name] = np.ascontiguousarray(I[name])
    arrays["u_tab"] = np.ascontiguousarray(I["u_tab_2"]).reshape(LAYERS * NEXP, D)
    arrays["v_tab"] = np.ascontiguousarray(I["v_tab_2"]).reshape(LAYERS * NEXP, D)
    cols = [_columns(I[n].reshape(-1)) for n in ("c", "b_ada", "g_mix", "g_sgu", "g_ffn", "g_final", "c_ctx_2", "c_2")]
    for l in range(LAYERS):
        for n in ("b_mod_2", "g_norm1_2", "g_ckv_2", "g_cq_2", "b_dw_2", "g_cln_2", "b_cln_2"):
            cols.append(_columns(I[n][l]))
        cols.append(I["w_dw_2"][l, :, 0, :].reshape(CV_W, 2, P).transpose(2, 1, 0).reshape(P, 2 * CV_W))
        cols.append(_columns(I["g_norm2_2"][l]))
    arrays["vec"] = np.ascontiguousarray(np.concatenate(cols, axis=1))
    arrays["xT"] = np.ascontiguousarray(I["x"][0].T.reshape(DT, P, SEQ).transpose(1, 0, 2))
    arrays["ctxT"] = np.ascontiguousarray(I["ctx_2"][0].T.reshape(DT, P, SEQ).transpose(1, 0, 2))
    arrays["wsgT"] = np.ascontiguousarray(I["w_sgu"][0].transpose(2, 0, 1))
    arrays["keys"] = np.ascontiguousarray(I["sub_keys_2"].transpose(0, 2, 4, 1, 3).reshape(LAYERS, P, PH, NKEY))
    arrays["gqk"] = np.ascontiguousarray(np.stack([I["g_qn_2"][0], I["g_kn_2"][0], I["g_qn_2"][1], I["g_kn_2"][1]], axis=1))

    f = np.float32
    arrays["ident"] = np.eye(P, dtype=f)
    key, q = np.arange(SEQ), np.arange(P)
    arrays["mask"] = np.stack([np.where(key[None, :] <= (t * P + q)[:, None], 0.0, -1e30) for t in range(2)], axis=1).astype(f)
    w = 2 * np.pi * (np.arange(SEQ)[:, None] * np.arange(SEQ)[None, :] % SEQ) / SEQ
    both = np.concatenate([np.cos(w), np.sin(w)], axis=1)
    arrays["dft"] = np.ascontiguousarray(both.reshape(2, P, 512).transpose(1, 0, 2)).astype(f)
    w = 2 * np.pi * (np.arange(64)[:, None] * np.arange(64)[None, :] % 64) / 64
    arrays["dftc"] = np.stack([np.kron(np.eye(2), np.cos(w)), -np.kron(np.eye(2), np.sin(w))], axis=1).astype(f) / f(128.0)
    half = ROPE // 2
    inv = np.power(f(10000.0), -np.arange(0, half, 2, dtype=f) / f(half)).astype(f)
    row, col = np.arange(SEQ) // 64, np.arange(SEQ) % 64
    ar, ac = row[:, None].astype(f) * inv, col[:, None].astype(f) * inv
    ang = np.concatenate([ar, ar, ac, ac], axis=1)
    rope = np.zeros((QK, 2, TALL), f)
    rope[:, 0, :] = 1.0
    rope[NOPE:, 0, SEQ:] = np.cos(ang).T
    rope[NOPE:, 1, SEQ:] = np.sin(ang).T
    arrays["rope"] = rope
    rot = np.zeros((QK, QK), f)
    for a in range(2):
        for i in range(8):
            lo = NOPE + 16 * a + i
            rot[lo + 8, lo] = -1.0
            rot[lo, lo + 8] = 1.0
    arrays["rotm"] = rot
    arrays["iota16"] = np.tile(np.arange(TOPK, dtype=f), (P, 1))

    nc = bacc.Bacc("TRN2", target_bir_lowering=False, num_devices=1)
    A = {}
    for name, a in arrays.items():
        A[name] = nc.dram_tensor(f"in_{name}", a.shape, mybir.dt.from_np(a.dtype), kind="ExternalInput").ap()
    out = nc.dram_tensor("out_x", (P, DT, SEQ), mybir.dt.float32, kind="ExternalOutput").ap()
    two_blocks_kernel(nc, A, out)
    r = run_bass_kernel_spmd(nc, [{f"in_{k}": v for k, v in arrays.items()}], core_ids=[0])
    y = r.results[0]["out_x"]
    return np.ascontiguousarray(y.transpose(1, 0, 2).reshape(D, SEQ).T)[None]
```

```python
import concourse.bass as bass
from concourse import mybir
from contextlib import ExitStack

P = 128
D = 1024
DT = D // P
SEQ = 256
TALL = 2 * SEQ
EPS = 1e-6
LAYERS = 2

HEADS1, HD1 = 8, 64
SGU_W, SGU_G = 512, 8
FF_T = 4096 // P

MH, QK, NOPE, ROPE, VH = 8, 96, 64, 32, 64
KV_IN, Q_LORA, FN_C, CV_C, CV_W = 160, 256, 256, 256, 31
COL_ZF = KV_IN + Q_LORA
COL_ZC = COL_ZF + FN_C
COL_ZG = COL_ZC + 2 * CV_C
PH, NKEY, TOPK = 8, 128, 16
NEXP = NKEY * NKEY

SLOTS = 8
QUAD = 4
GROUP = 32
SEG = 16

VEC = {}
_at = 0
for _n, _w in [("c", 8), ("b_ada", 48), ("g_mix", 8), ("g_sgu", 4), ("g_ffn", 8), ("g_final", 8),
               ("c_ctx_2", 8), ("c_2", 8)]:
    VEC[_n] = (_at, _w)
    _at += _w
for _l in range(LAYERS):
    for _n, _w in [("b_mod", 48), ("g_norm1", 8), ("g_ckv", 1), ("g_cq", 2), ("b_dw", 2), ("g_cln", 2),
                   ("b_cln", 2), ("w_dw", 2 * CV_W), ("g_norm2", 8)]:
        VEC[_n, _l] = (_at, _w)
        _at += _w
NVEC = _at


def two_blocks_kernel(nc, A, out):
    f32, bf16, u32 = mybir.dt.float32, mybir.dt.bfloat16, mybir.dt.uint32
    ALU = mybir.AluOpType
    ACT = mybir.ActivationFunctionType
    AX = mybir.AxisListType
    MUL, ADD, SUB = ALU.mult, ALU.add, ALU.subtract

    ctx = ExitStack()
    with ctx:
        def sb(name, shape, dt=f32):
            return ctx.enter_context(nc.sbuf_tensor(name, shape, dt))

        sems = {}

        def sem(name):
            if name not in sems:
                sems[name] = ctx.enter_context(nc.semaphore(name))
            return sems[name]

        X = sb("X", [P, DT, TALL])
        H = sb("H", [P, DT, TALL])
        RING = 2
        W = sb("W", [P, RING, 4096])
        vec = sb("vec", [P, NVEC])
        ident = sb("ident", [P, P])
        ones = sb("ones", [P, P])
        dft = sb("dft", [P, 2, 512])
        dftc = sb("dftc", [P, 2, P])
        ropet = sb("ropet", [QK, 2, TALL])
        rotm = sb("rotm", [QK, QK])
        gqk = sb("gqk", [QK, 2 * LAYERS])
        iota16 = sb("iota16", [P, TOPK])
        selb = sb("selb", [96, 32], bf16)
        cond = sb("cond", [P, 3, DT])
        condt = sb("condt", [P, 3 * DT])
        cond2 = sb("cond2", [P, DT, 2])
        mod1 = sb("mod1", [P, 48])
        mod2 = sb("mod2", [P, LAYERS, 48, 2])
        onecol = sb("onecol", [P, 31])
        gs = sb("gs", [P, 2, DT, 2])
        half = sb("half", [P, DT, 2])
        lnh = sb("lnh", [P, 4])
        stat = sb("stat", [P, 4, 16])
        varb = sb("varb", [P, TALL])
        rstd = sb("rstd", [P, TALL])
        idxT = sb("idxT", [P, 2, P], u32)
        gateT = sb("gateT", [P, 2, P])
        idl = sb("idl", [P, 4, QUAD], u32)
        dots = sb("dots", [P, SLOTS])
        gel = sb("gel", [P, SLOTS])
        acts = sb("acts", [P, SLOTS, SLOTS])
        yev = sb("yev", [SLOTS, D])
        ARENA = 30208
        arena = sb("arena", [P, ARENA])

        def view(at, *shape, dt=None, parts=P):
            n = 1
            for s in shape:
                n *= s
            words = n if dt is None else (n + 1) // 2
            assert at + words <= ARENA
            ap = arena[0:parts, at:at + words]
            if dt is not None:
                ap = ap.bitcast(dt)
            if len(shape) == 2:
                ap = ap.rearrange("p (a b) -> p a b", b=shape[1])
            if len(shape) == 3:
                ap = ap.rearrange("p (a b c) -> p a b c", b=shape[1], c=shape[2])
            if len(shape) == 4:
                ap = ap.rearrange("p (a b c d) -> p a b c d", b=shape[1], c=shape[2], d=shape[3])
            return ap

        q1 = view(0, 4, SEQ)
        k1 = view(1024, 4, SEQ)
        v1 = view(2048, 2, 512)
        u1 = view(3072, 4, SEQ)
        vs1 = view(4096, 2, SGU_W)
        vsq1 = view(5120, 2, SGU_W)
        gate1 = view(6144, DT, 2, SEQ)
        P1 = view(10240, 16, SEQ)
        PT1 = view(14336, 2, 2, SEQ)
        att1 = view(15360, 4, SEQ)
        ysg1 = view(16384, 4, SEQ)
        wsg1 = view(17408, SGU_G, P)
        bsg1 = view(18432, 4, P)
        mrg1 = view(18944, DT, SEQ)
        sq1 = view(20992, DT, SEQ)
        mask1 = view(23040, 2, SEQ)
        mt1 = view(23552, 2, 2, SEQ)
        ff1 = view(0, FF_T, SEQ)
        ssg1 = stat[:, 0, 0:2]
        kT = view(0, MH, TALL, parts=QK)
        qT = view(4096, MH, TALL, parts=QK)
        vtok = view(8192, 4, 512)
        PT2 = view(10240, 2, 4, SEQ)
        P2 = view(12288, 16, TALL)
        hsq = view(10240, 3, TALL, parts=QK)
        ltmp = view(11776, TALL)
        hvar = view(28672, TALL, parts=16)
        hrs = view(29184, TALL, parts=16)
        htmp = view(29696, TALL, parts=16)
        rtmp = view(29696, TALL, parts=QK)
        br = view(20480, DT, TALL)
        ckv = view(24576, TALL)
        cq = view(25088, 2, TALL)
        lsq = view(26112, 3, TALL)
        cqvar = view(27648, TALL)
        cqrs = view(28160, TALL)
        ckvn = view(24576, TALL)
        cqn = view(25088, 2, TALL)
        zft = view(12288, 4, FN_C)
        g1f = view(13312, 4, 512)
        upad = view(15360, 2, 2, SEQ + CV_W - 1)
        acc = view(16512, 2, TALL)
        csq = view(17536, 2, TALL)
        mu = view(18560, TALL)
        cah = view(19072, TALL)
        cth = view(19584, TALL)
        sqx = view(12288, DT, TALL)
        m2 = view(0, DT, TALL)
        sig2 = view(10240, 2, TALL)
        br2 = view(11264, 2, TALL)
        Us = view(0, SLOTS, D)
        Vs = view(8192, SLOTS, D)
        hs = view(16384, 2, 4, D, dt=bf16, parts=96)
        qp = view(20480, DT, TALL)
        sc = view(24576, 16, NKEY)
        cand = view(26624, PH // 2, 256)
        eqp = view(27648, PH // 2, TOPK, TOPK, dt=bf16)
        hp1 = view(24576, D, dt=bf16)
        hp2 = view(25088, D, dt=bf16)
        hp3 = view(25600, D, dt=bf16)
        hres = view(26624, D)
        top = sb("top", [P, 16, TOPK])
        tix = varb[:, 0:256].bitcast(u32).rearrange("p (a b) -> p a b", b=TOPK)
        tixf = varb[:, 256:512].rearrange("p (a b) -> p a b", b=TOPK)
        best = rstd[:, 0:128].rearrange("p (a b) -> p a b", b=TOPK)
        pos = rstd[:, 128:256].bitcast(u32).rearrange("p (a b) -> p a b", b=TOPK)
        posi = rstd[:, 256:512].bitcast(u32).rearrange("p (a b) -> p a b", a=2)
        posf = view(24576, 2, PH, TOPK)
        ij = view(24832, 2, PH, TOPK)
        eid = view(25088, P)
        gat = view(25216, PH, TOPK)
        gsum = view(25344, 2, PH)
        yscr = nc.dram_tensor("yscr", (6 * P, D), f32, kind="Internal").ap()

        NA, NBANK = 6, 8
        HB, YB = 0, 4
        ps = ctx.enter_context(nc.psum_tensor("ps", [P, NBANK, 512], f32))

        def V(name, l=None):
            a, n = VEC[name] if l is None else VEC[name, l]
            return vec[:, a:a + n]

        chunks = []

        def chunk(name, src, kt, n):
            chunks.append((name, src, kt, n))

        def rows(ap):
            return ap.rearrange("(k p) n -> p k n", p=P)

        def modulation_chunks(l):
            for j in range(12):
                chunk(("mod", l, j), rows(A["w_mod_2"][l])[:, :, j * 512:(j + 1) * 512], 8, 512)

        for j in range(12):
            chunk(("ada", j), rows(A["w_ada"][0])[:, :, j * 512:(j + 1) * 512], 8, 512)
        for j in range(9):
            chunk(("in1", j), rows(A["w_in"][0])[:, :, j * 512:(j + 1) * 512], 8, 512)
        chunk("pa1", rows(A["w_proj_attn"][0]), 4, 1024)
        chunk("ps1", rows(A["w_proj_sgu"][0]), 4, 1024)
        for j in range(2):
            chunk(("out1", j), rows(A["w_out"][0])[:, :, j * 512:(j + 1) * 512], 8, 512)
        for j in range(8):
            chunk(("ffa", j), rows(A["w_ff1"][0])[:, :, j * 512:(j + 1) * 512], 8, 512)
        for j in range(8):
            chunk(("ffb", j), rows(A["w_ff2"][0])[:, :, j * P:(j + 1) * P], 32, P)
        for l in range(LAYERS):
            if l == 0:
                modulation_chunks(l)
            win = rows(A["w_in_2"][l])
            chunk(("inA", l), win[:, :, 0:COL_ZF], 8, COL_ZF)
            chunk(("inB", l), win[:, :, COL_ZF:COL_ZC], 8, FN_C)
            chunk(("inC", l), win[:, :, COL_ZC:COL_ZG], 8, 512)
            chunk(("ukv", l), rows(A["w_ukv_2"][l]), 1, MH * P)
            chunk(("uq", l), rows(A["w_uq_2"][l]), 2, MH * QK)
            if l + 1 < LAYERS:
                modulation_chunks(l + 1)
            for j in range(2):
                for b, (wb, kt) in enumerate([("wb_attn_2", 4), ("wb_fnet_2", 2), ("wb_conv_2", 2)]):
                    at = COL_ZG + b * D + j * 512
                    chunk(("zg", l, j, b), win[:, :, at:at + 512], 8, 512)
                    chunk(("wb", l, j, b), rows(A[wb][l])[:, :, j * 512:(j + 1) * 512], kt, 512)
            for j in range(2):
                chunk(("out2", l, j), rows(A["w_out_2"][l])[:, :, j * 512:(j + 1) * 512], 8, 512)
            for j in range(2):
                chunk(("wq", l, j), rows(A["w_query_2"][l])[:, :, j * 512:(j + 1) * 512], 8, 512)
            chunk(("keys", l), A["keys"][l], PH, NKEY)
        chunk_at = {c[0]: i for i, c in enumerate(chunks)}

        def ytok(l):
            return W[:, chunk_at["keys", l] % RING, D:2 * D]

        def ring_slot(i):
            _, _, kt, n = chunks[i]
            return W[:, i % RING, 0:kt * n].rearrange("p (k n) -> p k n", n=n)

        QC = [0, SEQ]
        TILES = [(l, t) for l in range(LAYERS) for t in range(QC[l] // P, TALL // P)]

        def streams(l):
            return range(QC[l] // SEQ, 2)

        ATT = [("a1", None, 0, SEQ)] + [(f"a2{l}{s}", l, s * SEQ, (s + 1) * SEQ) for l in range(LAYERS) for s in streams(l)]

        ahead = {"projected": [0, 1, 2]}
        for n, i in enumerate((5, 10, 15)):
            ahead["norm", i] = [3 + n]
        for n, i in enumerate((5, 10, 15)):
            for s in range(2):
                ahead[f"a20{s}", i] = [6 + 3 * s + n]

        group = {}

        block = ctx.enter_context(nc.Block())

        @block.tensor
        def _(pe):
            mm = pe.matmul

            turns = [0, 0]
            fulls = [0]
            newest = [None]
            uses = [0] * NBANK

            def bank(name, routing=False):
                b = NA + turns[1] % 2 if routing else turns[0] % NA
                turns[routing] += 1
                group[name] = [None, b]
                newest[0] = name
                if uses[b]:
                    pe.wait_ge(sem(f"bank_free{b}"), uses[b])
                uses[b] += 1
                return ps[:, b, :]

            def full(last, name=None):
                group[name or newest[0]][0] = fulls[0]
                fulls[0] += 1
                last.then_inc(sem("psum_full"), 1)

            def weights(name):
                i = chunk_at[name]
                pe.wait_ge(sem(f"w_arrived{i % RING}"), 16 * (i // RING + 1))
                return ring_slot(i)

            def done_with_weights():
                pe.drain().then_inc(sem("w_used"), 1)

            def acc_mm(o, lhs, rhs):
                n = len(lhs)
                for k in range(n):
                    last = mm(o, lhs[k], rhs[k], start=(k == 0), stop=(k == n - 1))
                return last

            def features(name, w, col, src, kt, c0, c1, m=P):
                o = bank(name)
                full(acc_mm(o[0:m, 0:c1 - c0], [w[:, k, col:col + m] for k in range(kt)],
                            [src[:, k, c0:c1] for k in range(kt)]))

            turned = [0]

            def turn(name, n, j):
                turned[0] += 1
                pe.wait_ge(sem("rows_copied"), turned[0])
                o = ps[:, group[name][1], :]
                for t in range(4):
                    last = pe.transpose(o[:, (4 * j + t) * n:(4 * j + t + 1) * n], yev[0:n, (j % 2) * 512 + t * P:(j % 2) * 512 + (t + 1) * P], ident[0:n, 0:n])
                if j < 11:
                    last.then_inc(sem("rows_turned"), 1)
                else:
                    full(last, name)

            def modulation(name, parts, lhs, n, these=range(12)):
                for j in these:
                    if j == 0:
                        bank(name, True)
                    w = weights((*parts, j))
                    o = bank((name, "rows", j))
                    full(acc_mm(o[0:n, :], lhs, [w[:, k, :] for k in range(8)]))
                    done_with_weights()
                    if j:
                        turn(name, n, j - 1)
                    if j == 11:
                        turn(name, n, 11)

            def modulation2(l, these=range(12)):
                modulation(("mod2", l), ("mod", l), [cond2[:, k, :] for k in range(8)], 2, these)

            def square_sums(name, sq, kt, c0, c1, m=P, sem_name="squares_ready", count=None):
                pe.wait_ge(sem(sem_name), count)
                o = bank(name)
                full(acc_mm(o[0:m, 0:c1 - c0], [ones[0:m, 0:m]] * kt, [sq[0:m, k, c0:c1] for k in range(kt)]))

            def attention(tag, q, k, v, pt, prob, qcols, nk, scores_of):
                ktiles = nk // P
                for i in range(16 + 5):
                    if i < 16:
                        h, t = i // 2, i % 2
                        lhs, rhs = scores_of(h, t)
                        o = bank((tag, "s", i))
                        full(mm(o[:, 0:nk], lhs, rhs, start=True, stop=True))
                    if 0 <= i - 3 < 16:
                        pe.wait_ge(sem(f"{tag}_probs"), i - 2)
                        o = bank((tag, "t", i - 3))
                        for kt in range(ktiles):
                            last = pe.transpose(o[:, kt * P:(kt + 1) * P], prob[:, i - 3, kt * P:(kt + 1) * P], ident[:, :])
                        full(last)
                    if 0 <= i - 5 < 16 and (i - 5) % 2:
                        h = (i - 5) // 2
                        pe.wait_ge(sem(f"{tag}_probsT"), 2 * h + 2)
                        o = bank((tag, "o", h))
                        full(acc_mm(o[:, 0:SEQ], [v(kt)[:, (h // 2) * P:(h // 2 + 1) * P] for kt in range(ktiles)],
                                    [pt[:, h % 2, kt, :] for kt in range(ktiles)]))
                    modulation2(1, ahead.get((tag, i), ()))

            pe.wait_ge(sem("ones_set"), 1)
            pe.wait_ge(sem("cond_ready"), 1)
            pe.wait_ge(sem("ident_set"), 16)
            modulation("mod1", ("ada",), [cond[:, 0, k:k + 1] for k in range(8)], 1)
            square_sums("ss_n1", sq1, DT, 0, SEQ, count=1)
            pe.wait_ge(sem("h_ready"), 1)
            X0 = SEQ
            for j in range(9):
                w = weights(("in1", j))
                for t in range(4):
                    if j in (2, 4):
                        if t < 2:
                            o = bank(("in1", j, t))
                            full(acc_mm(o, [H[:, k, X0 + t * P:X0 + (t + 1) * P] for k in range(8)], [w[:, k, :] for k in range(8)]))
                    else:
                        features(("in1", j, t), w, t * P, H, 8, X0, TALL)
                done_with_weights()

            def scores1(h, t):
                r = slice((h % 2) * HD1, (h % 2) * HD1 + HD1)
                return q1[r, h // 2, t * P:(t + 1) * P], k1[r, h // 2, :]

            pe.wait_ge(sem("qkv1_ready"), 10)
            attention("a1", q1, k1, lambda kt: v1[:, kt, :], PT1, P1, 0, SEQ, scores1)
            pe.wait_ge(sem("sgu_ready"), 2)
            for p in range(4):
                o = bank(("sg", p))
                for c in range(2):
                    last = mm(o[:, c * SEQ:(c + 1) * SEQ], vs1[:, c, p * P:(p + 1) * P], wsg1[:, 2 * p:2 * p + 2, :], start=True, stop=True)
                full(last)
            pe.wait_ge(sem("mix1_ready"), 12)
            wa, ws = weights("pa1"), weights("ps1")
            for n in range(DT):
                o = bank(("mg1", n))
                acc_mm(o[:, 0:SEQ], [wa[:, k, n * P:(n + 1) * P] for k in range(4)], [att1[:, k, :] for k in range(4)])
                full(acc_mm(o[:, SEQ:], [ws[:, k, n * P:(n + 1) * P] for k in range(4)], [ysg1[:, k, :] for k in range(4)]))
            done_with_weights()
            done_with_weights()
            pe.wait_ge(sem("merged1"), DT)
            for j in range(2):
                w = weights(("out1", j))
                for t in range(4):
                    features(("out1", 4 * j + t), w, t * P, mrg1, 8, 0, SEQ)
                done_with_weights()
            square_sums("ss_n2", sq1, DT, 0, SEQ, count=2)
            pe.wait_ge(sem("h_ready"), 2)
            for j in range(8):
                w = weights(("ffa", j))
                for t in range(4):
                    features(("ffa", 4 * j + t), w, t * P, H, 8, X0, TALL)
                done_with_weights()
            pe.wait_ge(sem("ff_ready"), FF_T)
            for n in range(DT):
                w = weights(("ffb", n))
                features(("ffb", n), w, 0, ff1, FF_T, 0, SEQ)
                done_with_weights()
            square_sums("ss_n3", sq1, DT, 0, SEQ, count=3)

            pe.wait_ge(sem("const_loaded"), 16 * 6)
            pe.wait_ge(sem("sel_ready"), 1)
            nsq = 3
            tile_no = 0
            for l in range(LAYERS):
                c0 = QC[l]
                if l == 0:
                    modulation2(l)
                nsq += 1
                square_sums(("ss_n1", l), sqx, DT, 0, TALL, count=nsq)
                pe.wait_ge(sem("h_ready"), 3 + 2 * l)
                w = weights(("inA", l))
                features(("ckv", l), w, 0, H, 8, 0, TALL)
                features(("kr", l), w, NOPE, H, 8, 0, TALL, m=QK)
                for t in range(2):
                    features(("cq", l, t), w, KV_IN + t * P, H, 8, c0, TALL)
                done_with_weights()
                w = weights(("inB", l))
                for t in range(c0 // P, 4):
                    o = bank(("zf", l, t))
                    full(acc_mm(o[:, 0:FN_C], [H[:, k, t * P:(t + 1) * P] for k in range(8)], [w[:, k, :] for k in range(8)]))
                done_with_weights()
                w = weights(("inC", l))
                for t in (0, 2, 1, 3):
                    features(("zc", l, t), w, t * P, H, 8, c0, TALL)
                done_with_weights()
                square_sums(("ss_ckv", l), lsq, 1, 0, TALL, sem_name="lat_squares", count=2 * l + 1)
                pe.wait_ge(sem("lat_squares"), 2 * l + 2)
                o = bank(("ss_cq", l))
                full(acc_mm(o[:, 0:TALL - c0], [ones[:, :]] * 2, [lsq[:, 1 + k, c0:TALL] for k in range(2)]))
                pe.wait_ge(sem("zf_ready"), 4 if l == 0 else 6)
                for s in streams(l):
                    for c in range(2):
                        o = bank(("dt", l, s, c))
                        full(acc_mm(o, [zft[:, 2 * s + t, c * P:(c + 1) * P] for t in range(2)], [dft[:, t, :] for t in range(2)]))
                for s in streams(l):
                    pe.wait_ge(sem("dft_ready"), 2 * (s + 1) if l == 0 else 6)
                    o = bank(("dc", l, s))
                    for c in range(2):
                        last = acc_mm(o[:, c * SEQ:(c + 1) * SEQ], [dftc[:, 0, :], dftc[:, 1, :]],
                                      [g1f[:, 2 * s + c, 0:SEQ], g1f[:, 2 * s + c, SEQ:512]])
                    full(last)
                wkv = weights(("ukv", l))
                pe.wait_ge(sem("ckvn_ready"), l + 1)
                vcols = wkv[:, 0, :].rearrange("p (h c) -> p h c", c=P)[:, :, NOPE:P]
                for t in range(4):
                    o = bank(("v", l, t))
                    full(mm(o, ckvn[:, t * P:(t + 1) * P], vcols, start=True, stop=True))
                sums = bank(("hsum", l), True)
                for i in range(16 + 1):
                    if i < 16:
                        h = i % 8
                        if i < 8:
                            o = bank(("hp", l, i))
                            full(mm(o[0:NOPE, :], wkv[:, 0, h * P:h * P + NOPE], ckvn[:, :], start=True, stop=True))
                        else:
                            if i == 8:
                                wuq = weights(("uq", l))
                                pe.wait_ge(sem("cqn_ready"), l + 1)
                            features(("hp", l, i), wuq, h * QK, cqn, 2, c0, TALL, m=QK)
                        if i in (7, 15):
                            done_with_weights()
                    if i >= 1:
                        k = i - 1
                        a = 0 if k < 8 else c0
                        pe.wait_ge(sem("head_squares"), 16 * l + i)
                        last = mm(sums[0:16, a:TALL], onecol[0:QK, 15 - k:31 - k], hsq[:, k % 3, a:TALL], start=(k == 0), stop=(k == 15))
                        if k < 15:
                            last.then_inc(sem("squares_summed"), 1)
                full(last, ("hsum", l))
                if l == 0:
                    modulation2(1, ahead["projected"])

                def spread_root(k):
                    a = 0 if k < 8 else c0
                    o = bank(("hb", l, k))
                    full(mm(o[0:QK, 0:TALL - a], ident[0:16, k:k + 1].to_broadcast([16, QK]), hrs[:, a:TALL], start=True, stop=True))

                pe.wait_ge(sem("conv_ready"), l + 1)
                o = bank(("cmean", l))
                full(acc_mm(o[:, 0:TALL - c0], [ones[:, :]] * 2, [acc[:, c, c0:TALL] for c in range(2)]))
                pe.wait_ge(sem("head_roots"), l + 1)
                for k in range(2):
                    spread_root(k)
                pe.wait_ge(sem("conv_squares"), l + 1)
                o = bank(("cvar", l))
                full(acc_mm(o[:, 0:TALL - c0], [ones[:, :]] * 2, [csq[:, c, c0:TALL] for c in range(2)]))
                for i in range(2, 16 + 4):
                    if i < 16:
                        spread_root(i)
                    if i >= 4 and i % 2 == 0:
                        pair = (i - 4) // 2
                        pe.wait_ge(sem("head_normed"), 16 * l + 2 * pair + 2)
                        o = bank(("hr", l, pair))
                        src = kT if pair < 4 else qT
                        for e in range(2):
                            last = mm(o[0:QK, e * SEQ:(e + 1) * SEQ], rotm[:, :], src[:, (2 * pair + e) % 8, SEQ:TALL], start=True, stop=True)
                        full(last)
                    if l == 0:
                        modulation2(1, ahead.get(("norm", i), ()))
                pe.wait_ge(sem("heads_ready"), 8 * (l + 1))
                for tag, al, q0, nk in ATT:
                    if al != l:
                        continue

                    def scores2(h, t):
                        return qT[:, h, q0 + t * P:q0 + (t + 1) * P], kT[:, h, 0:nk]

                    attention(tag, qT, kT, lambda kt: vtok[:, kt, :], PT2, P2, q0, nk, scores2)
                pe.wait_ge(sem("conv_done"), l + 1)
                pe.wait_ge(sem("att_ready"), 8 * (len([a for a in ATT if a[1] is not None and a[1] <= l])))
                for j in range(2):
                    for b, (k0, kt) in enumerate([(0, 4), (4, 2), (6, 2)]):
                        wz = weights(("zg", l, j, b))
                        for t in range(4):
                            features(("zg", l, j, b, t), wz, t * P, H, 8, c0, TALL)
                        done_with_weights()
                        wb = weights(("wb", l, j, b))
                        for t in range(4):
                            o = bank(("br", l, j, b, t))
                            full(acc_mm(o[:, 0:TALL - c0], [wb[:, k, t * P:(t + 1) * P] for k in range(kt)],
                                        [br[:, k0 + k, c0:TALL] for k in range(kt)]))
                        done_with_weights()
                pe.wait_ge(sem("merged2"), DT * (l + 1))
                for j in range(2):
                    w = weights(("out2", l, j))
                    for t in range(4):
                        features(("out2", l, 4 * j + t), w, t * P, m2, 8, c0, TALL)
                    done_with_weights()
                nsq += 1
                square_sums(("ss_n2", l), sqx, DT, c0, TALL, count=nsq)
                pe.wait_ge(sem("h_ready"), 4 + 2 * l)
                mine = [t for ll, t in TILES if ll == l]

                def hidden(n, tt):
                    for a in range(2):
                        o = bank(("ht", n, a), True)
                        for k in range(4):
                            last = pe.transpose(o[:, k * P:(k + 1) * P], H[:, 4 * a + k, tt * P:(tt + 1) * P], ident[:, :])
                        full(last)

                def scores(n, tt, a):
                    for p in range(2):
                        o = bank(("sc", n, a, p), True)
                        for hh in range(4):
                            h = 4 * a + hh
                            last = mm(o[:, hh * P:(hh + 1) * P], qp[64 * p:64 * p + 64, h, tt * P:(tt + 1) * P],
                                      keys[64 * p:64 * p + 64, h, :], start=True, stop=True)
                        full(last)

                def routes(n):
                    pe.wait_ge(sem("routed"), n + 1)
                    o = bank(("ij", n), True)
                    pe.transpose(o[:, 0:P], eid, ident[:, :])
                    full(pe.transpose(o[:, P:2 * P], gat.rearrange("p a b -> p (a b)"), ident[:, :]))

                def outputs_back(n):
                    pe.wait_ge(sem("y_back"), 16 * (n + 1))
                    for a in range(2):
                        o = bank(("yt", n, a), True)
                        for k in range(4):
                            last = pe.transpose(o[:, k * P:(k + 1) * P], ytok(l)[:, (4 * a + k) * P:(4 * a + k + 1) * P], ident[:, :])
                        full(last)

                def spread(n, g, it, j):
                    pe.wait_ge(sem("dots"), it * SLOTS + (n * P + g * GROUP + SLOTS + j - 1))
                    one = selb[:, bass.ds(it * SLOTS + j, 1)]
                    for hf in range(2):
                        last = mm(ps[:, HB + 2 * (j % 2) + hf, :], one.to_broadcast([96, P]),
                                  hs[:, n % 2, g, hf * 512:(hf + 1) * 512], start=True, stop=True)
                    last.then_inc(sem("spread"), 1)

                def outputs(n, g, it, c):
                    t0 = n * P + g * GROUP
                    pe.wait_ge(sem("acts"), it * 2 + (t0 // QUAD + c + 1))
                    if c == 0:
                        pe.wait_ge(sem("y_copied"), it + (t0 // SLOTS + 1))
                    for j in range(QUAD * c, QUAD * (c + 1)):
                        pe.wait_ge(sem(f"v_arrived{j}"), it * 16 + 16 * (t0 // SLOTS + 1))
                        for hf in range(2):
                            last = mm(ps[0:SLOTS, YB + hf, :], acts[:, j, :], Vs[:, j, hf * 512:(hf + 1) * 512],
                                      start=(j == 0), stop=(j == SLOTS - 1))
                        last.then_inc(sem("outputs"), 1)

                def eight(n, g, it, last_one):
                    for j in range(QUAD, SLOTS):
                        spread(n, g, it, j)
                    outputs(n, g, it, 0)
                    if not last_one:
                        for j in range(SLOTS, SLOTS + QUAD):
                            spread(n, g, it, j)
                    outputs(n, g, it, 1)

                hidden(tile_no, mine[0])
                for j in range(2):
                    w = weights(("wq", l, j))
                    for t in range(4):
                        features(("wq", l, 4 * j + t), w, t * P, H, 8, c0, TALL)
                        if (j, t) == (1, 1):
                            keys = weights(("keys", l))
                            pe.wait_ge(sem("query_ready"), DT * l + 4)
                            scores(tile_no, mine[0], 0)
                    done_with_weights()
                pe.wait_ge(sem("query_ready"), DT * (l + 1))
                scores(tile_no, mine[0], 1)
                routes(tile_no)
                for b in range(NA):
                    pe.wait_ge(sem(f"bank_free{b}"), uses[b])
                if l == 0:
                    pe.sem_inc(sem("outputs"), SLOTS)
                for tt in mine:
                    n = tile_no
                    tile_no += 1
                    pe.wait_ge(sem("hs_ready"), n + 1)
                    for g in range(P // GROUP):
                        if tt != mine[-1] and g == 0:
                            hidden(n + 1, tt + 1)
                        for j in range(QUAD):
                            spread(n, g, 0, j)
                        with pe.Fori(0, GROUP // SLOTS - 1) as it:
                            eight(n, g, it, False)
                        eight(n, g, GROUP // SLOTS - 1, True)
                        if tt != mine[-1] and g < 2:
                            scores(n + 1, tt + 1, g)
                        if tt != mine[0] and g == 2:
                            outputs_back(n - 1)
                    if tt != mine[-1]:
                        routes(n + 1)
                outputs_back(n)
                done_with_weights()
                pe.wait_ge(sem("dots"), (n + 1) * P + SLOTS)
                pe.wait_ge(sem("y_copied"), (n + 1) * P // SLOTS + 1)

        def full_bank(eng, name):
            g, b = group[name]
            eng.wait_ge(sem("psum_full"), g + 1)
            return ps[:, b, :]

        def free(name):
            return sem(f"bank_free{group[name][1]}")

        @block.sync
        def _(sp):
            sp.dma_start(vec[:, :], A["vec"]).then_inc(sem("vec_loaded"), 16)
            sp.dma_start(ident[:, :], A["ident"]).then_inc(sem("ident_set"), 16)
            sp.dma_start(X[:, :, SEQ:], A["xT"]).then_inc(sem("x_loaded"), 16)

            def weight(i):
                if i >= RING:
                    sp.wait_ge(sem("w_used"), i - RING + 1)
                sp.dma_start(ring_slot(i), chunks[i][1]).then_inc(sem(f"w_arrived{i % RING}"), 16)

            for i in range(RING):
                weight(i)
            sp.dma_start(X[:, :, 0:SEQ], A["ctxT"]).then_inc(sem("ctx_loaded"), 16)
            sp.dma_start(mask1, A["mask"]).then_inc(sem("mask_loaded"), 16)
            sp.dma_start(wsg1, A["wsgT"]).then_inc(sem("wsg_loaded"), 16)
            for p in range(4):
                for a in range(2):
                    sp.dma_start(bsg1[64 * a:64 * a + 64, p, :], A["b_sgu"][0, 2 * p + a:2 * p + a + 1, :].to_broadcast([64, P])).then_inc(sem("bsg_loaded"), 16)
            sp.dma_start(dft[:, :, :], A["dft"]).then_inc(sem("const_loaded"), 16)
            sp.dma_start(dftc[:, :, :], A["dftc"]).then_inc(sem("const_loaded"), 16)
            sp.dma_start(ropet[:, :, :], A["rope"]).then_inc(sem("const_loaded"), 16)
            sp.dma_start(rotm[:, :], A["rotm"]).then_inc(sem("const_loaded"), 16)
            sp.dma_start(gqk[:, :], A["gqk"]).then_inc(sem("const_loaded"), 16)
            sp.dma_start(iota16[:, :], A["iota16"]).then_inc(sem("const_loaded"), 16)
            for i in range(RING, len(chunks)):
                weight(i)
            sp.wait_ge(sem("x_final"), 2)
            sp.dma_start(out, X[:, :, SEQ:]).then_inc(sem("stored"), 16)
            sp.wait_ge(sem("stored"), 16)

        @block.vector
        def _(dve):
            chain = [0]

            def link(ins):
                chain[0] += 1
                ins.then_inc(sem("dve_chain"), 1)
                dve.wait_ge(sem("dve_chain"), chain[0])

            root_no = [0]

            def mean_square(name, v, n, m=P, width=TALL):
                p = full_bank(dve, name)
                link(dve.tensor_scalar(out=v, in0=p[0:m, 0:width], scalar1=1.0 / n, scalar2=EPS, op0=MUL, op1=ADD))
                dve.sem_inc(free(name), 1)
                dve.sem_inc(sem("var_ready"), 1)

            def rsqrt(v, r, tmp):
                root_no[0] += 1
                dve.wait_ge(sem("root_ready"), root_no[0])
                link(dve.reciprocal(r, r))
                link(dve.scalar_tensor_tensor(out=tmp, in0=r, scalar=-0.5, in1=r, op0=MUL, op1=MUL))
                link(dve.tensor_tensor(out=tmp, in0=tmp, in1=v, op=MUL))
                link(dve.scalar_tensor_tensor(out=r, in0=tmp, scalar=1.5, in1=r, op0=ADD, op1=MUL))

            def gate_norm(dst, gvec, scale, s):
                dve.scalar_tensor_tensor(out=dst, in0=scale, scalar=1.0, in1=gvec, op0=ADD, op1=MUL)

            def h_from(name, c0, c1):
                mean_square(name, varb[:, c0:c1], D, width=c1 - c0)
                rsqrt(varb[:, c0:c1], rstd[:, c0:c1], H[:, 0, c0:c1])
                dve.tensor_tensor(out=H[:, :, c0:c1], in0=X[:, :, c0:c1],
                                  in1=rstd[:, c0:c1].unsqueeze(1).to_broadcast([P, DT, c1 - c0]), op=MUL).then_inc(sem("xn_ready"), 1)

            def attention(tag, prob, nk, scale, mask):
                for i in range(16 + 1):
                    if i < 16:
                        p = full_bank(dve, (tag, "s", i))
                        if mask is not None:
                            link(dve.tensor_tensor(out=p[:, 0:nk], in0=p[:, 0:nk], in1=mask[:, i % 2, :], op=ADD))
                        link(dve.tensor_reduce(out=stat[:, 0, i:i + 1], in_=p[:, 0:nk], axis=AX.X, op=ALU.max))
                        dve.tensor_scalar(out=stat[:, 1, i:i + 1], in0=stat[:, 0, i:i + 1], scalar1=-scale, scalar2=None, op0=MUL).then_inc(sem(f"{tag}_max"), 1)
                    if i >= 1:
                        dve.wait_ge(sem(f"{tag}_exp"), i)
                        link(dve.reciprocal(stat[:, 3, i - 1:i], stat[:, 2, i - 1:i]))
                        dve.tensor_scalar(out=prob[:, i - 1, 0:nk], in0=prob[:, i - 1, 0:nk], scalar1=stat[:, 3, i - 1:i], scalar2=None, op0=MUL).then_inc(sem(f"{tag}_probs"), 1)

            dve.memset(ones[:, :], 1.0).then_inc(sem("ones_set"), 1)
            dve.memset(acts[:, :, :], 0.0)
            link(dve.memset(onecol[:, :], 0.0))
            dve.memset(onecol[:, 15:16], 1.0)
            dve.wait_ge(sem("ident_set"), 16)
            for i in range(3):
                last = dve.tensor_copy(selb[32 * i:32 * i + 32, :], ident[0:32, 0:32])
            last.then_inc(sem("sel_ready"), 1)
            dve.wait_ge(sem("vec_loaded"), 16)
            for i, name in enumerate(("c", "c_ctx_2", "c_2")):
                last = dve.tensor_scalar(out=cond[:, i, :], in0=V(name), scalar1=0.5, scalar2=None, op0=MUL)
            link(last)
            dve.sem_inc(sem("cond_half"), 1)
            dve.wait_ge(sem("cond_tanh"), 1)
            ct = condt[:, :].rearrange("p (a b) -> p a b", a=3)
            link(dve.scalar_tensor_tensor(out=cond[:, :, :], in0=ct, scalar=1.0, in1=cond[:, :, :], op0=ADD, op1=MUL))
            link(dve.tensor_copy(cond2[:, :, :], cond[:, 1:3, :].rearrange("p a k -> p k a")))
            dve.sem_inc(sem("cond_ready"), 1)
            def modulations1():
                p = full_bank(dve, "mod1")
                link(dve.tensor_tensor(out=mod1[:, :], in0=p[:, 0:48], in1=V("b_ada"), op=ADD))
                dve.sem_inc(free("mod1"), 1)
                gate_norm(gs[:, 0, :, 0], V("g_mix"), mod1[:, 8:16], 0)
                gate_norm(gs[:, 1, :, 0], V("g_ffn"), mod1[:, 32:40], 0)
                link(dve.tensor_scalar(out=half[:, :, 0], in0=mod1[:, 16:24], scalar1=0.5, scalar2=None, op0=MUL))
                dve.sem_inc(sem("mod_ready"), 1)

            modulations1()
            h_from("ss_n1", SEQ, TALL)
            dve.wait_ge(sem("vs_squares"), 1)
            link(dve.tensor_scalar(out=stat[:, 1, 0:2], in0=ssg1, scalar1=1.0 / SGU_W, scalar2=EPS, op0=MUL, op1=ADD))
            dve.sem_inc(sem("var_ready"), 1)
            rsqrt(stat[:, 1, 0:2], stat[:, 2, 0:2], stat[:, 3, 0:2])
            for c in range(2):
                last = dve.tensor_scalar(out=vs1[:, c, :], in0=vs1[:, c, :], scalar1=stat[:, 2, c:c + 1], scalar2=None, op0=MUL)
            link(last)
            dve.sem_inc(sem("sgu_ready"), 1)
            dve.wait_ge(sem("mask_loaded"), 16)
            attention("a1", P1, SEQ, 1.0, mask1)
            dve.wait_ge(sem("bsg_loaded"), 128)
            for p4 in range(4):
                p = full_bank(dve, ("sg", p4))
                for c in range(2):
                    for a in range(2):
                        rr = slice(64 * a, 64 * a + 64)
                        last = dve.scalar_tensor_tensor(out=ysg1[rr, p4, c * P:(c + 1) * P], in0=p[rr, c * SEQ + a * P:c * SEQ + (a + 1) * P],
                                                        scalar=V("g_sgu")[rr, p4:p4 + 1], in1=bsg1[rr, p4, :], op0=MUL, op1=ADD)
                link(last)
                dve.sem_inc(free(("sg", p4)), 1)
                dve.tensor_tensor(out=ysg1[:, p4, :], in0=ysg1[:, p4, :], in1=u1[:, p4, :], op=MUL).then_inc(sem("mix1_ready"), 1)
            dve.wait_ge(sem("gates1"), 16)
            for t in range(DT):
                p = full_bank(dve, ("mg1", t))
                link(dve.scalar_tensor_tensor(out=mt1[:, t % 2, :, :], in0=gate1[:, t, :, :], scalar=1.0,
                                              in1=p.rearrange("p (a b) -> p a b", a=2), op0=ADD, op1=MUL))
                dve.sem_inc(free(("mg1", t)), 1)
                dve.tensor_tensor(out=mrg1[:, t, :], in0=mt1[:, t % 2, 0, :], in1=mt1[:, t % 2, 1, :], op=ADD).then_inc(sem("merged1"), 1)

            def residual(name_of, gate, c0, c1, tiles=DT):
                for t in range(tiles):
                    p = full_bank(dve, name_of(t))
                    last = dve.scalar_tensor_tensor(out=X[:, t, c0:c1], in0=p[:, 0:c1 - c0], scalar=gate(t), in1=X[:, t, c0:c1], op0=MUL, op1=ADD)
                    last.then_inc(free(name_of(t)), 1)
                return last

            residual(lambda t: ("out1", t), lambda t: half[:, t, 0:1], SEQ, TALL)
            link(dve.memset(stat[:, 3, 0:1], 0.0))
            dve.sem_inc(sem("x_ready"), 1)
            h_from("ss_n2", SEQ, TALL)
            residual(lambda t: ("ffb", t), lambda t: mod1[:, 40 + t:41 + t], SEQ, TALL)
            link(dve.memset(stat[:, 3, 0:1], 0.0))
            dve.sem_inc(sem("x_ready"), 1)
            mean_square("ss_n3", varb[:, SEQ:], D, width=SEQ)
            rsqrt(varb[:, SEQ:], rstd[:, SEQ:], H[:, 0, SEQ:])
            link(dve.tensor_tensor(out=X[:, :, SEQ:], in0=X[:, :, SEQ:], in1=rstd[:, SEQ:].unsqueeze(1).to_broadcast([P, DT, SEQ]), op=MUL))
            link(dve.tensor_tensor(out=X[:, :, SEQ:], in0=X[:, :, SEQ:], in1=V("g_final").unsqueeze(2).to_broadcast([P, DT, SEQ]), op=MUL))
            dve.sem_inc(sem("x_ready"), 1)
            def modulations2(l):
                p = full_bank(dve, ("mod2", l))
                link(dve.tensor_tensor(out=mod2[:, l, :, :], in0=p[:, 0:96].rearrange("p (a b) -> p a b", b=2),
                                       in1=V("b_mod", l).unsqueeze(2).to_broadcast([P, 48, 2]), op=ADD))
                dve.sem_inc(free(("mod2", l)), 1)

            tile_no = 0
            dve.wait_ge(sem("const_loaded"), 16 * 6)
            for l in range(LAYERS):
                c0 = QC[l]
                wq = TALL - c0
                if l == 0:
                    modulations2(l)
                for s in range(2):
                    gate_norm(gs[:, 0, :, s], V("g_norm1", l), mod2[:, l, 8:16, s], s)
                    gate_norm(gs[:, 1, :, s], V("g_norm2", l), mod2[:, l, 32:40, s], s)
                dve.tensor_scalar(out=lnh[:, 0:2], in0=V("g_cln", l), scalar1=0.5, scalar2=None, op0=MUL)
                dve.tensor_scalar(out=lnh[:, 2:4], in0=V("b_cln", l), scalar1=0.5, scalar2=None, op0=MUL)
                link(dve.tensor_scalar(out=half[:, :, :], in0=mod2[:, l, 16:24, :], scalar1=0.5, scalar2=None, op0=MUL))
                dve.sem_inc(sem("mod_ready"), 1)
                h_from(("ss_n1", l), 0, TALL)
                dve.wait_ge(sem("pad_clear"), l + 1)
                for c in range(2):
                    dve.wait_ge(sem("glu_parts"), 2 * l + c + 1)
                    s0 = c0 // SEQ
                    src = cth[:, c0:TALL].rearrange("p (s t) -> p s t", t=SEQ)
                    oth = cah[:, c0:TALL].rearrange("p (s t) -> p s t", t=SEQ)
                    link(dve.scalar_tensor_tensor(out=upad[:, c, s0:2, CV_W // 2:CV_W // 2 + SEQ], in0=src, scalar=1.0, in1=oth, op0=ADD, op1=MUL))
                    dve.sem_inc(sem("glu_done"), 1)
                mean_square(("ss_ckv", l), varb[:, :], P)
                mean_square(("ss_cq", l), cqvar[:, c0:], Q_LORA, width=wq)
                rsqrt(varb[:, :], rstd[:, :], ltmp)
                link(dve.scalar_tensor_tensor(out=ckvn, in0=ckv, scalar=V("g_ckv", l), in1=rstd[:, :], op0=MUL, op1=MUL))
                dve.sem_inc(sem("ckvn_ready"), 1)
                rsqrt(cqvar[:, c0:], cqrs[:, c0:], ltmp[:, c0:])
                for t in range(2):
                    last = dve.scalar_tensor_tensor(out=cqn[:, t, c0:], in0=cq[:, t, c0:], scalar=V("g_cq", l)[:, t:t + 1], in1=cqrs[:, c0:], op0=MUL, op1=MUL)
                link(last)
                dve.sem_inc(sem("cqn_ready"), 1)
                for w in range(CV_W):
                    for c in range(2):
                        s0 = c0 // SEQ
                        u = upad[:, c, s0:2, w:w + SEQ]
                        a = acc[:, c, c0:TALL].rearrange("p (s t) -> p s t", t=SEQ)
                        wt = V("w_dw", l)[:, c * CV_W + w:c * CV_W + w + 1]
                        if w == 0:
                            last = dve.tensor_scalar(out=a, in0=u, scalar1=wt, scalar2=V("b_dw", l)[:, c:c + 1], op0=MUL, op1=ADD)
                        else:
                            last = dve.scalar_tensor_tensor(out=a, in0=u, scalar=wt, in1=a, op0=MUL, op1=ADD)
                    link(last)
                dve.sem_inc(sem("conv_ready"), 1)

                def head(k):
                    return (kT if k < 8 else qT)[:, k % 8, :]

                def head_norm(k):
                    a = 0 if k < 8 else c0
                    p = full_bank(dve, ("hb", l, k))
                    g = gqk[:, 2 * l + (k < 8):2 * l + (k < 8) + 1]
                    link(dve.scalar_tensor_tensor(out=head(k)[:, a:], in0=head(k)[:, a:], scalar=g, in1=p[0:QK, 0:TALL - a], op0=MUL, op1=MUL))
                    dve.sem_inc(free(("hb", l, k)), 1)
                    dve.sem_inc(sem("head_normed"), 1)

                def rotate(pair):
                    p = full_bank(dve, ("hr", l, pair))[NOPE:QK, :].rearrange("p (e t) -> p e t", e=2)
                    two = [ROPE, 2, SEQ]
                    dst = (kT if pair < 4 else qT)[NOPE:QK, 2 * pair % 8:2 * pair % 8 + 2, SEQ:TALL]
                    tmp = rtmp[NOPE:QK, :].rearrange("p (e t) -> p e t", e=2)
                    dve.tensor_tensor(out=dst, in0=dst, in1=ropet[NOPE:QK, 0, SEQ:].unsqueeze(1).to_broadcast(two), op=MUL)
                    link(dve.tensor_tensor(out=tmp, in0=p, in1=ropet[NOPE:QK, 1, SEQ:].unsqueeze(1).to_broadcast(two), op=MUL))
                    dve.sem_inc(free(("hr", l, pair)), 1)
                    link(dve.tensor_tensor(out=dst, in0=dst, in1=tmp, op=ADD))
                    dve.sem_inc(sem("heads_ready"), 1)

                mean_square(("hsum", l), hvar, QK, m=16)
                p = full_bank(dve, ("cmean", l))
                link(dve.tensor_scalar(out=mu[:, c0:], in0=p[:, 0:wq], scalar1=1.0 / CV_C, scalar2=None, op0=MUL))
                dve.sem_inc(free(("cmean", l)), 1)
                link(dve.tensor_tensor(out=acc[:, :, c0:], in0=acc[:, :, c0:], in1=mu[:, c0:].unsqueeze(1).to_broadcast([P, 2, wq]), op=SUB))
                dve.sem_inc(sem("centred"), 1)
                rsqrt(hvar, hrs, htmp)
                dve.sem_inc(sem("head_roots"), 1)
                for k in range(2):
                    head_norm(k)
                mean_square(("cvar", l), varb[:, c0:], CV_C, width=wq)
                for i in range(2, 16 + 4):
                    if i < 16:
                        head_norm(i)
                    if i >= 4 and i % 2 == 0:
                        rotate((i - 4) // 2)
                    if i == 4:
                        rsqrt(varb[:, c0:], rstd[:, c0:], mu[:, c0:])
                        link(dve.tensor_tensor(out=acc[:, :, c0:], in0=acc[:, :, c0:], in1=rstd[:, c0:].unsqueeze(1).to_broadcast([P, 2, wq]), op=MUL))
                        dve.sem_inc(sem("ln_ready"), 1)
                    if i == 9:
                        dve.wait_ge(sem("ln_tanh"), l + 1)
                        link(dve.scalar_tensor_tensor(out=br[:, 6:8, c0:], in0=csq[:, :, c0:], scalar=1.0, in1=acc[:, :, c0:], op0=ADD, op1=MUL))
                        dve.sem_inc(sem("conv_done"), 1)
                for tag, al, q0, nk in ATT:
                    if al == l:
                        attention(tag, P2, nk, QK ** -0.5, None)
                if l + 1 < LAYERS:
                    modulations2(l + 1)
                i = 0
                for j in range(2):
                    for b in range(3):
                        for t in range(4):
                            f = 4 * j + t
                            dve.wait_ge(sem("gates2"), 24 * l + i + 1)
                            p = full_bank(dve, ("br", l, j, b, t))
                            dst = m2[:, f, c0:] if b == 0 else br2[:, i % 2, c0:]
                            link(dve.scalar_tensor_tensor(out=dst, in0=sig2[:, i % 2, c0:], scalar=1.0, in1=p[:, 0:wq], op0=ADD, op1=MUL))
                            dve.sem_inc(free(("br", l, j, b, t)), 1)
                            dve.sem_inc(sem("gates_used"), 1)
                            if b:
                                link(dve.tensor_tensor(out=m2[:, f, c0:], in0=m2[:, f, c0:], in1=br2[:, i % 2, c0:], op=ADD))
                            if b == 2:
                                dve.sem_inc(sem("merged2"), 1)
                            i += 1
                for t in range(DT):
                    name = ("out2", l, t)
                    p = full_bank(dve, name)
                    for s in streams(l):
                        last = dve.scalar_tensor_tensor(out=X[:, t, s * SEQ:(s + 1) * SEQ], in0=p[:, s * SEQ - c0:(s + 1) * SEQ - c0],
                                                        scalar=half[:, t, s:s + 1], in1=X[:, t, s * SEQ:(s + 1) * SEQ], op0=MUL, op1=ADD)
                    last.then_inc(free(name), 1)
                link(dve.memset(stat[:, 3, 0:1], 0.0))
                dve.sem_inc(sem("x_ready"), 1)
                h_from(("ss_n2", l), c0, TALL)
                mine = [t for ll, t in TILES if ll == l]
                f4 = tixf.rearrange("p (h q) k -> p h q k", q=2)
                t4 = top[:, :, :].rearrange("p (h q) k -> p h q k", q=2)
                half4 = [P, PH // 2, TOPK, TOPK]

                def sixteen_best(value, index, data, these):
                    for i, d in these:
                        last = dve.max(value[:, i, 0:8], data[:, d, :])
                    link(last)
                    for i, d in these:
                        last = dve.max_index(index[:, i, 0:8], value[:, i, 0:8], data[:, d, :])
                    link(last)
                    for i, d in these:
                        last = dve.match_replace(data[:, d, :], value[:, i, 0:8], data[:, d, :], -3.0e38)
                    link(last)
                    for i, d in these:
                        last = dve.max(value[:, i, 8:16], data[:, d, :])
                    link(last)
                    for i, d in these:
                        last = dve.max_index(index[:, i, 8:16], value[:, i, 8:16], data[:, d, :])
                    link(last)

                def keys_by_rank(a):
                    for e in range(2):
                        hh = slice(4 * e, 4 * e + 4)
                        link(dve.tensor_tensor(out=eqp, in0=posf[:, a, hh, :].unsqueeze(3).to_broadcast(half4),
                                               in1=iota16[:, :].unsqueeze(1).unsqueeze(1).to_broadcast(half4), op=ALU.is_equal))
                        link(dve.tensor_tensor(out=eqp, in0=eqp, in1=f4[:, hh, a, :].unsqueeze(2).to_broadcast(half4), op=MUL))
                        link(dve.tensor_reduce(out=ij[:, a, hh, :], in_=eqp, axis=AX.X, op=ADD))

                def route(n, step):
                    if step == 0:
                        for a in range(2):
                            dve.wait_ge(sem("part1"), 2 * n + a + 1)
                            p = full_bank(dve, ("ht", n, a))
                            link(dve.tensor_tensor(out=hres[:, a * 512:(a + 1) * 512], in0=p, in1=hp1[:, a * 512:(a + 1) * 512], op=SUB))
                            dve.sem_inc(free(("ht", n, a)), 1)
                        dve.sem_inc(sem("residue"), 1)
                    elif step == 1:
                        dve.wait_ge(sem("part2"), n + 1)
                        link(dve.tensor_tensor(out=hp3, in0=hres, in1=hp2, op=SUB))
                        for i, part in enumerate((hp1, hp2, hp3)):
                            for g in range(4):
                                last = dve.tensor_copy(hs[32 * i:32 * i + 32, n % 2, g, :], part[32 * g:32 * g + 32, :])
                        link(last)
                        dve.sem_inc(sem("hs_ready"), 1)
                    elif step in (2, 4):
                        e = step // 4
                        dve.wait_ge(sem("scores_ready"), 4 * n + 2 * (e + 1))
                        sixteen_best(top, tix, sc, [(i, i) for i in range(8 * e, 8 * e + 8)])
                    elif step in (3, 5):
                        e = step // 4
                        link(dve.tensor_tensor(out=cand.rearrange("p h (i j) -> p h i j", j=TOPK),
                                               in0=t4[:, 4 * e:4 * e + 4, 0, :].unsqueeze(3).to_broadcast(half4),
                                               in1=t4[:, 4 * e:4 * e + 4, 1, :].unsqueeze(2).to_broadcast(half4), op=ADD))
                        sixteen_best(best, pos, cand, [(4 * e + i, i) for i in range(4)])
                        if e:
                            link(dve.tensor_tensor(out=gat, in0=best, in1=best[:, :, 0:1].to_broadcast([P, PH, TOPK]), op=SUB))
                            dve.sem_inc(sem("best_ready"), 1)
                            dve.tensor_copy(tixf, tix)
                            posv = pos.rearrange("p a b -> p (a b)")
                            dve.tensor_scalar(out=posi[:, 0, :], in0=posv, scalar1=4, scalar2=None, op0=ALU.logical_shift_right)
                            link(dve.tensor_scalar(out=posi[:, 1, :], in0=posv, scalar1=15, scalar2=None, op0=ALU.bitwise_and))
                            link(dve.tensor_copy(posf.rearrange("p a b c -> p (a b c)"), posi.rearrange("p a b -> p (a b)")))
                    elif step == 6:
                        keys_by_rank(0)
                    else:
                        keys_by_rank(1)
                        link(dve.scalar_tensor_tensor(out=eid, in0=ij[:, 0, :, :].rearrange("p a b -> p (a b)"), scalar=float(NKEY),
                                                      in1=ij[:, 1, :, :].rearrange("p a b -> p (a b)"), op0=MUL, op1=ADD))
                        dve.wait_ge(sem("best_exp"), n + 1)
                        link(dve.tensor_reduce(out=gsum[:, 0, :], in_=gat, axis=AX.X, op=ADD))
                        link(dve.reciprocal(gsum[:, 1, :], gsum[:, 0, :]))
                        link(dve.tensor_tensor(out=gat, in0=gat, in1=gsum[:, 1, :].unsqueeze(2).to_broadcast([P, PH, TOPK]), op=MUL))
                        dve.sem_inc(sem("routed"), 1)
                        p = full_bank(dve, ("ij", n))
                        dve.tensor_scalar(out=idxT[:, n % 2, :], in0=p[:, 0:P], scalar1=float(l * NEXP), scalar2=None, op0=ADD)
                        link(dve.tensor_copy(gateT[:, n % 2, :], p[:, P:2 * P]))
                        dve.sem_inc(free(("ij", n)), 1)
                        dve.sem_inc(sem("idx_ready"), 1)

                def add_outputs(n, tt):
                    for a in range(2):
                        p = full_bank(dve, ("yt", n, a))
                        for k in range(4):
                            f = 4 * a + k
                            last = dve.scalar_tensor_tensor(out=X[:, f, tt * P:(tt + 1) * P], in0=p[:, k * P:(k + 1) * P],
                                                            scalar=mod2[:, l, 40 + f, tt // 2:tt // 2 + 1], in1=X[:, f, tt * P:(tt + 1) * P], op0=MUL, op1=ADD)
                        link(last)
                        dve.sem_inc(free(("yt", n, a)), 1)

                def eight(n, g, it):
                    t0 = n * P + g * SEG
                    for j in range(SLOTS):
                        dve.wait_ge(sem(f"u_arrived{j}"), it * 16 + 16 * (t0 // SLOTS + 1))
                        dve.wait_ge(sem("spread"), it * SLOTS + (t0 + j + 1))
                        if j % QUAD == 0:
                            dve.wait_ge(sem("gelus"), it * 2 + (t0 // QUAD + j // QUAD + 1))
                        b = HB + 2 * (j % 2)
                        dve.scalar_tensor_tensor(out=Us[:, j, :], in0=ps[:, b:b + 2, :].rearrange("p a b -> p (a b)"), scalar=1.0,
                                                 in1=Us[:, j, :], op0=MUL, op1=MUL, accum_out=dots[:, j:j + 1]).then_inc(sem("dots"), 1)
                        if j % QUAD == QUAD - 1:
                            a = j - QUAD + 1
                            dve.wait_ge(sem("gelus"), it * 2 + (t0 // QUAD + j // QUAD + 3))
                            dve.wait_ge(sem("outputs"), it * SLOTS + (t0 + j + 1))
                            diag = acts[:, :, :].rearrange("p a b -> p (a b)")[:, a * (SLOTS + 1):(a + QUAD - 1) * (SLOTS + 1) + 1:SLOTS + 1]
                            dve.tensor_tensor(out=diag, in0=gel[:, a:a + QUAD], in1=gateT[:, n % 2, bass.ds(it * SLOTS + (g * SEG + a), QUAD)],
                                              op=MUL).then_inc(sem("acts"), 1)

                for step in range(8):
                    route(tile_no, step)
                if l == 0:
                    dve.sem_inc(sem("dots"), SLOTS)
                for tt in mine:
                    n = tile_no
                    tile_no += 1
                    for g in range(P // SEG):
                        with dve.Fori(0, SEG // SLOTS) as it:
                            eight(n, g, it)
                        if tt != mine[0] and g == 6:
                            add_outputs(n - 1, tt - 1)
                        if tt != mine[-1]:
                            route(n + 1, g)
                add_outputs(n, tt)
                dve.sem_inc(sem("x_ready"), 1)
                dve.sem_inc(sem("x_final"), 1)

        @block.scalar
        def _(act):
            link_no = [0]

            def link(ins):
                link_no[0] += 1
                ins.then_inc(sem("act_chain"), 1)
                act.wait_ge(sem("act_chain"), link_no[0])

            def A_(o, i, f=ACT.Copy, **kw):
                return act.activation(o, i, f, **kw)

            def evac(name, o, m=slice(0, P), width=None, f=ACT.Copy, **kw):
                p = full_bank(act, name)
                return A_(o, p[m, 0:width] if width else p[m, :], f, **kw)

            def squares(c0, c1, dst, xr):
                act.wait_ge(*xr)
                A_(dst[:, :, c0:c1] if dst is sqx else dst, X[:, :, c0:c1], ACT.Square).then_inc(sem("squares_ready"), 1)

            nroot = [0]

            def root(v, o):
                nroot[0] += 1
                act.wait_ge(sem("var_ready"), nroot[0])
                A_(o, v, ACT.Sqrt).then_inc(sem("root_ready"), 1)

            def modulate(which, nh, mod, shift, ss, c0, nmod):
                act.wait_ge(sem("xn_ready"), nh)
                act.wait_ge(sem("mod_ready"), nmod)
                for k in range(DT):
                    for s in ss:
                        cs = slice(max(c0, s * SEQ), (s + 1) * SEQ)
                        gi = 0 if mod is mod1 else s
                        bias = mod[:, shift + k:shift + k + 1] if mod is mod1 else mod[:, nmod - 2, shift + k, s:s + 1]
                        last = A_(H[:, k, cs], H[:, k, cs], ACT.Identity, bias=bias, scale=gs[:, which, k, gi:gi + 1])
                last.then_inc(sem("h_ready"), 1)

            def attention(tag, prob, pt, dst, nk, scale, done):
                kts = nk // P
                for i in range(16 + 5):
                    if i < 16:
                        act.wait_ge(sem(f"{tag}_max"), i + 1)
                        p = full_bank(act, (tag, "s", i))
                        link(A_(prob[:, i, 0:nk], p[:, 0:nk], ACT.Exp, bias=stat[:, 1, i:i + 1], scale=scale, accum_out=stat[:, 2, i:i + 1]))
                        act.sem_inc(free((tag, "s", i)), 1)
                        act.sem_inc(sem(f"{tag}_exp"), 1)
                    if 0 <= i - 3 < 16:
                        h, t = (i - 3) // 2, (i - 3) % 2
                        p = full_bank(act, (tag, "t", i - 3))
                        link(A_(pt[:, h % 2, 0:kts, t * P:(t + 1) * P], p[:, 0:nk].rearrange("p (k q) -> p k q", q=P)))
                        act.sem_inc(free((tag, "t", i - 3)), 1)
                        act.sem_inc(sem(f"{tag}_probsT"), 1)
                    if 0 <= i - 5 < 16 and (i - 5) % 2:
                        h = (i - 5) // 2
                        r = slice(64 * (h % 2), 64 * (h % 2) + 64)
                        link(evac((tag, "o", h), dst(h)[r], m=r, width=SEQ))
                        act.sem_inc(free((tag, "o", h)), 1)
                        act.sem_inc(sem(done), 1)
                    rows(("mod2", 1), 2, ahead.get((tag, i), ()))

            def rows(name, n, these=range(12)):
                for j in these:
                    modulations = 0 if name == "mod1" else 1 + name[1]
                    if j >= 2:
                        act.wait_ge(sem("rows_turned"), 11 * modulations + j - 1)
                    link(evac((name, "rows", j), yev[0:n, (j % 2) * 512:(j % 2 + 1) * 512], m=slice(0, n)))
                    act.sem_inc(free((name, "rows", j)), 1)
                    act.sem_inc(sem("rows_copied"), 1)

            act.wait_ge(sem("cond_half"), 1)
            A_(condt[:, :], cond[:, :, :].rearrange("p a b -> p (a b)"), ACT.Tanh).then_inc(sem("cond_tanh"), 1)
            rows("mod1", 1)
            squares(SEQ, TALL, sq1, (sem("x_loaded"), 16))
            root(varb[:, SEQ:], rstd[:, SEQ:])
            modulate(0, 1, mod1, 0, [1], SEQ, 1)
            for j in range(9):
                for t in range(4):
                    if j in (2, 4) and t >= 2:
                        continue
                    name = ("in1", j, t)
                    if j == 0:
                        ins = evac(name, q1[:, t, :], width=SEQ, scale=HD1 ** -0.5)
                    elif j == 1:
                        ins = evac(name, k1[:, t, :], width=SEQ)
                    elif j == 2:
                        ins = evac(name, v1[:, t, :])
                    elif j == 3:
                        ins = evac(name, u1[:, t, :], width=SEQ, f=ACT.Gelu_apprx_tanh)
                    elif j == 4:
                        ins = evac(name, vs1[:, t, :], f=ACT.Gelu_apprx_tanh)
                    else:
                        g = 4 * ((j - 5) % 2) + t
                        ins = evac(name, gate1[:, g, (j - 5) // 2, :], width=SEQ, f=ACT.Tanh, scale=0.5)
                    link(ins)
                    act.sem_inc(free(name), 1)
                    if j < 3:
                        act.sem_inc(sem("qkv1_ready"), 1)
                    if j == 4:
                        link(A_(vsq1[:, t, :], vs1[:, t, :], ACT.Square, accum_out=ssg1[:, t:t + 1]))
                        if t == 1:
                            act.sem_inc(sem("vs_squares"), 1)
                            root(stat[:, 1, 0:2], stat[:, 2, 0:2])
                    if j > 4:
                        act.sem_inc(sem("gates1"), 1)
            attention("a1", P1, PT1, lambda h: att1[:, h // 2, :], SEQ, 1.0, "mix1_ready")
            squares(SEQ, TALL, sq1, (sem("x_ready"), 1))
            root(varb[:, SEQ:], rstd[:, SEQ:])
            modulate(1, 2, mod1, 24, [1], SEQ, 1)
            for t in range(FF_T):
                link(evac(("ffa", t), ff1[:, t, :], width=SEQ, f=ACT.Relu))
                act.sem_inc(free(("ffa", t)), 1)
                A_(ff1[:, t, :], ff1[:, t, :], ACT.Square).then_inc(sem("ff_ready"), 1)
            squares(SEQ, TALL, sq1, (sem("x_ready"), 2))
            root(varb[:, SEQ:], rstd[:, SEQ:])
            tile_no = 0
            nh = 2
            nx = 3
            for l in range(LAYERS):
                c0 = QC[l]
                wq = TALL - c0
                if l == 0:
                    rows(("mod2", 0), 2)
                    act.wait_ge(sem("ctx_loaded"), 16)
                squares(0, TALL, sqx, (sem("x_ready"), nx))
                root(varb[:, :], rstd[:, :])
                nh += 1
                modulate(0, nh, mod2, 0, [0, 1], 0, 2 + l)
                link(evac(("ckv", l), ckv))
                A_(lsq[:, 0, :], ckv, ACT.Square).then_inc(sem("lat_squares"), 1)
                act.sem_inc(free(("ckv", l)), 1)
                p = full_bank(act, ("kr", l))
                A_(kT[NOPE:QK, :, :], p[NOPE:QK, :].unsqueeze(1).to_broadcast([ROPE, MH, TALL]))
                for i in range(3):
                    last = A_(hsq[NOPE:QK, i, :], p[NOPE:QK, :], ACT.Square)
                last.then_inc(free(("kr", l)), 1)
                for t in range(2):
                    link(evac(("cq", l, t), cq[:, t, c0:], width=wq))
                    act.sem_inc(free(("cq", l, t)), 1)
                A_(lsq[:, 1:3, c0:], cq[:, :, c0:], ACT.Square).then_inc(sem("lat_squares"), 1)
                for t in range(c0 // P, 4):
                    link(evac(("zf", l, t), zft[:, t, :], width=FN_C))
                    act.sem_inc(free(("zf", l, t)), 1)
                    act.sem_inc(sem("zf_ready"), 1)
                for c in range(2):
                    if c or l:
                        act.wait_ge(sem("glu_done"), 2 * l + c)
                    link(evac(("zc", l, c), cah[:, c0:], width=wq, scale=0.5))
                    act.sem_inc(free(("zc", l, c)), 1)
                    link(evac(("zc", l, 2 + c), cth[:, c0:], width=wq, f=ACT.Tanh, scale=0.5))
                    act.sem_inc(free(("zc", l, 2 + c)), 1)
                    act.sem_inc(sem("glu_parts"), 1)
                root(varb[:, :], rstd[:, :])
                root(cqvar[:, c0:], cqrs[:, c0:])
                for s in streams(l):
                    for c in range(2):
                        link(evac(("dt", l, s, c), g1f[:, 2 * s + c, :]))
                        act.sem_inc(free(("dt", l, s, c)), 1)
                        act.sem_inc(sem("dft_ready"), 1)
                for s in streams(l):
                    p = full_bank(act, ("dc", l, s))
                    A_(br[:, 4:6, s * SEQ:(s + 1) * SEQ], p.rearrange("p (a b) -> p a b", a=2)).then_inc(free(("dc", l, s)), 1)
                for t in range(4):
                    evac(("v", l, t), vtok[:, t, :]).then_inc(free(("v", l, t)), 1)
                for i in range(16):
                    a = 0 if i < 8 else c0
                    m = slice(0, NOPE) if i < 8 else slice(0, QK)
                    p = full_bank(act, ("hp", l, i))
                    A_((kT if i < 8 else qT)[m, i % 8, a:], p[m, 0:TALL - a])
                    if i >= 3:
                        act.wait_ge(sem("squares_summed"), 15 * l + i - 2)
                    link(A_(hsq[m, i % 3, a:], p[m, 0:TALL - a], ACT.Square))
                    act.sem_inc(free(("hp", l, i)), 1)
                    act.sem_inc(sem("head_squares"), 1)
                if l == 0:
                    rows(("mod2", 1), 2, ahead["projected"])
                root(hvar, hrs)
                act.wait_ge(sem("centred"), l + 1)
                A_(csq[:, :, c0:], acc[:, :, c0:], ACT.Square).then_inc(sem("conv_squares"), 1)
                root(varb[:, c0:], rstd[:, c0:])
                act.wait_ge(sem("ln_ready"), l + 1)
                for c in range(2):
                    last = A_(acc[:, c, c0:], acc[:, c, c0:], ACT.Identity, scale=lnh[:, c:c + 1], bias=lnh[:, 2 + c:3 + c])
                link(last)
                A_(csq[:, :, c0:], acc[:, :, c0:], ACT.Tanh).then_inc(sem("ln_tanh"), 1)
                if l == 0:
                    for i in range(2, 16 + 4):
                        rows(("mod2", 1), 2, ahead.get(("norm", i), ()))
                for tag, al, q0, nk in ATT:
                    if al == l:
                        attention(tag, P2, PT2, lambda h: br[:, h // 2, q0:q0 + SEQ], nk, QK ** -0.5, "att_ready")
                i = 0
                for j in range(2):
                    for b in range(3):
                        for t in range(4):
                            if 24 * l + i >= 2:
                                act.wait_ge(sem("gates_used"), 24 * l + i - 1)
                            link(evac(("zg", l, j, b, t), sig2[:, i % 2, c0:], width=wq, f=ACT.Tanh, scale=0.5))
                            act.sem_inc(free(("zg", l, j, b, t)), 1)
                            act.sem_inc(sem("gates2"), 1)
                            i += 1
                nx += 1
                squares(c0, TALL, sqx, (sem("x_ready"), nx))
                root(varb[:, c0:], rstd[:, c0:])
                nh += 1
                modulate(1, nh, mod2, 24, streams(l), c0, 2 + l)
                mine = [t for ll, t in TILES if ll == l]
                s4 = sc.rearrange("p (h q) k -> p h q k", q=2)

                def route(n, step):
                    if step == 0:
                        for a in range(2):
                            evac(("ht", n, a), hp1[:, a * 512:(a + 1) * 512]).then_inc(sem("part1"), 1)
                        act.wait_ge(sem("residue"), n + 1)
                        A_(hp2, hres).then_inc(sem("part2"), 1)
                    elif step in (2, 4):
                        act.wait_ge(sem("hs_ready"), n + 1)
                        a = step // 4
                        for q in range(2):
                            p = full_bank(act, ("sc", n, a, q))
                            link(A_(s4[:, 4 * a:4 * a + 4, q, :], p.rearrange("p (a b) -> p a b", b=P)))
                            act.sem_inc(free(("sc", n, a, q)), 1)
                            act.sem_inc(sem("scores_ready"), 1)
                    elif step == 6:
                        act.wait_ge(sem("best_ready"), n + 1)
                        A_(gat, gat, ACT.Exp).then_inc(sem("best_exp"), 1)

                def copy_outputs(it, n8):
                    act.wait_ge(sem("outputs"), it * SLOTS + (n8 + 2) * SLOTS)
                    act.wait_ge(sem("y_out"), it * 16 + 16 * (n8 + 1))
                    A_(yev[:, :], ps[0:SLOTS, YB:YB + 2, :].rearrange("p a b -> p (a b)")).then_inc(sem("y_copied"), 1)
                    act.wait_ge(sem("y_copied"), it + (n8 + 2))
                    act.dma_start(yscr[bass.ds(it * SLOTS + n8 * SLOTS, SLOTS), :], yev[:, :]).then_inc(sem("y_out"), 16)

                def eight(n, g, it, first):
                    t0 = n * P + g * SEG
                    for hf in range(2):
                        q0 = QUAD * hf
                        act.wait_ge(sem("dots"), it * SLOTS + (t0 + SLOTS + q0 + QUAD))
                        A_(gel[:, q0:q0 + QUAD], dots[:, q0:q0 + QUAD], ACT.Gelu_apprx_tanh).then_inc(sem("gelus"), 1)
                        if hf == 0 and not first:
                            copy_outputs(it, t0 // SLOTS - 1)

                def read_back(n):
                    act.wait_ge(sem("y_out"), 16 + 16 * (P // SLOTS) * (n + 1))
                    act.dma_start(ytok(l), yscr[n * P:(n + 1) * P, :]).then_inc(sem("y_back"), 16)

                route(tile_no, 0)
                for t in range(DT):
                    link(evac(("wq", l, t), qp[:, t, c0:], width=wq))
                    act.sem_inc(free(("wq", l, t)), 1)
                    act.sem_inc(sem("query_ready"), 1)
                    if t == 5:
                        route(tile_no, 2)
                for step in (4, 6):
                    route(tile_no, step)
                if l == 0:
                    act.sem_inc(sem("gelus"), 2)
                    act.sem_inc(sem("y_copied"), 1)
                    act.sem_inc(sem("y_out"), 16)
                for tt in mine:
                    n = tile_no
                    tile_no += 1
                    for g in range(P // SEG):
                        if g == 0 and tt == mine[0]:
                            eight(n, g, 0, True)
                            eight(n, g, 1, False)
                        else:
                            with act.Fori(0, SEG // SLOTS) as it:
                                eight(n, g, it, False)
                        if g == 1 and tt != mine[0]:
                            read_back(n - 1)
                        if tt != mine[-1]:
                            route(n + 1, g)
                copy_outputs(0, (n + 1) * P // SLOTS - 1)
                read_back(n)
                nx += 1

        @block.gpsimd
        def _(pool):
            pool.wait_ge(sem("wsg_loaded"), 16)
            pool.affine_select(out=wsg1, in_=wsg1, compare_op=ALU.is_ge, fill=0.0, base=0,
                               pattern=[[0, SGU_G], [1, P]], channel_multiplier=-1).then_inc(sem("sgu_ready"), 1)
            tile_no = 0
            for l in range(LAYERS):
                pool.wait_ge(sem("h_ready"), 3 + 2 * l)
                for e in (0, SEQ + CV_W // 2):
                    last = pool.memset(upad[:, :, :, e:e + CV_W // 2], 0.0)
                last.then_inc(sem("pad_clear"), 1)
                for tt in [t for ll, t in TILES if ll == l]:
                    n = tile_no
                    tile_no += 1
                    t0 = n * P

                    def gather(table, dst, used, arrived, it, c):
                        pool.wait_ge(sem(used), it * SEG + (t0 + QUAD * (c + 1)))
                        pool.sem_inc(sem("pool_paced"), 1)
                        for j in range(QUAD):
                            s = QUAD * (c % 2) + j
                            off = bass.IndirectOffsetOnAxis(idl[:, c % 4, j:j + 1], 0)
                            pool.indirect_dma_start(dst[:, s, :], None, table, off).then_inc(sem(f"{arrived}{s}"), 16)

                    def indices(it, c):
                        pool.tensor_copy(idl[:, c % 4, :], idxT[:, n % 2, bass.ds(it * SEG + QUAD * c, QUAD)]).then_inc(sem("idl_ready"), 1)
                        pool.wait_ge(sem("idl_ready"), it * 4 + (t0 // QUAD + c + 1))
                        pool.sem_inc(sem("pool_paced"), 1)

                    def sixteen(it, last_one):
                        for c in range(4):
                            if not (last_one and c == 3):
                                indices(it, c + 1)
                                gather(A["u_tab"], Us, "dots", "u_arrived", it, c + 1)
                            gather(A["v_tab"], Vs, "outputs", "v_arrived", it, c)

                    pool.wait_ge(sem("idx_ready"), n + 1)
                    indices(0, 0)
                    gather(A["u_tab"], Us, "dots", "u_arrived", 0, 0)
                    with pool.Fori(0, P // SEG - 1) as it:
                        sixteen(it, False)
                    sixteen(P // SEG - 1, True)


def _columns(v):
    return v.reshape(-1, P).T


def kernel(**inputs):
    import numpy as np
    import concourse.bacc as bacc
    from concourse.bass_utils import run_bass_kernel_spmd

    I = {k: np.asarray(v) for k, v in inputs.items()}
    arrays = {}
    for name in ("w_ada", "w_in", "w_proj_attn", "w_proj_sgu", "w_out", "w_ff1", "w_ff2", "b_sgu", "w_mod_2", "w_in_2", "w_ukv_2",
                 "w_uq_2", "wb_attn_2", "wb_fnet_2", "wb_conv_2", "w_out_2", "w_query_2"):
        arrays[name] = np.ascontiguousarray(I[name])
    arrays["u_tab"] = np.ascontiguousarray(I["u_tab_2"]).reshape(LAYERS * NEXP, D)
    arrays["v_tab"] = np.ascontiguousarray(I["v_tab_2"]).reshape(LAYERS * NEXP, D)
    cols = [_columns(I[n].reshape(-1)) for n in ("c", "b_ada", "g_mix", "g_sgu", "g_ffn", "g_final", "c_ctx_2", "c_2")]
    for l in range(LAYERS):
        for n in ("b_mod_2", "g_norm1_2", "g_ckv_2", "g_cq_2", "b_dw_2", "g_cln_2", "b_cln_2"):
            cols.append(_columns(I[n][l]))
        cols.append(I["w_dw_2"][l, :, 0, :].reshape(CV_W, 2, P).transpose(2, 1, 0).reshape(P, 2 * CV_W))
        cols.append(_columns(I["g_norm2_2"][l]))
    arrays["vec"] = np.ascontiguousarray(np.concatenate(cols, axis=1))
    arrays["xT"] = np.ascontiguousarray(I["x"][0].T.reshape(DT, P, SEQ).transpose(1, 0, 2))
    arrays["ctxT"] = np.ascontiguousarray(I["ctx_2"][0].T.reshape(DT, P, SEQ).transpose(1, 0, 2))
    arrays["wsgT"] = np.ascontiguousarray(I["w_sgu"][0].transpose(2, 0, 1))
    arrays["keys"] = np.ascontiguousarray(I["sub_keys_2"].transpose(0, 2, 4, 1, 3).reshape(LAYERS, P, PH, NKEY))
    arrays["gqk"] = np.ascontiguousarray(np.stack([I["g_qn_2"][0], I["g_kn_2"][0], I["g_qn_2"][1], I["g_kn_2"][1]], axis=1))

    f = np.float32
    arrays["ident"] = np.eye(P, dtype=f)
    key, q = np.arange(SEQ), np.arange(P)
    arrays["mask"] = np.stack([np.where(key[None, :] <= (t * P + q)[:, None], 0.0, -1e30) for t in range(2)], axis=1).astype(f)
    w = 2 * np.pi * (np.arange(SEQ)[:, None] * np.arange(SEQ)[None, :] % SEQ) / SEQ
    both = np.concatenate([np.cos(w), np.sin(w)], axis=1)
    arrays["dft"] = np.ascontiguousarray(both.reshape(2, P, 512).transpose(1, 0, 2)).astype(f)
    w = 2 * np.pi * (np.arange(64)[:, None] * np.arange(64)[None, :] % 64) / 64
    arrays["dftc"] = np.stack([np.kron(np.eye(2), np.cos(w)), -np.kron(np.eye(2), np.sin(w))], axis=1).astype(f) / f(128.0)
    half = ROPE // 2
    inv = np.power(f(10000.0), -np.arange(0, half, 2, dtype=f) / f(half)).astype(f)
    row, col = np.arange(SEQ) // 64, np.arange(SEQ) % 64
    ar, ac = row[:, None].astype(f) * inv, col[:, None].astype(f) * inv
    ang = np.concatenate([ar, ar, ac, ac], axis=1)
    rope = np.zeros((QK, 2, TALL), f)
    rope[:, 0, :] = 1.0
    rope[NOPE:, 0, SEQ:] = np.cos(ang).T
    rope[NOPE:, 1, SEQ:] = np.sin(ang).T
    arrays["rope"] = rope
    rot = np.zeros((QK, QK), f)
    for a in range(2):
        for i in range(8):
            lo = NOPE + 16 * a + i
            rot[lo + 8, lo] = -1.0
            rot[lo, lo + 8] = 1.0
    arrays["rotm"] = rot
    arrays["iota16"] = np.tile(np.arange(TOPK, dtype=f), (P, 1))

    nc = bacc.Bacc("TRN2", target_bir_lowering=False, num_devices=1)
    A = {}
    for name, a in arrays.items():
        A[name] = nc.dram_tensor(f"in_{name}", a.shape, mybir.dt.from_np(a.dtype), kind="ExternalInput").ap()
    out = nc.dram_tensor("out_x", (P, DT, SEQ), mybir.dt.float32, kind="ExternalOutput").ap()
    two_blocks_kernel(nc, A, out)
    r = run_bass_kernel_spmd(nc, [{f"in_{k}": v for k, v in arrays.items()}], core_ids=[0])
    y = r.results[0]["out_x"]
    return np.ascontiguousarray(y.transpose(1, 0, 2).reshape(D, SEQ).T)[None]
```

```python
import concourse.bass as bass
from concourse import mybir
from contextlib import ExitStack

P = 128
D = 1024
DT = D // P
SEQ = 256
TALL = 2 * SEQ
EPS = 1e-6
LAYERS = 2

HEADS1, HD1 = 8, 64
SGU_W, SGU_G = 512, 8
FF_T = 4096 // P

MH, QK, NOPE, ROPE, VH = 8, 96, 64, 32, 64
KV_IN, Q_LORA, FN_C, CV_C, CV_W = 160, 256, 256, 256, 31
COL_ZF = KV_IN + Q_LORA
COL_ZC = COL_ZF + FN_C
COL_ZG = COL_ZC + 2 * CV_C
PH, NKEY, TOPK = 8, 128, 16
NEXP = NKEY * NKEY

SLOTS = 8
QUAD = 4
GROUP = 32
SEG = 16
EIGHTS = P // SLOTS
STEPS = ["residue", "parts", "top 0", "top 1", "pairs 0", "pairs 1", "top 2", "top 3", "pairs 2", "pairs 3",
         "keys 0", "keys 1", "keys 2", "keys 3", "experts", None]
ACT_STEPS = {0: "residue", 1: "scores 0", 5: "scores 1", 10: "exp"}

VEC = {}
_at = 0
for _n, _w in [("c", 8), ("b_ada", 48), ("g_mix", 8), ("g_sgu", 4), ("g_ffn", 8), ("g_final", 8),
               ("c_ctx_2", 8), ("c_2", 8)]:
    VEC[_n] = (_at, _w)
    _at += _w
for _l in range(LAYERS):
    for _n, _w in [("b_mod", 48), ("g_norm1", 8), ("g_ckv", 1), ("g_cq", 2), ("b_dw", 2), ("g_cln", 2),
                   ("b_cln", 2), ("w_dw", 2 * CV_W), ("g_norm2", 8)]:
        VEC[_n, _l] = (_at, _w)
        _at += _w
NVEC = _at


def two_blocks_kernel(nc, A, out):
    f32, bf16, u32 = mybir.dt.float32, mybir.dt.bfloat16, mybir.dt.uint32
    ALU = mybir.AluOpType
    ACT = mybir.ActivationFunctionType
    AX = mybir.AxisListType
    MUL, ADD, SUB = ALU.mult, ALU.add, ALU.subtract

    ctx = ExitStack()
    with ctx:
        def sb(name, shape, dt=f32):
            return ctx.enter_context(nc.sbuf_tensor(name, shape, dt))

        sems = {}

        def sem(name):
            if name not in sems:
                sems[name] = ctx.enter_context(nc.semaphore(name))
            return sems[name]

        X = sb("X", [P, DT, TALL])
        H = sb("H", [P, DT, TALL])
        RING = 2
        W = sb("W", [P, RING, 4096])
        vec = sb("vec", [P, NVEC])
        ident = sb("ident", [P, P])
        ones = sb("ones", [P, P])
        dft = sb("dft", [P, 2, 512])
        dftc = sb("dftc", [P, 2, P])
        ropet = sb("ropet", [QK, 2, TALL])
        rotm = sb("rotm", [QK, QK])
        gqk = sb("gqk", [QK, 2 * LAYERS])
        iota16 = sb("iota16", [P, TOPK])
        selb = sb("selb", [96, 32], bf16)
        cond = sb("cond", [P, 3, DT])
        condt = sb("condt", [P, 3 * DT])
        mod1 = sb("mod1", [P, 48])
        mod2 = sb("mod2", [P, LAYERS, 48, 2])
        onecol = sb("onecol", [P, 31])
        gs = sb("gs", [P, 2, DT, 2])
        half = sb("half", [P, DT, 2])
        lnh = sb("lnh", [P, 4])
        stat = sb("stat", [P, 4, 16])
        varb = sb("varb", [P, TALL])
        rstd = sb("rstd", [P, TALL])
        idxT = sb("idxT", [P, 2, P], u32)
        gateT = sb("gateT", [P, 2, P])
        idl = sb("idl", [P, 4, QUAD], u32)
        dots = sb("dots", [P, SLOTS])
        gel = sb("gel", [P, SLOTS])
        acts = sb("acts", [P, SLOTS, SLOTS])
        yev = sb("yev", [SLOTS, D])
        ARENA = 30208
        arena = sb("arena", [P, ARENA])

        def view(at, *shape, dt=None, parts=P):
            n = 1
            for s in shape:
                n *= s
            words = n if dt is None else (n + 1) // 2
            assert at + words <= ARENA
            ap = arena[0:parts, at:at + words]
            if dt is not None:
                ap = ap.bitcast(dt)
            if len(shape) == 2:
                ap = ap.rearrange("p (a b) -> p a b", b=shape[1])
            if len(shape) == 3:
                ap = ap.rearrange("p (a b c) -> p a b c", b=shape[1], c=shape[2])
            if len(shape) == 4:
                ap = ap.rearrange("p (a b c d) -> p a b c d", b=shape[1], c=shape[2], d=shape[3])
            return ap

        q1 = view(0, 4, SEQ)
        k1 = view(1024, 4, SEQ)
        v1 = view(2048, 2, 512)
        u1 = view(3072, 4, SEQ)
        vs1 = view(4096, 2, SGU_W)
        vsq1 = view(5120, 2, SGU_W)
        gate1 = view(6144, DT, 2, SEQ)
        P1 = view(10240, 16, SEQ)
        PT1 = view(14336, 2, 2, SEQ)
        att1 = view(15360, 4, SEQ)
        ysg1 = view(16384, 4, SEQ)
        wsg1 = view(17408, SGU_G, P)
        bsg1 = view(18432, 4, P)
        mrg1 = view(18944, DT, SEQ)
        sq1 = view(20992, DT, SEQ)
        mask1 = view(23040, 2, SEQ)
        mt1 = view(23552, 2, 2, SEQ)
        ff1 = view(0, FF_T, SEQ)
        ssg1 = stat[:, 0, 0:2]
        modw = view(24576, 2, 4, 512)

        def products(b, s):
            return H[:, 4 * b + 2 * s:4 * b + 2 * s + 2, 0:SEQ]

        kT = view(0, MH, TALL, parts=QK)
        qT = view(4096, MH, TALL, parts=QK)
        vtok = view(8192, 4, 512)
        PT2 = view(10240, 2, 4, SEQ)
        P2 = view(12288, 16, TALL)
        hsq = view(10240, 3, TALL, parts=QK)
        ltmp = view(11776, TALL)
        hvar = view(28672, TALL, parts=16)
        hrs = view(29184, TALL, parts=16)
        htmp = view(29696, TALL, parts=16)
        rtmp = view(29696, TALL, parts=QK)
        br = view(20480, DT, TALL)
        ckv = view(24576, TALL)
        cq = view(25088, 2, TALL)
        lsq = view(26112, 3, TALL)
        cqvar = view(27648, TALL)
        cqrs = view(28160, TALL)
        ckvn = view(24576, TALL)
        cqn = view(25088, 2, TALL)
        zft = view(12288, 4, FN_C)
        g1f = view(13312, 4, 512)
        upad = view(15360, 2, 2, SEQ + CV_W - 1)
        acc = view(16512, 2, TALL)
        csq = view(17536, 2, TALL)
        mu = view(18560, TALL)
        cah = view(19072, TALL)
        cth = view(19584, TALL)
        sqx = view(12288, DT, TALL)
        m2 = view(0, DT, TALL)
        sig2 = view(10240, 2, TALL)
        br2 = view(11264, 2, TALL)
        Us = view(0, SLOTS, D)
        Vs = view(8192, SLOTS, D)
        hs = view(16384, 2, 4, D, dt=bf16, parts=96)
        qp = view(20480, DT, TALL)
        sc = view(24576, 16, NKEY)
        cand = view(26624, PH // 2, 256)
        eqp = view(27648, PH // 2, TOPK, TOPK, dt=bf16)
        keys = view(28160, PH, NKEY)
        ytok = view(29184, D)
        hp1 = view(24576, D, dt=bf16)
        hp2 = view(25088, D, dt=bf16)
        hp3 = view(25600, D, dt=bf16)
        hres = view(26624, D)
        top = sb("top", [P, 16, TOPK])
        tix = varb[:, 0:256].bitcast(u32).rearrange("p (a b) -> p a b", b=TOPK)
        tixf = varb[:, 256:512].rearrange("p (a b) -> p a b", b=TOPK)
        best = rstd[:, 0:128].rearrange("p (a b) -> p a b", b=TOPK)
        pos = rstd[:, 128:256].bitcast(u32).rearrange("p (a b) -> p a b", b=TOPK)
        posi = rstd[:, 256:512].bitcast(u32).rearrange("p (a b) -> p a b", a=2)
        posf = view(24576, 2, PH, TOPK)
        ij = view(24832, 2, PH, TOPK)
        eid = view(25088, P)
        gat = view(25216, PH, TOPK)
        gsum = view(25344, 2, PH)
        yscr = nc.dram_tensor("yscr", (6 * P, D), f32, kind="Internal").ap()

        NA, NBANK = 6, 8
        HB, YB = 0, 4
        ps = ctx.enter_context(nc.psum_tensor("ps", [P, NBANK, 512], f32))

        def V(name, l=None):
            a, n = VEC[name] if l is None else VEC[name, l]
            return vec[:, a:a + n]

        chunks = []

        def chunk(name, src, kt, n):
            chunks.append((name, src, kt, n))

        def rows(ap):
            return ap.rearrange("(k p) n -> p k n", p=P)

        products_of = [("mod1", 1, j) for j in range(2, 12, 3)] + [(("mod2", l), 2, j) for l in range(LAYERS) for j in range(12)]
        ahead = {"n3": [27], **{("ada", j): [j // 3] for j in range(1, 12, 3)}}
        for j in range(8):
            ahead["in1", j + 1] = [4 + j]
            ahead["ffb", j] = [19 + j]
            if j:
                ahead["ffa", j] = [11 + j]

        ADA = [j for j in range(12) if j % 3 < 2]
        for j in ADA:
            chunk(("ada", j), rows(A["w_ada"][0])[:, :, j * 512:(j + 1) * 512], 8, 512)
        for j in range(9):
            chunk(("in1", j), rows(A["w_in"][0])[:, :, j * 512:(j + 1) * 512], 8, 512)
        chunk("pa1", rows(A["w_proj_attn"][0]), 4, 1024)
        chunk("ps1", rows(A["w_proj_sgu"][0]), 4, 1024)
        for j in range(2):
            chunk(("out1", j), rows(A["w_out"][0])[:, :, j * 512:(j + 1) * 512], 8, 512)
        for j in range(8):
            chunk(("ffa", j), rows(A["w_ff1"][0])[:, :, j * 512:(j + 1) * 512], 8, 512)
        for j in range(8):
            chunk(("ffb", j), rows(A["w_ff2"][0])[:, :, j * P:(j + 1) * P], 32, P)
        for l in range(LAYERS):
            win = rows(A["w_in_2"][l])
            chunk(("inC", l), win[:, :, COL_ZC:COL_ZG], 8, 512)
            chunk(("inA", l), win[:, :, 0:COL_ZF], 8, COL_ZF)
            chunk(("inB", l), win[:, :, COL_ZF:COL_ZC], 8, FN_C)
            chunk(("ukv", l), rows(A["w_ukv_2"][l]), 1, MH * P)
            chunk(("uq", l), rows(A["w_uq_2"][l]), 2, MH * QK)
            for j in range(2):
                for b, (wb, kt) in enumerate([("wb_attn_2", 4), ("wb_fnet_2", 2), ("wb_conv_2", 2)]):
                    at = COL_ZG + b * D + j * 512
                    chunk(("zg", l, j, b), win[:, :, at:at + 512], 8, 512)
                    chunk(("wb", l, j, b), rows(A[wb][l])[:, :, j * 512:(j + 1) * 512], kt, 512)
            for j in range(2):
                chunk(("out2", l, j), rows(A["w_out_2"][l])[:, :, j * 512:(j + 1) * 512], 8, 512)
            for j in range(2):
                chunk(("wq", l, j), rows(A["w_query_2"][l])[:, :, j * 512:(j + 1) * 512], 8, 512)
        chunk_at = {c[0]: i for i, c in enumerate(chunks)}

        def ring_slot(i):
            _, _, kt, n = chunks[i]
            return W[:, i % RING, 0:kt * n].rearrange("p (k n) -> p k n", n=n)

        QC = [0, SEQ]
        TILES = [(l, t) for l in range(LAYERS) for t in range(QC[l] // P, TALL // P)]

        def streams(l):
            return range(QC[l] // SEQ, 2)

        ATT = [("a1", None, 0, SEQ)] + [(f"a2{l}{s}", l, s * SEQ, (s + 1) * SEQ) for l in range(LAYERS) for s in streams(l)]

        group = {}

        block = ctx.enter_context(nc.Block())

        @block.tensor
        def _(pe):
            mm = pe.matmul

            turns = [0, 0]
            fulls = [0]
            newest = [None]
            uses = [0] * NBANK

            def bank(name, routing=False):
                b = NA + turns[1] % 2 if routing else turns[0] % NA
                turns[routing] += 1
                group[name] = [None, b]
                newest[0] = name
                if uses[b]:
                    pe.wait_ge(sem(f"bank_free{b}"), uses[b])
                uses[b] += 1
                return ps[:, b, :]

            def full(last, name=None):
                group[name or newest[0]][0] = fulls[0]
                fulls[0] += 1
                last.then_inc(sem("psum_full"), 1)

            def weights(name):
                i = chunk_at[name]
                pe.wait_ge(sem(f"w_arrived{i % RING}"), 16 * (i // RING + 1))
                return ring_slot(i)

            def done_with_weights():
                pe.drain().then_inc(sem("w_used"), 1)

            def acc_mm(o, lhs, rhs):
                n = len(lhs)
                for k in range(n):
                    last = mm(o, lhs[k], rhs[k], start=(k == 0), stop=(k == n - 1))
                return last

            def features(name, w, col, src, kt, c0, c1, m=P, first=False):
                o = bank(name)
                for k in range(kt):
                    if first:
                        h_ready(k)
                    last = mm(o[0:m, 0:c1 - c0], w[:, k, col:col + m], src[:, k, c0:c1], start=(k == 0), stop=(k == kt - 1))
                full(last)

            turned = [0]

            def turn(name, n, j):
                turned[0] += 1
                pe.wait_ge(sem("rows_copied"), turned[0])
                o = ps[:, group[name][1], :]
                for t in range(4):
                    last = pe.transpose(o[:, (4 * j + t) * n:(4 * j + t + 1) * n], yev[0:n, (j % 2) * 512 + t * P:(j % 2) * 512 + (t + 1) * P], ident[0:n, 0:n])
                if j < 11:
                    last.then_inc(sem("rows_turned"), 1)
                else:
                    full(last, name)

            def modulation(name, parts, lhs, n, these):
                bank(name, True)
                for j in these:
                    w = weights((*parts, j))
                    o = bank((name, "rows", j))
                    full(acc_mm(o[0:n, :], lhs, [w[:, k, :] for k in range(8)]))
                    done_with_weights()
                    if j:
                        turn(name, n, j - 1)
                    run_ahead((*parts, j))

            def run_ahead(step):
                for m in ahead.get(step, ()):
                    name, n, j = products_of[m]
                    if j == 0:
                        bank(name, True)
                    pe.wait_ge(sem("products_ready"), m + 1)
                    o = bank((name, "rows", j))
                    full(acc_mm(o[0:n, :], [onecol[:, 15 - s:15 - s + n] for s in range(n)], [products(m % 2, s) for s in range(n)]))
                    if j:
                        turn(name, n, j - 1)
                    if j == 11:
                        turn(name, n, 11)

            norms, made = [0], [0]

            def norm(name, sq, c0, c1, summed=False):
                o = bank(name)
                last = None
                if summed:
                    pe.wait_ge(sem("squares_added"), summed)
                for k in (0, DT - 1) if summed else range(DT):
                    pe.wait_ge(sem("squares_ready"), DT * norms[0] + k + 1)
                    last = mm(o[:, 0:c1 - c0], ones[:, :], sq[:, k, c0:c1], start=(k == 0), stop=(k == DT - 1))
                full(last)
                norms[0] += 1
                made[0] += 1

            def h_ready(k):
                pe.wait_ge(sem("h_ready"), DT * (made[0] - 1) + k + 1)

            def attention(tag, q, k, v, pt, prob, qcols, nk, scores_of):
                ktiles = nk // P
                for i in range(16 + 5):
                    if i < 16:
                        h, t = i // 2, i % 2
                        lhs, rhs = scores_of(h, t)
                        o = bank((tag, "s", i))
                        full(mm(o[:, 0:nk], lhs, rhs, start=True, stop=True))
                    if 0 <= i - 3 < 16:
                        pe.wait_ge(sem(f"{tag}_probs"), i - 2)
                        o = bank((tag, "t", i - 3))
                        for kt in range(ktiles):
                            last = pe.transpose(o[:, kt * P:(kt + 1) * P], prob[:, i - 3, kt * P:(kt + 1) * P], ident[:, :])
                        full(last)
                    if 0 <= i - 5 < 16 and (i - 5) % 2:
                        h = (i - 5) // 2
                        pe.wait_ge(sem(f"{tag}_probsT"), 2 * h + 2)
                        o = bank((tag, "o", h))
                        full(acc_mm(o[:, 0:SEQ], [v(kt)[:, (h // 2) * P:(h // 2 + 1) * P] for kt in range(ktiles)],
                                    [pt[:, h % 2, kt, :] for kt in range(ktiles)]))

            pe.wait_ge(sem("ones_set"), 1)
            pe.wait_ge(sem("cond_ready"), 1)
            pe.wait_ge(sem("ident_set"), 16)
            modulation("mod1", ("ada",), [cond[:, 0, k:k + 1] for k in range(8)], 1, ADA)
            norm("ss_n1", sq1, 0, SEQ)
            X0 = SEQ
            for j in range(9):
                w = weights(("in1", j))
                for t in range(4):
                    if j in (2, 4):
                        if t < 2:
                            o = bank(("in1", j, t))
                            full(acc_mm(o, [H[:, k, X0 + t * P:X0 + (t + 1) * P] for k in range(8)], [w[:, k, :] for k in range(8)]))
                    else:
                        features(("in1", j, t), w, t * P, H, 8, X0, TALL, first=(j + t == 0))
                done_with_weights()
                run_ahead(("in1", j))

            def scores1(h, t):
                r = slice((h % 2) * HD1, (h % 2) * HD1 + HD1)
                return q1[r, h // 2, t * P:(t + 1) * P], k1[r, h // 2, :]

            pe.wait_ge(sem("qkv1_ready"), 10)
            attention("a1", q1, k1, lambda kt: v1[:, kt, :], PT1, P1, 0, SEQ, scores1)
            pe.wait_ge(sem("sgu_ready"), 2)
            for p in range(4):
                o = bank(("sg", p))
                for c in range(2):
                    last = mm(o[:, c * SEQ:(c + 1) * SEQ], vs1[:, c, p * P:(p + 1) * P], wsg1[:, 2 * p:2 * p + 2, :], start=True, stop=True)
                full(last)
            pe.wait_ge(sem("mix1_ready"), 12)
            wa, ws = weights("pa1"), weights("ps1")
            for n in range(DT):
                o = bank(("mg1", n))
                acc_mm(o[:, 0:SEQ], [wa[:, k, n * P:(n + 1) * P] for k in range(4)], [att1[:, k, :] for k in range(4)])
                full(acc_mm(o[:, SEQ:], [ws[:, k, n * P:(n + 1) * P] for k in range(4)], [ysg1[:, k, :] for k in range(4)]))
            done_with_weights()
            done_with_weights()
            pe.wait_ge(sem("merged1"), DT)
            for j in range(2):
                w = weights(("out1", j))
                for t in range(4):
                    features(("out1", 4 * j + t), w, t * P, mrg1, 8, 0, SEQ)
                done_with_weights()
            norm("ss_n2", sq1, 0, SEQ, summed=1)
            for j in range(8):
                w = weights(("ffa", j))
                for t in range(4):
                    features(("ffa", 4 * j + t), w, t * P, H, 8, X0, TALL, first=(j + t == 0))
                done_with_weights()
                run_ahead(("ffa", j))
            pe.wait_ge(sem("ff_ready"), FF_T)
            for n in range(DT):
                w = weights(("ffb", n))
                features(("ffb", n), w, 0, ff1, FF_T, 0, SEQ)
                done_with_weights()
                run_ahead(("ffb", n))
            norm("ss_n3", sq1, 0, SEQ, summed=2)
            made[0] -= 1
            run_ahead("n3")

            pe.wait_ge(sem("const_loaded"), 16 * 6)
            pe.wait_ge(sem("sel_ready"), 1)
            tile_no = 0
            for l in range(LAYERS):
                c0 = QC[l]
                norm(("ss_n1", l), sqx, 0, TALL)
                w = weights(("inC", l))
                for t in (0, 2, 1, 3):
                    features(("zc", l, t), w, t * P, H, 8, c0, TALL, first=(t == 0))
                done_with_weights()
                w = weights(("inA", l))
                features(("ckv", l), w, 0, H, 8, 0, TALL)
                features(("kr", l), w, NOPE, H, 8, 0, TALL, m=QK)
                for t in range(2):
                    features(("cq", l, t), w, KV_IN + t * P, H, 8, c0, TALL)
                done_with_weights()
                w = weights(("inB", l))
                for t in range(c0 // P, 4):
                    o = bank(("zf", l, t))
                    full(acc_mm(o[:, 0:FN_C], [H[:, k, t * P:(t + 1) * P] for k in range(8)], [w[:, k, :] for k in range(8)]))
                done_with_weights()
                pe.wait_ge(sem("lat_squares"), 2 * l + 1)
                o = bank(("ss_ckv", l))
                full(mm(o, ones[:, :], lsq[:, 0, :], start=True, stop=True))
                pe.wait_ge(sem("lat_squares"), 2 * l + 2)
                o = bank(("ss_cq", l))
                full(acc_mm(o[:, 0:TALL - c0], [ones[:, :]] * 2, [lsq[:, 1 + k, c0:TALL] for k in range(2)]))
                pe.wait_ge(sem("zf_ready"), 4 if l == 0 else 6)
                for s in streams(l):
                    for c in range(2):
                        o = bank(("dt", l, s, c))
                        full(acc_mm(o, [zft[:, 2 * s + t, c * P:(c + 1) * P] for t in range(2)], [dft[:, t, :] for t in range(2)]))
                for s in streams(l):
                    pe.wait_ge(sem("dft_ready"), 2 * (s + 1) if l == 0 else 6)
                    o = bank(("dc", l, s))
                    for c in range(2):
                        last = acc_mm(o[:, c * SEQ:(c + 1) * SEQ], [dftc[:, 0, :], dftc[:, 1, :]],
                                      [g1f[:, 2 * s + c, 0:SEQ], g1f[:, 2 * s + c, SEQ:512]])
                    full(last)
                wkv = weights(("ukv", l))
                pe.wait_ge(sem("ckvn_ready"), l + 1)
                vcols = wkv[:, 0, :].rearrange("p (h c) -> p h c", c=P)[:, :, NOPE:P]
                for t in range(4):
                    o = bank(("v", l, t))
                    full(mm(o, ckvn[:, t * P:(t + 1) * P], vcols, start=True, stop=True))
                sums = bank(("hsum", l), True)
                for i in range(16 + 1):
                    if i < 16:
                        h = i % 8
                        if i < 8:
                            o = bank(("hp", l, i))
                            full(mm(o[0:NOPE, :], wkv[:, 0, h * P:h * P + NOPE], ckvn[:, :], start=True, stop=True))
                        else:
                            if i == 8:
                                wuq = weights(("uq", l))
                                pe.wait_ge(sem("cqn_ready"), l + 1)
                            features(("hp", l, i), wuq, h * QK, cqn, 2, c0, TALL, m=QK)
                        if i in (7, 15):
                            done_with_weights()
                    if i >= 1:
                        k = i - 1
                        a = 0 if k < 8 else c0
                        pe.wait_ge(sem("head_squares"), 16 * l + i)
                        last = mm(sums[0:16, a:TALL], onecol[0:QK, 15 - k:31 - k], hsq[:, k % 3, a:TALL], start=(k == 0), stop=(k == 15))
                        if k < 15:
                            last.then_inc(sem("squares_summed"), 1)
                full(last, ("hsum", l))

                def spread_root(k):
                    a = 0 if k < 8 else c0
                    o = bank(("hb", l, k))
                    full(mm(o[0:QK, 0:TALL - a], ident[0:16, k:k + 1].to_broadcast([16, QK]), hrs[:, a:TALL], start=True, stop=True))

                pe.wait_ge(sem("conv_ready"), l + 1)
                o = bank(("cmean", l))
                full(acc_mm(o[:, 0:TALL - c0], [ones[:, :]] * 2, [acc[:, c, c0:TALL] for c in range(2)]))
                pe.wait_ge(sem("head_roots"), l + 1)
                for k in range(2):
                    spread_root(k)
                pe.wait_ge(sem("conv_squares"), l + 1)
                o = bank(("cvar", l))
                full(acc_mm(o[:, 0:TALL - c0], [ones[:, :]] * 2, [csq[:, c, c0:TALL] for c in range(2)]))
                for i in range(2, 16 + 4):
                    if i < 16:
                        spread_root(i)
                    if i >= 4 and i % 2 == 0:
                        pair = (i - 4) // 2
                        pe.wait_ge(sem("head_normed"), 16 * l + 2 * pair + 2)
                        o = bank(("hr", l, pair))
                        src = kT if pair < 4 else qT
                        for e in range(2):
                            last = mm(o[0:QK, e * SEQ:(e + 1) * SEQ], rotm[:, :], src[:, (2 * pair + e) % 8, SEQ:TALL], start=True, stop=True)
                        full(last)
                pe.wait_ge(sem("heads_ready"), 8 * (l + 1))
                for tag, al, q0, nk in ATT:
                    if al != l:
                        continue

                    def scores2(h, t):
                        return qT[:, h, q0 + t * P:q0 + (t + 1) * P], kT[:, h, 0:nk]

                    attention(tag, qT, kT, lambda kt: vtok[:, kt, :], PT2, P2, q0, nk, scores2)
                pe.wait_ge(sem("conv_done"), l + 1)
                pe.wait_ge(sem("att_ready"), 8 * (len([a for a in ATT if a[1] is not None and a[1] <= l])))
                for j in range(2):
                    for b, (k0, kt) in enumerate([(0, 4), (4, 2), (6, 2)]):
                        wz = weights(("zg", l, j, b))
                        for t in range(4):
                            features(("zg", l, j, b, t), wz, t * P, H, 8, c0, TALL)
                        done_with_weights()
                        wb = weights(("wb", l, j, b))
                        for t in range(4):
                            o = bank(("br", l, j, b, t))
                            full(acc_mm(o[:, 0:TALL - c0], [wb[:, k, t * P:(t + 1) * P] for k in range(kt)],
                                        [br[:, k0 + k, c0:TALL] for k in range(kt)]))
                        done_with_weights()
                pe.wait_ge(sem("merged2"), DT * (l + 1))
                for j in range(2):
                    w = weights(("out2", l, j))
                    for t in range(4):
                        features(("out2", l, 4 * j + t), w, t * P, m2, 8, c0, TALL)
                    done_with_weights()
                norm(("ss_n2", l), sqx, c0, TALL, summed=3 + l)
                mine = [t for ll, t in TILES if ll == l]

                def hidden(n, tt, first=False):
                    for a in range(2):
                        o = bank(("ht", n, a), True)
                        for k in range(4):
                            if first:
                                h_ready(4 * a + k)
                            last = pe.transpose(o[:, k * P:(k + 1) * P], H[:, 4 * a + k, tt * P:(tt + 1) * P], ident[:, :])
                        full(last)

                def scores(n, tt, a):
                    for p in range(2):
                        o = bank(("sc", n, a, p), True)
                        for hh in range(4):
                            h = 4 * a + hh
                            last = mm(o[:, hh * P:(hh + 1) * P], qp[64 * p:64 * p + 64, h, tt * P:(tt + 1) * P],
                                      keys[64 * p:64 * p + 64, h, :], start=True, stop=True)
                        full(last)

                def routes(n):
                    pe.wait_ge(sem("routed"), n + 1)
                    o = bank(("ij", n), True)
                    pe.transpose(o[:, 0:P], eid, ident[:, :])
                    full(pe.transpose(o[:, P:2 * P], gat.rearrange("p a b -> p (a b)"), ident[:, :]))

                def outputs_back(n):
                    pe.wait_ge(sem("y_back"), 16 * (n + 1))
                    for a in range(2):
                        o = bank(("yt", n, a), True)
                        for k in range(4):
                            last = pe.transpose(o[:, k * P:(k + 1) * P], ytok[:, (4 * a + k) * P:(4 * a + k + 1) * P], ident[:, :])
                        full(last)

                def spread(n, g, it, j):
                    pe.wait_ge(sem("dots"), it * SLOTS + (n * P + g * GROUP + SLOTS + j - 1))
                    one = selb[:, bass.ds(it * SLOTS + j, 1)]
                    for hf in range(2):
                        last = mm(ps[:, HB + 2 * (j % 2) + hf, :], one.to_broadcast([96, P]),
                                  hs[:, n % 2, g, hf * 512:(hf + 1) * 512], start=True, stop=True)
                    last.then_inc(sem("spread"), 1)

                def outputs(n, g, it, c):
                    t0 = n * P + g * GROUP
                    pe.wait_ge(sem("acts"), it * 2 + (t0 // QUAD + c + 1))
                    if c == 0:
                        pe.wait_ge(sem("y_copied"), it + (t0 // SLOTS + 1))
                    for j in range(QUAD * c, QUAD * (c + 1)):
                        pe.wait_ge(sem(f"v_arrived{j}"), it * 16 + 16 * (t0 // SLOTS + 1))
                        for hf in range(2):
                            last = mm(ps[0:SLOTS, YB + hf, :], acts[:, j, :], Vs[:, j, hf * 512:(hf + 1) * 512],
                                      start=(j == 0), stop=(j == SLOTS - 1))
                        last.then_inc(sem("outputs"), 1)

                def eight(n, g, it, last_one):
                    for j in range(QUAD, SLOTS):
                        spread(n, g, it, j)
                    outputs(n, g, it, 0)
                    if not last_one:
                        for j in range(SLOTS, SLOTS + QUAD):
                            spread(n, g, it, j)
                    outputs(n, g, it, 1)

                hidden(tile_no, mine[0], True)
                both = [weights(("wq", l, j)) for j in range(2)]
                first = c0 + P
                for t in range(DT):
                    features(("wq", l, t, 0), both[t // 4], t % 4 * P, H, 8, c0, first)
                pe.wait_ge(sem("keys_loaded"), 16 * (l + 1))
                for a in range(2):
                    pe.wait_ge(sem("query_ready"), 2 * DT * l + 4 * (a + 1))
                    scores(tile_no, mine[0], a)
                for t in range(DT):
                    features(("wq", l, t, 1), both[t // 4], t % 4 * P, H, 8, first, TALL)
                    if t % 4 == 3:
                        done_with_weights()
                pe.wait_ge(sem("query_ready"), 2 * DT * (l + 1))
                routes(tile_no)
                for b in range(NA):
                    pe.wait_ge(sem(f"bank_free{b}"), uses[b])
                if l == 0:
                    pe.sem_inc(sem("outputs"), SLOTS)
                for tt in mine:
                    n = tile_no
                    tile_no += 1
                    pe.wait_ge(sem("hs_ready"), n + 1)
                    for g in range(P // GROUP):
                        if tt != mine[-1] and g == 0:
                            hidden(n + 1, tt + 1)
                        for j in range(QUAD):
                            spread(n, g, 0, j)
                        more = tt != mine[-1]
                        early = more and g != 2
                        with pe.Fori(0, GROUP // SLOTS - (2 if early else 1)) as it:
                            eight(n, g, it, False)
                        if early:
                            if g < 2:
                                scores(n + 1, tt + 1, g)
                            else:
                                routes(n + 1)
                            eight(n, g, GROUP // SLOTS - 2, False)
                        eight(n, g, GROUP // SLOTS - 1, True)
                        if tt != mine[0] and g == 2:
                            outputs_back(n - 1)
                outputs_back(n)
                pe.wait_ge(sem("dots"), (n + 1) * P + SLOTS)
                pe.wait_ge(sem("y_copied"), (n + 1) * P // SLOTS + 1)

        def full_bank(eng, name):
            g, b = group[name]
            eng.wait_ge(sem("psum_full"), g + 1)
            return ps[:, b, :]

        def free(name):
            return sem(f"bank_free{group[name][1]}")

        @block.sync
        def _(sp):
            sp.dma_start(vec[:, :], A["vec"]).then_inc(sem("vec_loaded"), 16)
            sp.dma_start(ident[:, :], A["ident"]).then_inc(sem("ident_set"), 16)

            def weight(i):
                if i >= RING:
                    sp.wait_ge(sem("w_used"), i - RING + 1)
                sp.dma_start(ring_slot(i), chunks[i][1]).then_inc(sem(f"w_arrived{i % RING}"), 16)

            for i in range(RING):
                weight(i)
            sp.dma_start(X[:, :, SEQ:], A["xT"]).then_inc(sem("x_loaded"), 16)
            for i in range(RING, len(ADA)):
                weight(i)
            sp.dma_start(X[:, :, 0:SEQ], A["ctxT"]).then_inc(sem("ctx_loaded"), 16)
            sp.dma_start(mask1, A["mask"]).then_inc(sem("mask_loaded"), 16)
            sp.dma_start(wsg1, A["wsgT"]).then_inc(sem("wsg_loaded"), 16)
            for p in range(4):
                for a in range(2):
                    sp.dma_start(bsg1[64 * a:64 * a + 64, p, :], A["b_sgu"][0, 2 * p + a:2 * p + a + 1, :].to_broadcast([64, P])).then_inc(sem("bsg_loaded"), 16)
            sp.dma_start(dft[:, :, :], A["dft"]).then_inc(sem("const_loaded"), 16)
            sp.dma_start(dftc[:, :, :], A["dftc"]).then_inc(sem("const_loaded"), 16)
            sp.dma_start(ropet[:, :, :], A["rope"]).then_inc(sem("const_loaded"), 16)
            sp.dma_start(rotm[:, :], A["rotm"]).then_inc(sem("const_loaded"), 16)
            sp.dma_start(gqk[:, :], A["gqk"]).then_inc(sem("const_loaded"), 16)
            sp.dma_start(iota16[:, :], A["iota16"]).then_inc(sem("const_loaded"), 16)
            for i in range(len(ADA), len(chunks)):
                weight(i)
                for l in range(LAYERS):
                    if chunks[i][0] == ("out2", l, 1):
                        sp.wait_ge(sem("heads_ready"), 8 * (l + 1))
                        sp.dma_start(keys, A["keys"][l]).then_inc(sem("keys_loaded"), 16)
            sp.wait_ge(sem("x_final"), 2)
            sp.dma_start(out, X[:, :, SEQ:]).then_inc(sem("stored"), 16)
            sp.wait_ge(sem("stored"), 16)

        @block.vector
        def _(dve):
            chain = [0]

            def link(ins):
                chain[0] += 1
                ins.then_inc(sem("dve_chain"), 1)
                dve.wait_ge(sem("dve_chain"), chain[0])

            root_no = [0]

            def mean_square(name, v, n, m=P, width=TALL):
                p = full_bank(dve, name)
                link(dve.tensor_scalar(out=v, in0=p[0:m, 0:width], scalar1=1.0 / n, scalar2=EPS, op0=MUL, op1=ADD))
                dve.sem_inc(free(name), 1)
                dve.sem_inc(sem("var_ready"), 1)

            def rsqrt(v, r, tmp):
                root_no[0] += 1
                dve.wait_ge(sem("root_ready"), root_no[0])
                link(dve.reciprocal(r, r))
                link(dve.scalar_tensor_tensor(out=tmp, in0=r, scalar=-0.5, in1=r, op0=MUL, op1=MUL))
                link(dve.tensor_tensor(out=tmp, in0=tmp, in1=v, op=MUL))
                link(dve.scalar_tensor_tensor(out=r, in0=tmp, scalar=1.5, in1=r, op0=ADD, op1=MUL))

            def multiply(m):
                name, n, j = products_of[m]
                if m >= 2:
                    former = products_of[m - 2]
                    dve.wait_ge(sem("rows_copied"), former[2] + 1 + (0 if former[0] == "mod1" else 12 * (1 + former[0][1])))
                for k in range(DT):
                    if k % 4 == 0:
                        dve.wait_ge(sem(f"modw_arrived{k // 4}"), 16 * (m + 1))
                    w = modw[:, k // 4, k % 4, :].rearrange("p (a b) -> p a b", b=SEQ)
                    for s in range(n):
                        c = cond[:, s + (n == 2), k:k + 1]
                        if k == 0:
                            last = dve.tensor_scalar(out=products(m % 2, s), in0=w, scalar1=c, scalar2=None, op0=MUL)
                        else:
                            last = dve.scalar_tensor_tensor(out=products(m % 2, s), in0=w, scalar=c, in1=products(m % 2, s), op0=MUL, op1=ADD)
                    link(last)
                    if k % 4 == 3:
                        dve.sem_inc(sem("modw_used"), 1)
                dve.sem_inc(sem("products_ready"), 1)

            def gate_norm(dst, gvec, scale, s):
                dve.scalar_tensor_tensor(out=dst, in0=scale, scalar=1.0, in1=gvec, op0=ADD, op1=MUL)

            def h_from(name, c0, c1):
                mean_square(name, varb[:, c0:c1], D, width=c1 - c0)
                rsqrt(varb[:, c0:c1], rstd[:, c0:c1], H[:, 0, c0:c1])
                for k in range(DT):
                    dve.tensor_tensor(out=H[:, k, c0:c1], in0=X[:, k, c0:c1], in1=rstd[:, c0:c1], op=MUL).then_inc(sem("xn_ready"), 1)

            def attention(tag, prob, nk, scale, mask):
                for i in range(16 + 1):
                    if i < 16:
                        p = full_bank(dve, (tag, "s", i))
                        if mask is not None:
                            link(dve.tensor_tensor(out=p[:, 0:nk], in0=p[:, 0:nk], in1=mask[:, i % 2, :], op=ADD))
                        link(dve.tensor_reduce(out=stat[:, 0, i:i + 1], in_=p[:, 0:nk], axis=AX.X, op=ALU.max))
                        dve.tensor_scalar(out=stat[:, 1, i:i + 1], in0=stat[:, 0, i:i + 1], scalar1=-scale, scalar2=None, op0=MUL).then_inc(sem(f"{tag}_max"), 1)
                    if i >= 1:
                        dve.wait_ge(sem(f"{tag}_exp"), i)
                        link(dve.reciprocal(stat[:, 3, i - 1:i], stat[:, 2, i - 1:i]))
                        dve.tensor_scalar(out=prob[:, i - 1, 0:nk], in0=prob[:, i - 1, 0:nk], scalar1=stat[:, 3, i - 1:i], scalar2=None, op0=MUL).then_inc(sem(f"{tag}_probs"), 1)

            dve.memset(ones[:, :], 1.0).then_inc(sem("ones_set"), 1)
            dve.memset(acts[:, :, :], 0.0)
            link(dve.memset(onecol[:, :], 0.0))
            dve.memset(onecol[:, 15:16], 1.0)
            dve.wait_ge(sem("ident_set"), 16)
            for i in range(3):
                last = dve.tensor_copy(selb[32 * i:32 * i + 32, :], ident[0:32, 0:32])
            last.then_inc(sem("sel_ready"), 1)
            dve.wait_ge(sem("vec_loaded"), 16)
            for i, name in enumerate(("c", "c_ctx_2", "c_2")):
                last = dve.tensor_scalar(out=cond[:, i, :], in0=V(name), scalar1=0.5, scalar2=None, op0=MUL)
            link(last)
            dve.sem_inc(sem("cond_half"), 1)
            dve.wait_ge(sem("cond_tanh"), 1)
            ct = condt[:, :].rearrange("p (a b) -> p a b", a=3)
            link(dve.scalar_tensor_tensor(out=cond[:, :, :], in0=ct, scalar=1.0, in1=cond[:, :, :], op0=ADD, op1=MUL))
            dve.sem_inc(sem("cond_ready"), 1)
            def modulations1():
                p = full_bank(dve, "mod1")
                link(dve.tensor_tensor(out=mod1[:, :], in0=p[:, 0:48], in1=V("b_ada"), op=ADD))
                dve.sem_inc(free("mod1"), 1)
                gate_norm(gs[:, 0, :, 0], V("g_mix"), mod1[:, 8:16], 0)
                gate_norm(gs[:, 1, :, 0], V("g_ffn"), mod1[:, 32:40], 0)
                link(dve.tensor_scalar(out=half[:, :, 0], in0=mod1[:, 16:24], scalar1=0.5, scalar2=None, op0=MUL))
                dve.sem_inc(sem("mod_ready"), 1)

            for m in range(4):
                multiply(m)
            modulations1()
            h_from("ss_n1", SEQ, TALL)
            for m in range(4, 12):
                multiply(m)
            dve.wait_ge(sem("vs_squares"), 1)
            link(dve.tensor_scalar(out=stat[:, 1, 0:2], in0=ssg1, scalar1=1.0 / SGU_W, scalar2=EPS, op0=MUL, op1=ADD))
            dve.sem_inc(sem("var_ready"), 1)
            rsqrt(stat[:, 1, 0:2], stat[:, 2, 0:2], stat[:, 3, 0:2])
            for c in range(2):
                last = dve.tensor_scalar(out=vs1[:, c, :], in0=vs1[:, c, :], scalar1=stat[:, 2, c:c + 1], scalar2=None, op0=MUL)
            link(last)
            dve.sem_inc(sem("sgu_ready"), 1)
            dve.wait_ge(sem("mask_loaded"), 16)
            attention("a1", P1, SEQ, 1.0, mask1)
            dve.wait_ge(sem("bsg_loaded"), 128)
            for p4 in range(4):
                p = full_bank(dve, ("sg", p4))
                for c in range(2):
                    for a in range(2):
                        rr = slice(64 * a, 64 * a + 64)
                        last = dve.scalar_tensor_tensor(out=ysg1[rr, p4, c * P:(c + 1) * P], in0=p[rr, c * SEQ + a * P:c * SEQ + (a + 1) * P],
                                                        scalar=V("g_sgu")[rr, p4:p4 + 1], in1=bsg1[rr, p4, :], op0=MUL, op1=ADD)
                link(last)
                dve.sem_inc(free(("sg", p4)), 1)
                dve.tensor_tensor(out=ysg1[:, p4, :], in0=ysg1[:, p4, :], in1=u1[:, p4, :], op=MUL).then_inc(sem("mix1_ready"), 1)
            dve.wait_ge(sem("gates1"), 16)
            for t in range(DT):
                p = full_bank(dve, ("mg1", t))
                link(dve.scalar_tensor_tensor(out=mt1[:, t % 2, :, :], in0=gate1[:, t, :, :], scalar=1.0,
                                              in1=p.rearrange("p (a b) -> p a b", a=2), op0=ADD, op1=MUL))
                dve.sem_inc(free(("mg1", t)), 1)
                dve.tensor_tensor(out=mrg1[:, t, :], in0=mt1[:, t % 2, 0, :], in1=mt1[:, t % 2, 1, :], op=ADD).then_inc(sem("merged1"), 1)

            norms = [1]

            def residual(name_of, gate, c0, ss, sq, before=lambda t: None):
                for t in range(DT):
                    before(t)
                    p = full_bank(dve, name_of(t))
                    for s in ss:
                        a, b = s * SEQ, (s + 1) * SEQ
                        last = dve.scalar_tensor_tensor(out=X[:, t, a:b], in0=p[:, a - c0:b - c0], scalar=gate(t, s), in1=X[:, t, a:b], op0=MUL, op1=ADD)
                    link(last)
                    dve.sem_inc(free(name_of(t)), 1)
                    dve.sem_inc(sem("x_ready"), 1)
                    if t >= 2:
                        dve.wait_ge(sem("squares_ready"), DT * norms[0] + t)
                        last = dve.tensor_tensor(out=sq[:, 0, :], in0=sq[:, 0, :], in1=sq[:, t - 1, :], op=ADD)
                        link(last)
                dve.sem_inc(sem("squares_added"), 1)
                norms[0] += 1

            residual(lambda t: ("out1", t), lambda t, s: half[:, t, 0:1], SEQ, [1], sq1)
            h_from("ss_n2", SEQ, TALL)
            for m in range(12, 20):
                multiply(m)
            residual(lambda t: ("ffb", t), lambda t, s: mod1[:, 40 + t:41 + t], SEQ, [1], sq1, lambda t: multiply(20 + t))
            mean_square("ss_n3", varb[:, SEQ:], D, width=SEQ)
            rsqrt(varb[:, SEQ:], rstd[:, SEQ:], H[:, 0, SEQ:])
            for k in range(DT):
                dve.scalar_tensor_tensor(out=X[:, k, SEQ:], in0=X[:, k, SEQ:], scalar=V("g_final")[:, k:k + 1], in1=rstd[:, SEQ:],
                                         op0=MUL, op1=MUL).then_inc(sem("x_ready"), 1)
            norms[0] += 1
            def modulations2(l):
                p = full_bank(dve, ("mod2", l))
                link(dve.tensor_tensor(out=mod2[:, l, :, :], in0=p[:, 0:96].rearrange("p (a b) -> p a b", b=2),
                                       in1=V("b_mod", l).unsqueeze(2).to_broadcast([P, 48, 2]), op=ADD))
                dve.sem_inc(free(("mod2", l)), 1)

            tile_no = 0
            dve.wait_ge(sem("const_loaded"), 16 * 6)
            for l in range(LAYERS):
                c0 = QC[l]
                wq = TALL - c0
                if l == 0:
                    for of in range(LAYERS):
                        modulations2(of)
                for s in range(2):
                    gate_norm(gs[:, 0, :, s], V("g_norm1", l), mod2[:, l, 8:16, s], s)
                    gate_norm(gs[:, 1, :, s], V("g_norm2", l), mod2[:, l, 32:40, s], s)
                dve.tensor_scalar(out=lnh[:, 0:2], in0=V("g_cln", l), scalar1=0.5, scalar2=None, op0=MUL)
                dve.tensor_scalar(out=lnh[:, 2:4], in0=V("b_cln", l), scalar1=0.5, scalar2=None, op0=MUL)
                link(dve.tensor_scalar(out=half[:, :, :], in0=mod2[:, l, 16:24, :], scalar1=0.5, scalar2=None, op0=MUL))
                dve.sem_inc(sem("mod_ready"), 1)
                h_from(("ss_n1", l), 0, TALL)
                dve.wait_ge(sem("pad_clear"), l + 1)
                for c in range(2):
                    dve.wait_ge(sem("glu_parts"), 2 * l + c + 1)
                    s0 = c0 // SEQ
                    src = cth[:, c0:TALL].rearrange("p (s t) -> p s t", t=SEQ)
                    oth = cah[:, c0:TALL].rearrange("p (s t) -> p s t", t=SEQ)
                    link(dve.scalar_tensor_tensor(out=upad[:, c, s0:2, CV_W // 2:CV_W // 2 + SEQ], in0=src, scalar=1.0, in1=oth, op0=ADD, op1=MUL))
                    dve.sem_inc(sem("glu_done"), 1)
                for w in range(CV_W):
                    for c in range(2):
                        s0 = c0 // SEQ
                        u = upad[:, c, s0:2, w:w + SEQ]
                        a = acc[:, c, c0:TALL].rearrange("p (s t) -> p s t", t=SEQ)
                        wt = V("w_dw", l)[:, c * CV_W + w:c * CV_W + w + 1]
                        if w == 0:
                            last = dve.tensor_scalar(out=a, in0=u, scalar1=wt, scalar2=V("b_dw", l)[:, c:c + 1], op0=MUL, op1=ADD)
                        else:
                            last = dve.scalar_tensor_tensor(out=a, in0=u, scalar=wt, in1=a, op0=MUL, op1=ADD)
                    link(last)
                dve.sem_inc(sem("conv_ready"), 1)
                mean_square(("ss_ckv", l), varb[:, :], P)
                mean_square(("ss_cq", l), cqvar[:, c0:], Q_LORA, width=wq)
                rsqrt(varb[:, :], rstd[:, :], ltmp)
                link(dve.scalar_tensor_tensor(out=ckvn, in0=ckv, scalar=V("g_ckv", l), in1=rstd[:, :], op0=MUL, op1=MUL))
                dve.sem_inc(sem("ckvn_ready"), 1)
                rsqrt(cqvar[:, c0:], cqrs[:, c0:], ltmp[:, c0:])
                for t in range(2):
                    last = dve.scalar_tensor_tensor(out=cqn[:, t, c0:], in0=cq[:, t, c0:], scalar=V("g_cq", l)[:, t:t + 1], in1=cqrs[:, c0:], op0=MUL, op1=MUL)
                link(last)
                dve.sem_inc(sem("cqn_ready"), 1)

                def head(k):
                    return (kT if k < 8 else qT)[:, k % 8, :]

                def head_norm(k):
                    a = 0 if k < 8 else c0
                    p = full_bank(dve, ("hb", l, k))
                    g = gqk[:, 2 * l + (k < 8):2 * l + (k < 8) + 1]
                    link(dve.scalar_tensor_tensor(out=head(k)[:, a:], in0=head(k)[:, a:], scalar=g, in1=p[0:QK, 0:TALL - a], op0=MUL, op1=MUL))
                    dve.sem_inc(free(("hb", l, k)), 1)
                    dve.sem_inc(sem("head_normed"), 1)

                def rotate(pair):
                    p = full_bank(dve, ("hr", l, pair))[NOPE:QK, :].rearrange("p (e t) -> p e t", e=2)
                    two = [ROPE, 2, SEQ]
                    dst = (kT if pair < 4 else qT)[NOPE:QK, 2 * pair % 8:2 * pair % 8 + 2, SEQ:TALL]
                    tmp = rtmp[NOPE:QK, :].rearrange("p (e t) -> p e t", e=2)
                    dve.tensor_tensor(out=dst, in0=dst, in1=ropet[NOPE:QK, 0, SEQ:].unsqueeze(1).to_broadcast(two), op=MUL)
                    link(dve.tensor_tensor(out=tmp, in0=p, in1=ropet[NOPE:QK, 1, SEQ:].unsqueeze(1).to_broadcast(two), op=MUL))
                    dve.sem_inc(free(("hr", l, pair)), 1)
                    link(dve.tensor_tensor(out=dst, in0=dst, in1=tmp, op=ADD))
                    dve.sem_inc(sem("heads_ready"), 1)

                mean_square(("hsum", l), hvar, QK, m=16)
                p = full_bank(dve, ("cmean", l))
                link(dve.tensor_scalar(out=mu[:, c0:], in0=p[:, 0:wq], scalar1=1.0 / CV_C, scalar2=None, op0=MUL))
                dve.sem_inc(free(("cmean", l)), 1)
                link(dve.tensor_tensor(out=acc[:, :, c0:], in0=acc[:, :, c0:], in1=mu[:, c0:].unsqueeze(1).to_broadcast([P, 2, wq]), op=SUB))
                dve.sem_inc(sem("centred"), 1)
                rsqrt(hvar, hrs, htmp)
                dve.sem_inc(sem("head_roots"), 1)
                for k in range(2):
                    head_norm(k)
                mean_square(("cvar", l), varb[:, c0:], CV_C, width=wq)
                for i in range(2, 16 + 4):
                    if i < 16:
                        head_norm(i)
                    if i >= 4 and i % 2 == 0:
                        rotate((i - 4) // 2)
                    if i == 4:
                        rsqrt(varb[:, c0:], rstd[:, c0:], mu[:, c0:])
                        link(dve.tensor_tensor(out=acc[:, :, c0:], in0=acc[:, :, c0:], in1=rstd[:, c0:].unsqueeze(1).to_broadcast([P, 2, wq]), op=MUL))
                        dve.sem_inc(sem("ln_ready"), 1)
                    if i == 9:
                        dve.wait_ge(sem("ln_tanh"), l + 1)
                        link(dve.scalar_tensor_tensor(out=br[:, 6:8, c0:], in0=csq[:, :, c0:], scalar=1.0, in1=acc[:, :, c0:], op0=ADD, op1=MUL))
                        dve.sem_inc(sem("conv_done"), 1)
                for tag, al, q0, nk in ATT:
                    if al == l:
                        attention(tag, P2, nk, QK ** -0.5, None)
                i = 0
                for j in range(2):
                    for b in range(3):
                        for t in range(4):
                            f = 4 * j + t
                            dve.wait_ge(sem("gates2"), 24 * l + i + 1)
                            p = full_bank(dve, ("br", l, j, b, t))
                            dst = m2[:, f, c0:] if b == 0 else br2[:, i % 2, c0:]
                            link(dve.scalar_tensor_tensor(out=dst, in0=sig2[:, i % 2, c0:], scalar=1.0, in1=p[:, 0:wq], op0=ADD, op1=MUL))
                            dve.sem_inc(free(("br", l, j, b, t)), 1)
                            dve.sem_inc(sem("gates_used"), 1)
                            if b:
                                link(dve.tensor_tensor(out=m2[:, f, c0:], in0=m2[:, f, c0:], in1=br2[:, i % 2, c0:], op=ADD))
                            if b == 2:
                                dve.sem_inc(sem("merged2"), 1)
                            i += 1
                residual(lambda t: ("out2", l, t), lambda t, s: half[:, t, s:s + 1], c0, streams(l), sqx[:, :, c0:])
                h_from(("ss_n2", l), c0, TALL)
                norms[0] += 1
                mine = [t for ll, t in TILES if ll == l]
                f4 = tixf.rearrange("p (h q) k -> p h q k", q=2)
                t4 = top[:, :, :].rearrange("p (h q) k -> p h q k", q=2)
                half4 = [P, PH // 2, TOPK, TOPK]

                def sixteen_best(value, index, data, these):
                    for i, d in these:
                        last = dve.max(value[:, i, 0:8], data[:, d, :])
                    link(last)
                    for i, d in these:
                        last = dve.max_index(index[:, i, 0:8], value[:, i, 0:8], data[:, d, :])
                    link(last)
                    for i, d in these:
                        last = dve.match_replace(data[:, d, :], value[:, i, 0:8], data[:, d, :], -3.0e38)
                    link(last)
                    for i, d in these:
                        last = dve.max(value[:, i, 8:16], data[:, d, :])
                    link(last)
                    for i, d in these:
                        last = dve.max_index(index[:, i, 8:16], value[:, i, 8:16], data[:, d, :])
                    link(last)

                def keys_by_rank(a, e):
                    hh = slice(4 * e, 4 * e + 4)
                    link(dve.tensor_tensor(out=eqp, in0=posf[:, a, hh, :].unsqueeze(3).to_broadcast(half4),
                                           in1=iota16[:, :].unsqueeze(1).unsqueeze(1).to_broadcast(half4), op=ALU.is_equal))
                    link(dve.tensor_tensor(out=eqp, in0=eqp, in1=f4[:, hh, a, :].unsqueeze(2).to_broadcast(half4), op=MUL))
                    link(dve.tensor_reduce(out=ij[:, a, hh, :], in_=eqp, axis=AX.X, op=ADD))

                def route(n, step):
                    what, e = step.split()[0], int(step.split()[-1]) if " " in step else None
                    if what == "residue":
                        for a in range(2):
                            dve.wait_ge(sem("part1"), 2 * n + a + 1)
                            p = full_bank(dve, ("ht", n, a))
                            link(dve.tensor_tensor(out=hres[:, a * 512:(a + 1) * 512], in0=p, in1=hp1[:, a * 512:(a + 1) * 512], op=SUB))
                            dve.sem_inc(free(("ht", n, a)), 1)
                        dve.sem_inc(sem("residue"), 1)
                    elif what == "parts":
                        dve.wait_ge(sem("part2"), n + 1)
                        link(dve.tensor_tensor(out=hp3, in0=hres, in1=hp2, op=SUB))
                        for i, part in enumerate((hp1, hp2, hp3)):
                            for g in range(4):
                                last = dve.tensor_copy(hs[32 * i:32 * i + 32, n % 2, g, :], part[32 * g:32 * g + 32, :])
                        link(last)
                        dve.sem_inc(sem("hs_ready"), 1)
                    elif what == "top":
                        dve.wait_ge(sem("scores_ready"), 4 * n + 2 * (e // 2 + 1))
                        sixteen_best(top, tix, sc, [(i, i) for i in range(4 * e, 4 * e + 4)])
                    elif what == "pairs":
                        if e % 2 == 0:
                            hh = slice(2 * e, 2 * e + 4)
                            link(dve.tensor_tensor(out=cand.rearrange("p h (i j) -> p h i j", j=TOPK),
                                                   in0=t4[:, hh, 0, :].unsqueeze(3).to_broadcast(half4),
                                                   in1=t4[:, hh, 1, :].unsqueeze(2).to_broadcast(half4), op=ADD))
                        sixteen_best(best, pos, cand, [(2 * e + i, 2 * (e % 2) + i) for i in range(2)])
                        if e == 3:
                            link(dve.tensor_tensor(out=gat, in0=best, in1=best[:, :, 0:1].to_broadcast([P, PH, TOPK]), op=SUB))
                            dve.sem_inc(sem("best_ready"), 1)
                            dve.tensor_copy(tixf, tix)
                            posv = pos.rearrange("p a b -> p (a b)")
                            dve.tensor_scalar(out=posi[:, 0, :], in0=posv, scalar1=4, scalar2=None, op0=ALU.logical_shift_right)
                            link(dve.tensor_scalar(out=posi[:, 1, :], in0=posv, scalar1=15, scalar2=None, op0=ALU.bitwise_and))
                            link(dve.tensor_copy(posf.rearrange("p a b c -> p (a b c)"), posi.rearrange("p a b -> p (a b)")))
                    elif what == "keys":
                        keys_by_rank(e // 2, e % 2)
                    if what == "keys" and e == 3:
                        link(dve.scalar_tensor_tensor(out=eid, in0=ij[:, 0, :, :].rearrange("p a b -> p (a b)"), scalar=float(NKEY),
                                                      in1=ij[:, 1, :, :].rearrange("p a b -> p (a b)"), op0=MUL, op1=ADD))
                        dve.wait_ge(sem("best_exp"), n + 1)
                        link(dve.tensor_reduce(out=gsum[:, 0, :], in_=gat, axis=AX.X, op=ADD))
                        link(dve.reciprocal(gsum[:, 1, :], gsum[:, 0, :]))
                        link(dve.tensor_tensor(out=gat, in0=gat, in1=gsum[:, 1, :].unsqueeze(2).to_broadcast([P, PH, TOPK]), op=MUL))
                        dve.sem_inc(sem("routed"), 1)
                    if what == "experts":
                        p = full_bank(dve, ("ij", n))
                        dve.tensor_scalar(out=idxT[:, n % 2, :], in0=p[:, 0:P], scalar1=float(l * NEXP), scalar2=None, op0=ADD)
                        link(dve.tensor_copy(gateT[:, n % 2, :], p[:, P:2 * P]))
                        dve.sem_inc(free(("ij", n)), 1)
                        dve.sem_inc(sem("idx_ready"), 1)

                def add_outputs(n, tt):
                    for a in range(2):
                        p = full_bank(dve, ("yt", n, a))
                        for k in range(4):
                            f = 4 * a + k
                            last = dve.scalar_tensor_tensor(out=X[:, f, tt * P:(tt + 1) * P], in0=p[:, k * P:(k + 1) * P],
                                                            scalar=mod2[:, l, 40 + f, tt // 2:tt // 2 + 1], in1=X[:, f, tt * P:(tt + 1) * P], op0=MUL, op1=ADD)
                        link(last)
                        dve.sem_inc(free(("yt", n, a)), 1)

                def eight(n, i, it):
                    t0 = n * P + i * SLOTS
                    for j in range(SLOTS):
                        dve.wait_ge(sem(f"u_arrived{j}"), it * 16 + 16 * (t0 // SLOTS + 1))
                        dve.wait_ge(sem("spread"), it * SLOTS + (t0 + j + 1))
                        if j % QUAD == 0:
                            dve.wait_ge(sem("gelus"), it * 2 + (t0 // QUAD + j // QUAD + 1))
                        b = HB + 2 * (j % 2)
                        dve.scalar_tensor_tensor(out=Us[:, j, :], in0=ps[:, b:b + 2, :].rearrange("p a b -> p (a b)"), scalar=1.0,
                                                 in1=Us[:, j, :], op0=MUL, op1=MUL, accum_out=dots[:, j:j + 1]).then_inc(sem("dots"), 1)
                        if j % QUAD == QUAD - 1:
                            a = j - QUAD + 1
                            dve.wait_ge(sem("gelus"), it * 2 + (t0 // QUAD + j // QUAD + 3))
                            dve.wait_ge(sem("outputs"), it * SLOTS + (t0 + j + 1))
                            diag = acts[:, :, :].rearrange("p a b -> p (a b)")[:, a * (SLOTS + 1):(a + QUAD - 1) * (SLOTS + 1) + 1:SLOTS + 1]
                            dve.tensor_tensor(out=diag, in0=gel[:, a:a + QUAD], in1=gateT[:, n % 2, bass.ds(it * SLOTS + (i * SLOTS + a), QUAD)],
                                              op=MUL).then_inc(sem("acts"), 1)

                def eights(n, i, end):
                    if end - i == 1:
                        eight(n, i, 0)
                    else:
                        with dve.Fori(0, end - i) as it:
                            eight(n, i, it)

                for step in STEPS[:-1]:
                    route(tile_no, step)
                if l == 0:
                    dve.sem_inc(sem("dots"), SLOTS)
                for tt in mine:
                    n = tile_no
                    tile_no += 1
                    i = 0
                    for end in range(1, EIGHTS + 1) if tt != mine[-1] else (13, EIGHTS):
                        eights(n, i, end)
                        i = end
                        if tt != mine[0] and i == 13:
                            add_outputs(n - 1, tt - 1)
                        if tt != mine[-1] and STEPS[i - 1]:
                            route(n + 1, STEPS[i - 1])
                add_outputs(n, tt)
                dve.sem_inc(sem("x_ready"), DT)
                dve.sem_inc(sem("x_final"), 1)

        @block.scalar
        def _(act):
            link_no = [0]

            def link(ins):
                link_no[0] += 1
                ins.then_inc(sem("act_chain"), 1)
                act.wait_ge(sem("act_chain"), link_no[0])

            def A_(o, i, f=ACT.Copy, **kw):
                return act.activation(o, i, f, **kw)

            def evac(name, o, m=slice(0, P), width=None, f=ACT.Copy, **kw):
                p = full_bank(act, name)
                return A_(o, p[m, 0:width] if width else p[m, :], f, **kw)

            xs = [0]

            def squares(c0, c1, dst, step=None):
                for k in range(DT):
                    if xs[0]:
                        act.wait_ge(sem("x_ready"), DT * (xs[0] - 1) + k + 1)
                    A_(dst[:, k, c0:c1] if dst is sqx else dst[:, k, :], X[:, k, c0:c1], ACT.Square).then_inc(sem("squares_ready"), 1)
                    run_ahead((step, k))
                xs[0] += 1

            nroot = [0]

            def root(v, o):
                nroot[0] += 1
                act.wait_ge(sem("var_ready"), nroot[0])
                A_(o, v, ACT.Sqrt).then_inc(sem("root_ready"), 1)

            def modulate(which, nh, mod, shift, ss, c0, nmod):
                act.wait_ge(sem("mod_ready"), nmod)
                for k in range(DT):
                    act.wait_ge(sem("xn_ready"), DT * (nh - 1) + k + 1)
                    for s in ss:
                        cs = slice(max(c0, s * SEQ), (s + 1) * SEQ)
                        gi = 0 if mod is mod1 else s
                        bias = mod[:, shift + k:shift + k + 1] if mod is mod1 else mod[:, nmod - 2, shift + k, s:s + 1]
                        last = A_(H[:, k, cs], H[:, k, cs], ACT.Identity, bias=bias, scale=gs[:, which, k, gi:gi + 1])
                    last.then_inc(sem("h_ready"), 1)

            def attention(tag, prob, pt, dst, nk, scale, done):
                kts = nk // P
                for i in range(16 + 5):
                    if i < 16:
                        act.wait_ge(sem(f"{tag}_max"), i + 1)
                        p = full_bank(act, (tag, "s", i))
                        link(A_(prob[:, i, 0:nk], p[:, 0:nk], ACT.Exp, bias=stat[:, 1, i:i + 1], scale=scale, accum_out=stat[:, 2, i:i + 1]))
                        act.sem_inc(free((tag, "s", i)), 1)
                        act.sem_inc(sem(f"{tag}_exp"), 1)
                    if 0 <= i - 3 < 16:
                        h, t = (i - 3) // 2, (i - 3) % 2
                        p = full_bank(act, (tag, "t", i - 3))
                        link(A_(pt[:, h % 2, 0:kts, t * P:(t + 1) * P], p[:, 0:nk].rearrange("p (k q) -> p k q", q=P)))
                        act.sem_inc(free((tag, "t", i - 3)), 1)
                        act.sem_inc(sem(f"{tag}_probsT"), 1)
                    if 0 <= i - 5 < 16 and (i - 5) % 2:
                        h = (i - 5) // 2
                        r = slice(64 * (h % 2), 64 * (h % 2) + 64)
                        link(evac((tag, "o", h), dst(h)[r], m=r, width=SEQ))
                        act.sem_inc(free((tag, "o", h)), 1)
                        act.sem_inc(sem(done), 1)

            def run_ahead(step):
                for m in ahead.get(step, ()):
                    name, n, j = products_of[m]
                    rows(name, n, [j])

            def rows(name, n, these):
                for j in these:
                    modulations = 0 if name == "mod1" else 1 + name[1]
                    if j >= 2:
                        act.wait_ge(sem("rows_turned"), 11 * modulations + j - 1)
                    link(evac((name, "rows", j), yev[0:n, (j % 2) * 512:(j % 2 + 1) * 512], m=slice(0, n)))
                    act.sem_inc(free((name, "rows", j)), 1)
                    act.sem_inc(sem("rows_copied"), 1)

            act.wait_ge(sem("cond_half"), 1)
            A_(condt[:, :], cond[:, :, :].rearrange("p a b -> p (a b)"), ACT.Tanh).then_inc(sem("cond_tanh"), 1)
            for j in ADA:
                rows("mod1", 1, [j])
                run_ahead(("ada", j))
            act.wait_ge(sem("x_loaded"), 16)
            squares(SEQ, TALL, sq1)
            root(varb[:, SEQ:], rstd[:, SEQ:])
            modulate(0, 1, mod1, 0, [1], SEQ, 1)
            for j in range(9):
                for t in range(4):
                    if j in (2, 4) and t >= 2:
                        continue
                    name = ("in1", j, t)
                    if j == 0:
                        ins = evac(name, q1[:, t, :], width=SEQ, scale=HD1 ** -0.5)
                    elif j == 1:
                        ins = evac(name, k1[:, t, :], width=SEQ)
                    elif j == 2:
                        ins = evac(name, v1[:, t, :])
                    elif j == 3:
                        ins = evac(name, u1[:, t, :], width=SEQ, f=ACT.Gelu_apprx_tanh)
                    elif j == 4:
                        ins = evac(name, vs1[:, t, :], f=ACT.Gelu_apprx_tanh)
                    else:
                        g = 4 * ((j - 5) % 2) + t
                        ins = evac(name, gate1[:, g, (j - 5) // 2, :], width=SEQ, f=ACT.Tanh, scale=0.5)
                    link(ins)
                    act.sem_inc(free(name), 1)
                    if j < 3:
                        act.sem_inc(sem("qkv1_ready"), 1)
                    if j == 4:
                        link(A_(vsq1[:, t, :], vs1[:, t, :], ACT.Square, accum_out=ssg1[:, t:t + 1]))
                        if t == 1:
                            act.sem_inc(sem("vs_squares"), 1)
                    if j > 4:
                        act.sem_inc(sem("gates1"), 1)
                run_ahead(("in1", j))
            root(stat[:, 1, 0:2], stat[:, 2, 0:2])
            attention("a1", P1, PT1, lambda h: att1[:, h // 2, :], SEQ, 1.0, "mix1_ready")
            squares(SEQ, TALL, sq1)
            root(varb[:, SEQ:], rstd[:, SEQ:])
            modulate(1, 2, mod1, 24, [1], SEQ, 1)
            for t in range(FF_T):
                link(evac(("ffa", t), ff1[:, t, :], width=SEQ, f=ACT.Relu))
                act.sem_inc(free(("ffa", t)), 1)
                A_(ff1[:, t, :], ff1[:, t, :], ACT.Square).then_inc(sem("ff_ready"), 1)
                if t % 4 == 3:
                    run_ahead(("ffa", t // 4))
            squares(SEQ, TALL, sq1, "ffb")
            root(varb[:, SEQ:], rstd[:, SEQ:])
            run_ahead("n3")
            tile_no = 0
            nh = 2
            for l in range(LAYERS):
                c0 = QC[l]
                wq = TALL - c0
                if l == 0:
                    act.wait_ge(sem("ctx_loaded"), 16)
                squares(0, TALL, sqx)
                root(varb[:, :], rstd[:, :])
                nh += 1
                modulate(0, nh, mod2, 0, [0, 1], 0, 2 + l)
                for c in range(2):
                    if c or l:
                        act.wait_ge(sem("glu_done"), 2 * l + c)
                    link(evac(("zc", l, c), cah[:, c0:], width=wq, scale=0.5))
                    act.sem_inc(free(("zc", l, c)), 1)
                    link(evac(("zc", l, 2 + c), cth[:, c0:], width=wq, f=ACT.Tanh, scale=0.5))
                    act.sem_inc(free(("zc", l, 2 + c)), 1)
                    act.sem_inc(sem("glu_parts"), 1)
                link(evac(("ckv", l), ckv))
                A_(lsq[:, 0, :], ckv, ACT.Square).then_inc(sem("lat_squares"), 1)
                act.sem_inc(free(("ckv", l)), 1)
                p = full_bank(act, ("kr", l))
                A_(kT[NOPE:QK, :, :], p[NOPE:QK, :].unsqueeze(1).to_broadcast([ROPE, MH, TALL]))
                for i in range(3):
                    last = A_(hsq[NOPE:QK, i, :], p[NOPE:QK, :], ACT.Square)
                last.then_inc(free(("kr", l)), 1)
                for t in range(2):
                    link(evac(("cq", l, t), cq[:, t, c0:], width=wq))
                    act.sem_inc(free(("cq", l, t)), 1)
                A_(lsq[:, 1:3, c0:], cq[:, :, c0:], ACT.Square).then_inc(sem("lat_squares"), 1)
                for t in range(c0 // P, 4):
                    link(evac(("zf", l, t), zft[:, t, :], width=FN_C))
                    act.sem_inc(free(("zf", l, t)), 1)
                    act.sem_inc(sem("zf_ready"), 1)
                root(varb[:, :], rstd[:, :])
                root(cqvar[:, c0:], cqrs[:, c0:])
                for s in streams(l):
                    for c in range(2):
                        link(evac(("dt", l, s, c), g1f[:, 2 * s + c, :]))
                        act.sem_inc(free(("dt", l, s, c)), 1)
                        act.sem_inc(sem("dft_ready"), 1)
                for s in streams(l):
                    p = full_bank(act, ("dc", l, s))
                    A_(br[:, 4:6, s * SEQ:(s + 1) * SEQ], p.rearrange("p (a b) -> p a b", a=2)).then_inc(free(("dc", l, s)), 1)
                for t in range(4):
                    evac(("v", l, t), vtok[:, t, :]).then_inc(free(("v", l, t)), 1)
                for i in range(16):
                    a = 0 if i < 8 else c0
                    m = slice(0, NOPE) if i < 8 else slice(0, QK)
                    p = full_bank(act, ("hp", l, i))
                    A_((kT if i < 8 else qT)[m, i % 8, a:], p[m, 0:TALL - a])
                    if i >= 3:
                        act.wait_ge(sem("squares_summed"), 15 * l + i - 2)
                    link(A_(hsq[m, i % 3, a:], p[m, 0:TALL - a], ACT.Square))
                    act.sem_inc(free(("hp", l, i)), 1)
                    act.sem_inc(sem("head_squares"), 1)
                root(hvar, hrs)
                act.wait_ge(sem("centred"), l + 1)
                A_(csq[:, :, c0:], acc[:, :, c0:], ACT.Square).then_inc(sem("conv_squares"), 1)
                root(varb[:, c0:], rstd[:, c0:])
                act.wait_ge(sem("ln_ready"), l + 1)
                for c in range(2):
                    last = A_(acc[:, c, c0:], acc[:, c, c0:], ACT.Identity, scale=lnh[:, c:c + 1], bias=lnh[:, 2 + c:3 + c])
                link(last)
                A_(csq[:, :, c0:], acc[:, :, c0:], ACT.Tanh).then_inc(sem("ln_tanh"), 1)
                for tag, al, q0, nk in ATT:
                    if al == l:
                        attention(tag, P2, PT2, lambda h: br[:, h // 2, q0:q0 + SEQ], nk, QK ** -0.5, "att_ready")
                i = 0
                for j in range(2):
                    for b in range(3):
                        for t in range(4):
                            if 24 * l + i >= 2:
                                act.wait_ge(sem("gates_used"), 24 * l + i - 1)
                            link(evac(("zg", l, j, b, t), sig2[:, i % 2, c0:], width=wq, f=ACT.Tanh, scale=0.5))
                            act.sem_inc(free(("zg", l, j, b, t)), 1)
                            act.sem_inc(sem("gates2"), 1)
                            i += 1
                squares(c0, TALL, sqx)
                root(varb[:, c0:], rstd[:, c0:])
                nh += 1
                modulate(1, nh, mod2, 24, streams(l), c0, 2 + l)
                mine = [t for ll, t in TILES if ll == l]
                s4 = sc.rearrange("p (h q) k -> p h q k", q=2)

                def route(n, step):
                    if step == "residue":
                        for a in range(2):
                            evac(("ht", n, a), hp1[:, a * 512:(a + 1) * 512]).then_inc(sem("part1"), 1)
                        act.wait_ge(sem("residue"), n + 1)
                        A_(hp2, hres).then_inc(sem("part2"), 1)
                    elif step in ("scores 0", "scores 1"):
                        act.wait_ge(sem("hs_ready"), n + 1)
                        a = int(step[-1])
                        for q in range(2):
                            p = full_bank(act, ("sc", n, a, q))
                            link(A_(s4[:, 4 * a:4 * a + 4, q, :], p.rearrange("p (a b) -> p a b", b=P)))
                            act.sem_inc(free(("sc", n, a, q)), 1)
                            act.sem_inc(sem("scores_ready"), 1)
                    else:
                        act.wait_ge(sem("best_ready"), n + 1)
                        A_(gat, gat, ACT.Exp).then_inc(sem("best_exp"), 1)

                def copy_outputs(it, n8):
                    act.wait_ge(sem("outputs"), it * SLOTS + (n8 + 2) * SLOTS)
                    act.wait_ge(sem("y_out"), it * 16 + 16 * (n8 + 1))
                    A_(yev[:, :], ps[0:SLOTS, YB:YB + 2, :].rearrange("p a b -> p (a b)")).then_inc(sem("y_copied"), 1)
                    act.wait_ge(sem("y_copied"), it + (n8 + 2))
                    act.dma_start(yscr[bass.ds(it * SLOTS + n8 * SLOTS, SLOTS), :], yev[:, :]).then_inc(sem("y_out"), 16)

                def eight(n, i, it, first):
                    t0 = n * P + i * SLOTS
                    for hf in range(2):
                        q0 = QUAD * hf
                        act.wait_ge(sem("dots"), it * SLOTS + (t0 + SLOTS + q0 + QUAD))
                        A_(gel[:, q0:q0 + QUAD], dots[:, q0:q0 + QUAD], ACT.Gelu_apprx_tanh).then_inc(sem("gelus"), 1)
                        if hf == 0 and not first:
                            copy_outputs(it, t0 // SLOTS - 1)

                def read_back(n):
                    act.wait_ge(sem("y_out"), 16 + 16 * (P // SLOTS) * (n + 1))
                    act.dma_start(ytok, yscr[n * P:(n + 1) * P, :]).then_inc(sem("y_back"), 16)

                route(tile_no, "residue")
                for part, (a, b) in enumerate([(c0, c0 + P), (c0 + P, TALL)]):
                    for t in range(DT):
                        link(evac(("wq", l, t, part), qp[:, t, a:b], width=b - a))
                        act.sem_inc(free(("wq", l, t, part)), 1)
                        act.sem_inc(sem("query_ready"), 1)
                    if part == 0:
                        route(tile_no, "scores 0")
                        route(tile_no, "scores 1")
                route(tile_no, "exp")
                if l == 0:
                    act.sem_inc(sem("gelus"), 2)
                    act.sem_inc(sem("y_copied"), 1)
                    act.sem_inc(sem("y_out"), 16)
                for tt in mine:
                    n = tile_no
                    tile_no += 1
                    i = 0
                    while i < EIGHTS:
                        end = min(x for x in (0, 1, 3, 5, 10, EIGHTS - 1) if x >= i) + 1
                        if end - i == 1:
                            eight(n, i, 0, i == 0 and tt == mine[0])
                        else:
                            with act.Fori(0, end - i) as it:
                                eight(n, i, it, False)
                        i = end
                        if end - 1 == 3 and tt != mine[0]:
                            read_back(n - 1)
                        if tt != mine[-1] and end - 1 in ACT_STEPS:
                            route(n + 1, ACT_STEPS[end - 1])
                copy_outputs(0, (n + 1) * P // SLOTS - 1)
                read_back(n)

        @block.gpsimd
        def _(pool):
            def load_for_products(these):
                for m in these:
                    name, n, j = products_of[m]
                    src = (A["w_ada"][0] if name == "mod1" else A["w_mod_2"][name[1]]).rearrange("(k p) n -> p k n", p=P)
                    for e in range(2):
                        if m:
                            pool.wait_ge(sem("modw_used"), 2 * m + e - 1)
                        pool.dma_start(modw[:, e, :, :], src[:, 4 * e:4 * e + 4, j * 512:(j + 1) * 512]).then_inc(sem(f"modw_arrived{e}"), 16)

            load_for_products(range(4))
            pool.wait_ge(sem("wsg_loaded"), 16)
            pool.affine_select(out=wsg1, in_=wsg1, compare_op=ALU.is_ge, fill=0.0, base=0,
                               pattern=[[0, SGU_G], [1, P]], channel_multiplier=-1).then_inc(sem("sgu_ready"), 1)
            load_for_products(range(4, len(products_of)))
            tile_no = 0
            for l in range(LAYERS):
                pool.wait_ge(sem("h_ready"), DT * (3 + 2 * l))
                for e in (0, SEQ + CV_W // 2):
                    last = pool.memset(upad[:, :, :, e:e + CV_W // 2], 0.0)
                last.then_inc(sem("pad_clear"), 1)
                for tt in [t for ll, t in TILES if ll == l]:
                    n = tile_no
                    tile_no += 1
                    t0 = n * P

                    def gather(table, dst, used, arrived, it, c):
                        pool.wait_ge(sem(used), it * SEG + (t0 + QUAD * (c + 1)))
                        pool.sem_inc(sem("pool_paced"), 1)
                        for j in range(QUAD):
                            s = QUAD * (c % 2) + j
                            off = bass.IndirectOffsetOnAxis(idl[:, c % 4, j:j + 1], 0)
                            pool.indirect_dma_start(dst[:, s, :], None, table, off).then_inc(sem(f"{arrived}{s}"), 16)

                    def indices(it, c):
                        pool.tensor_copy(idl[:, c % 4, :], idxT[:, n % 2, bass.ds(it * SEG + QUAD * c, QUAD)]).then_inc(sem("idl_ready"), 1)
                        pool.wait_ge(sem("idl_ready"), it * 4 + (t0 // QUAD + c + 1))
                        pool.sem_inc(sem("pool_paced"), 1)

                    def sixteen(it, last_one):
                        for c in range(4):
                            if not (last_one and c == 3):
                                indices(it, c + 1)
                                gather(A["u_tab"], Us, "dots", "u_arrived", it, c + 1)
                            gather(A["v_tab"], Vs, "outputs", "v_arrived", it, c)

                    pool.wait_ge(sem("idx_ready"), n + 1)
                    indices(0, 0)
                    gather(A["u_tab"], Us, "dots", "u_arrived", 0, 0)
                    with pool.Fori(0, P // SEG - 1) as it:
                        sixteen(it, False)
                    sixteen(P // SEG - 1, True)


def _columns(v):
    return v.reshape(-1, P).T


def kernel(**inputs):
    import numpy as np
    import concourse.bacc as bacc
    from concourse.bass_utils import run_bass_kernel_spmd

    I = {k: np.asarray(v) for k, v in inputs.items()}
    arrays = {}
    for name in ("w_ada", "w_in", "w_proj_attn", "w_proj_sgu", "w_out", "w_ff1", "w_ff2", "b_sgu", "w_mod_2", "w_in_2", "w_ukv_2",
                 "w_uq_2", "wb_attn_2", "wb_fnet_2", "wb_conv_2", "w_out_2", "w_query_2"):
        arrays[name] = np.ascontiguousarray(I[name])
    arrays["u_tab"] = np.ascontiguousarray(I["u_tab_2"]).reshape(LAYERS * NEXP, D)
    arrays["v_tab"] = np.ascontiguousarray(I["v_tab_2"]).reshape(LAYERS * NEXP, D)
    cols = [_columns(I[n].reshape(-1)) for n in ("c", "b_ada", "g_mix", "g_sgu", "g_ffn", "g_final", "c_ctx_2", "c_2")]
    for l in range(LAYERS):
        for n in ("b_mod_2", "g_norm1_2", "g_ckv_2", "g_cq_2", "b_dw_2", "g_cln_2", "b_cln_2"):
            cols.append(_columns(I[n][l]))
        cols.append(I["w_dw_2"][l, :, 0, :].reshape(CV_W, 2, P).transpose(2, 1, 0).reshape(P, 2 * CV_W))
        cols.append(_columns(I["g_norm2_2"][l]))
    arrays["vec"] = np.ascontiguousarray(np.concatenate(cols, axis=1))
    arrays["xT"] = np.ascontiguousarray(I["x"][0].T.reshape(DT, P, SEQ).transpose(1, 0, 2))
    arrays["ctxT"] = np.ascontiguousarray(I["ctx_2"][0].T.reshape(DT, P, SEQ).transpose(1, 0, 2))
    arrays["wsgT"] = np.ascontiguousarray(I["w_sgu"][0].transpose(2, 0, 1))
    arrays["keys"] = np.ascontiguousarray(I["sub_keys_2"].transpose(0, 2, 4, 1, 3).reshape(LAYERS, P, PH, NKEY))
    arrays["gqk"] = np.ascontiguousarray(np.stack([I["g_qn_2"][0], I["g_kn_2"][0], I["g_qn_2"][1], I["g_kn_2"][1]], axis=1))

    f = np.float32
    arrays["ident"] = np.eye(P, dtype=f)
    key, q = np.arange(SEQ), np.arange(P)
    arrays["mask"] = np.stack([np.where(key[None, :] <= (t * P + q)[:, None], 0.0, -1e30) for t in range(2)], axis=1).astype(f)
    w = 2 * np.pi * (np.arange(SEQ)[:, None] * np.arange(SEQ)[None, :] % SEQ) / SEQ
    both = np.concatenate([np.cos(w), np.sin(w)], axis=1)
    arrays["dft"] = np.ascontiguousarray(both.reshape(2, P, 512).transpose(1, 0, 2)).astype(f)
    w = 2 * np.pi * (np.arange(64)[:, None] * np.arange(64)[None, :] % 64) / 64
    arrays["dftc"] = np.stack([np.kron(np.eye(2), np.cos(w)), -np.kron(np.eye(2), np.sin(w))], axis=1).astype(f) / f(128.0)
    half = ROPE // 2
    inv = np.power(f(10000.0), -np.arange(0, half, 2, dtype=f) / f(half)).astype(f)
    row, col = np.arange(SEQ) // 64, np.arange(SEQ) % 64
    ar, ac = row[:, None].astype(f) * inv, col[:, None].astype(f) * inv
    ang = np.concatenate([ar, ar, ac, ac], axis=1)
    rope = np.zeros((QK, 2, TALL), f)
    rope[:, 0, :] = 1.0
    rope[NOPE:, 0, SEQ:] = np.cos(ang).T
    rope[NOPE:, 1, SEQ:] = np.sin(ang).T
    arrays["rope"] = rope
    rot = np.zeros((QK, QK), f)
    for a in range(2):
        for i in range(8):
            lo = NOPE + 16 * a + i
            rot[lo + 8, lo] = -1.0
            rot[lo, lo + 8] = 1.0
    arrays["rotm"] = rot
    arrays["iota16"] = np.tile(np.arange(TOPK, dtype=f), (P, 1))

    nc = bacc.Bacc("TRN2", target_bir_lowering=False, num_devices=1)
    A = {}
    for name, a in arrays.items():
        A[name] = nc.dram_tensor(f"in_{name}", a.shape, mybir.dt.from_np(a.dtype), kind="ExternalInput").ap()
    out = nc.dram_tensor("out_x", (P, DT, SEQ), mybir.dt.float32, kind="ExternalOutput").ap()
    two_blocks_kernel(nc, A, out)
    r = run_bass_kernel_spmd(nc, [{f"in_{k}": v for k, v in arrays.items()}], core_ids=[0])
    y = r.results[0]["out_x"]
    return np.ascontiguousarray(y.transpose(1, 0, 2).reshape(D, SEQ).T)[None]
```
